# Optimizing a Trainium2 kernel written in Bass

```python
import math
import jax, jax.numpy as jnp
from jax import lax
import numpy as np

D_MODEL = 1024
BATCH = 1
SEQ = 256
DEPTH = 2

N_MEM = 256
EPS = 1e-6
NEG_INF = -1e30
MOBA_HEADS = 8
MOBA_HEAD_DIM = 64
MOBA_WIDTH = MOBA_HEADS * MOBA_HEAD_DIM
MOBA_BLOCK = 256
MOBA_TOPK = 3
MOBA_Q_CHUNK = 32
ROPE_THETA = 10000.0
SSM_WIDTH = 512
SSM_GROUP = 16
SSM_GROUPS = SSM_WIDTH // SSM_GROUP
SSM_STATE = 64
DT_MIN = 1e-3
DT_MAX = 1e-1
GDN_HEADS = 4
GDN_HEAD_DIM = 128
GDN_WIDTH = GDN_HEADS * GDN_HEAD_DIM
GDN_CONV = 4
GDN_CHUNK = 64
XA_HEADS = 4
XA_HEAD_DIM = 128
XA_WIDTH = XA_HEADS * XA_HEAD_DIM
D_FF = 2816
N_EXPERTS = 8
TOP_K = 2
N_DENSE = (DEPTH + 1) // 2
N_MOE = DEPTH // 2
N_BRANCH = 3
IN_SIZES = (MOBA_WIDTH, MOBA_WIDTH, MOBA_WIDTH,
            SSM_WIDTH,
            GDN_WIDTH, GDN_WIDTH, GDN_WIDTH,
            GDN_HEADS, GDN_HEADS,
            GDN_WIDTH,
            D_MODEL, D_MODEL, D_MODEL)
D_IN = 3 * MOBA_WIDTH + SSM_WIDTH + 4 * GDN_WIDTH + 2 * GDN_HEADS + N_BRANCH * D_MODEL

kernel_name = "hybrid_moba_s5_gdn_xattn_moe_block"

def rms_norm(x, g):
    xf = x.astype(jnp.float32)
    y = xf * lax.rsqrt(jnp.mean(xf * xf, axis=-1, keepdims=True) + EPS)
    return (y * g.astype(jnp.float32)).astype(x.dtype)

def l2_norm(x):
    xf = x.astype(jnp.float32)
    return xf * lax.rsqrt(jnp.sum(xf * xf, axis=-1, keepdims=True) + EPS)

def split_columns(p):
    parts, start = [], 0
    for size in IN_SIZES:
        parts.append(p[..., start:start + size])
        start += size
    return parts

def rope_tables(positions):
    inv = 1.0 / (ROPE_THETA ** (jnp.arange(0, MOBA_HEAD_DIM, 2, dtype=jnp.float32) / MOBA_HEAD_DIM))
    ang = positions.astype(jnp.float32)[..., None] * inv
    return jnp.cos(ang), jnp.sin(ang)

def apply_rope(x, cos, sin):
    x1, x2 = jnp.split(x.astype(jnp.float32), 2, axis=-1)
    c, s = cos[:, :, None, :], sin[:, :, None, :]
    return jnp.concatenate([x1 * c - x2 * s, x2 * c + x1 * s], axis=-1).astype(x.dtype)

def moba_attention(q, k, v):
    b_, s_, h_, dh = q.shape
    pad = (-s_) % MOBA_BLOCK
    widths = ((0, 0), (0, pad), (0, 0), (0, 0))
    q, k, v = (jnp.pad(t, widths) for t in (q, k, v))
    sp = s_ + pad
    nb = sp // MOBA_BLOCK
    nc = sp // MOBA_Q_CHUNK
    top = min(MOBA_TOPK, nb)
    scale = dh ** -0.5
    qh = jnp.transpose(q, (0, 2, 1, 3))
    kb = jnp.transpose(k, (0, 2, 1, 3)).reshape(b_, h_, nb, MOBA_BLOCK, dh)
    vb = jnp.transpose(v, (0, 2, 1, 3)).reshape(b_, h_, nb, MOBA_BLOCK, dh)
    k_mean = jnp.mean(kb.astype(jnp.float32), axis=3)
    q_blk = jnp.arange(sp) // MOBA_BLOCK
    gate = jnp.einsum('bhsd,bhnd->bhsn', qh.astype(jnp.float32), k_mean)
    gate = jnp.where(jnp.arange(nb)[None, :] < q_blk[:, None], gate, NEG_INF)
    _, sel = lax.top_k(gate, top)
    valid = jnp.arange(top)[None, :] < jnp.minimum(q_blk, top)[:, None]

    qc = qh.reshape(b_, h_, nc, MOBA_Q_CHUNK, dh).transpose(2, 0, 1, 3, 4)
    selc = sel.reshape(b_, h_, nc, MOBA_Q_CHUNK, top).transpose(2, 0, 1, 3, 4)
    validc = valid.reshape(nc, MOBA_Q_CHUNK, top)
    gather_blocks = jax.vmap(jax.vmap(lambda blocks, idx: blocks[idx]))

    def one_chunk(args):
        ci, q_c, sel_c, valid_c = args
        own = (ci * MOBA_Q_CHUNK) // MOBA_BLOCK
        k_own = lax.dynamic_index_in_dim(kb, own, axis=2, keepdims=False)
        v_own = lax.dynamic_index_in_dim(vb, own, axis=2, keepdims=False)
        k_sel = gather_blocks(kb, sel_c)
        v_sel = gather_blocks(vb, sel_c)
        s_sel = jnp.einsum('bhcd,bhckjd->bhckj', q_c, k_sel).astype(jnp.float32) * scale
        s_sel = jnp.where(valid_c[None, None, :, :, None], s_sel, NEG_INF)
        s_own = jnp.einsum('bhcd,bhjd->bhcj', q_c, k_own).astype(jnp.float32) * scale
        q_pos = ci * MOBA_Q_CHUNK + jnp.arange(MOBA_Q_CHUNK)
        k_pos = own * MOBA_BLOCK + jnp.arange(MOBA_BLOCK)
        s_own = jnp.where(k_pos[None, :] <= q_pos[:, None], s_own, NEG_INF)
        logits = jnp.concatenate([s_sel.reshape(b_, h_, MOBA_Q_CHUNK, top * MOBA_BLOCK), s_own], axis=-1)
        p = jax.nn.softmax(logits, axis=-1).astype(v_own.dtype)
        p_sel = p[..., :top * MOBA_BLOCK].reshape(b_, h_, MOBA_Q_CHUNK, top, MOBA_BLOCK)
        p_own = p[..., top * MOBA_BLOCK:]
        return (jnp.einsum('bhckj,bhckjd->bhcd', p_sel, v_sel)
                + jnp.einsum('bhcj,bhjd->bhcd', p_own, v_own))

    out = lax.map(one_chunk, (jnp.arange(nc), qc, selc, validc))
    out = out.transpose(1, 0, 3, 2, 4).reshape(b_, sp, h_ * dh)
    return out[:, :s_]

def s5_ssm(u, a_re, a_im, log_dt, b_re, b_im, c_re, c_im, d_skip):
    b_, s_, _ = u.shape
    uf = u.astype(jnp.float32).reshape(b_, s_, SSM_GROUPS, SSM_GROUP)
    lam = lax.complex(a_re.astype(jnp.float32), a_im.astype(jnp.float32))
    dt = jnp.exp(log_dt.astype(jnp.float32))[:, None]
    lam_bar = jnp.exp(lam * dt)
    b_mat = lax.complex(b_re.astype(jnp.float32), b_im.astype(jnp.float32))
    b_bar = ((lam_bar - 1.0) / lam)[..., None] * b_mat
    c_mat = lax.complex(c_re.astype(jnp.float32), c_im.astype(jnp.float32))
    bu = jnp.einsum('gpn,bsgn->bsgp', b_bar, uf)
    a_elems = jnp.broadcast_to(lam_bar, (1, s_, SSM_GROUPS, SSM_STATE))

    def combine(e1, e2):
        a1, h1 = e1
        a2, h2 = e2
        return a2 * a1, a2 * h1 + h2

    _, h = lax.associative_scan(combine, (a_elems, bu), axis=1)
    y = jnp.einsum('gnp,bsgp->bsgn', c_mat, h).real
    y = y + d_skip.astype(jnp.float32).reshape(SSM_GROUPS, SSM_GROUP) * uf
    return y.reshape(b_, s_, SSM_WIDTH).astype(u.dtype)

def causal_conv(x, w):
    return lax.conv_general_dilated(x, w[:, None, :], window_strides=(1,), padding=[(GDN_CONV - 1, 0)],
                                    dimension_numbers=('NWC', 'WIO', 'NWC'),
                                    feature_group_count=x.shape[-1])

def gated_delta_rule(q, k, v, g, beta):
    b_, s_, h_, dk = q.shape
    dv = v.shape[-1]
    L = GDN_CHUNK
    n = s_ // L

    def to_chunks(t):
        t = jnp.moveaxis(t.astype(jnp.float32), 2, 1)
        return t.reshape((b_, h_, n, L) + t.shape[3:])

    q = to_chunks(q) * (dk ** -0.5)
    k, v, g, beta = to_chunks(k), to_chunks(v), to_chunks(g), to_chunks(beta)
    g = jnp.cumsum(g, axis=-1)
    tril = jnp.tril(jnp.ones((L, L), dtype=bool))
    strict = jnp.tril(jnp.ones((L, L), dtype=bool), -1)
    diff = g[..., :, None] - g[..., None, :]
    decay = jnp.where(tril, jnp.exp(jnp.where(tril, diff, 0.0)), 0.0)
    k_beta = k * beta[..., None]
    v_beta = v * beta[..., None]
    a_low = jnp.where(strict, jnp.einsum('bhnid,bhnjd->bhnij', k_beta, k) * decay, 0.0)
    t_mat = a_low + jnp.eye(L, dtype=jnp.float32)
    u = lax.linalg.triangular_solve(t_mat, v_beta, left_side=True, lower=True, unit_diagonal=True)
    w = lax.linalg.triangular_solve(t_mat, k_beta * jnp.exp(g)[..., None], left_side=True,
                                    lower=True, unit_diagonal=True)
    qk = jnp.einsum('bhnid,bhnjd->bhnij', q, k) * decay
    g_last = g[..., -1]
    k_dec = k * jnp.exp(g_last[..., None] - g)[..., None]
    q_dec = q * jnp.exp(g)[..., None]
    xs = tuple(jnp.moveaxis(t, 2, 0) for t in (q_dec, qk, u, w, k_dec, g_last))

    def step(state, inp):
        q_i, qk_i, u_i, w_i, kd_i, gl_i = inp
        v_new = u_i - jnp.einsum('bhld,bhde->bhle', w_i, state)
        o = jnp.einsum('bhld,bhde->bhle', q_i, state) + jnp.einsum('bhij,bhje->bhie', qk_i, v_new)
        state = state * jnp.exp(gl_i)[..., None, None] + jnp.einsum('bhld,bhle->bhde', kd_i, v_new)
        return state, o

    state0 = jnp.zeros((b_, h_, dk, dv), jnp.float32)
    _, o = lax.scan(step, state0, xs)
    o = jnp.moveaxis(o, 0, 2).reshape(b_, h_, s_, dv)
    return jnp.moveaxis(o, 1, 2)

def cross_attention(h, mem_n, wq, wk, wv, wo):
    b_, s_, _ = h.shape
    m_ = mem_n.shape[1]
    q = (h @ wq).reshape(b_, s_, XA_HEADS, XA_HEAD_DIM)
    k = (mem_n @ wk).reshape(b_, m_, XA_HEADS, XA_HEAD_DIM)
    v = (mem_n @ wv).reshape(b_, m_, XA_HEADS, XA_HEAD_DIM)
    s = jnp.einsum('bshd,bmhd->bhsm', q, k).astype(jnp.float32) * (XA_HEAD_DIM ** -0.5)
    p = jax.nn.softmax(s, axis=-1).astype(v.dtype)
    o = jnp.einsum('bhsm,bmhd->bshd', p, v).reshape(b_, s_, XA_WIDTH)
    return o @ wo

def swiglu(h, w_gate, w_up, w_down):
    return (jax.nn.silu(h @ w_gate) * (h @ w_up)) @ w_down

def moe_swiglu(h, w_router, w_gate, w_up, w_down):
    logits = (h @ w_router).astype(jnp.float32)
    top_val, top_idx = lax.top_k(logits, TOP_K)
    top_w = jax.nn.softmax(top_val, axis=-1)
    comb = jnp.sum(jax.nn.one_hot(top_idx, N_EXPERTS, dtype=jnp.float32) * top_w[..., None], axis=-2)
    comb = comb.astype(h.dtype)
    out = jnp.zeros_like(h)
    for e in range(N_EXPERTS):
        out = out + comb[..., e:e + 1] * swiglu(h, w_gate[e], w_up[e], w_down[e])
    return out

def setup_inputs(seed: int = 0) -> dict:
    key = jax.random.key(seed)
    ks = iter(jax.random.split(key, 48))
    f32 = jnp.float32

    def nrm(shape, scale):
        return jax.random.normal(next(ks), shape, f32) * scale

    def gain(shape):
        return 1.0 + 0.02 * jax.random.normal(next(ks), shape, f32)

    def log_uniform(shape, lo, hi):
        return jax.random.uniform(next(ks), shape, f32, math.log(lo), math.log(hi))

    x = nrm((BATCH, SEQ, D_MODEL), 1.0)
    mem = nrm((BATCH, N_MEM, D_MODEL), 1.0)
    positions = (jax.random.randint(next(ks), (BATCH, 1), 0, 1024)
                 + jnp.arange(SEQ, dtype=jnp.int32)[None, :]).astype(jnp.int32)
    norm_mix = gain((DEPTH, D_MODEL))
    w_in = nrm((DEPTH, D_MODEL, D_IN), D_MODEL ** -0.5)
    n_idx = jnp.arange(SSM_STATE, dtype=f32)
    ssm_a_re = -0.5 + nrm((DEPTH, SSM_GROUPS, SSM_STATE), 0.01)
    ssm_a_im = math.pi * n_idx + nrm((DEPTH, SSM_GROUPS, SSM_STATE), 0.01)
    ssm_log_dt = log_uniform((DEPTH, SSM_GROUPS), DT_MIN, DT_MAX)
    ssm_b_re = nrm((DEPTH, SSM_GROUPS, SSM_STATE, SSM_GROUP), (2 * SSM_GROUP) ** -0.5)
    ssm_b_im = nrm((DEPTH, SSM_GROUPS, SSM_STATE, SSM_GROUP), (2 * SSM_GROUP) ** -0.5)
    ssm_c_re = nrm((DEPTH, SSM_GROUPS, SSM_GROUP, SSM_STATE), 0.5 ** 0.5)
    ssm_c_im = nrm((DEPTH, SSM_GROUPS, SSM_GROUP, SSM_STATE), 0.5 ** 0.5)
    ssm_d = nrm((DEPTH, SSM_WIDTH), 1.0)
    ssm_w_glu = nrm((DEPTH, SSM_WIDTH, 2 * D_MODEL), SSM_WIDTH ** -0.5)
    gdn_conv = nrm((DEPTH, GDN_CONV, 3 * GDN_WIDTH), GDN_CONV ** -0.5)
    gdn_a_log = jnp.log(jax.random.uniform(next(ks), (DEPTH, GDN_HEADS), f32, 1.0, 16.0))
    dt = jnp.exp(log_uniform((DEPTH, GDN_HEADS), DT_MIN, DT_MAX))
    gdn_dt_bias = dt + jnp.log(-jnp.expm1(-dt))
    gdn_norm = gain((DEPTH, GDN_HEAD_DIM))
    w_up_moba = nrm((DEPTH, MOBA_WIDTH, D_MODEL), MOBA_WIDTH ** -0.5)
    w_up_gdn = nrm((DEPTH, GDN_WIDTH, D_MODEL), GDN_WIDTH ** -0.5)
    w_out = nrm((DEPTH, D_MODEL, D_MODEL), D_MODEL ** -0.5)
    norm_xa = gain((DEPTH, D_MODEL))
    norm_mem = gain((DEPTH, D_MODEL))
    xa_wq = nrm((DEPTH, D_MODEL, XA_WIDTH), D_MODEL ** -0.5)
    xa_wk = nrm((DEPTH, D_MODEL, XA_WIDTH), D_MODEL ** -0.5)
    xa_wv = nrm((DEPTH, D_MODEL, XA_WIDTH), D_MODEL ** -0.5)
    xa_wo = nrm((DEPTH, XA_WIDTH, D_MODEL), XA_WIDTH ** -0.5)
    norm_ffn = gain((DEPTH, D_MODEL))
    ffn_w_gate = nrm((N_DENSE, D_MODEL, D_FF), D_MODEL ** -0.5)
    ffn_w_up = nrm((N_DENSE, D_MODEL, D_FF), D_MODEL ** -0.5)
    ffn_w_down = nrm((N_DENSE, D_FF, D_MODEL), D_FF ** -0.5)
    moe_w_router = nrm((N_MOE, D_MODEL, N_EXPERTS), D_MODEL ** -0.5)
    moe_w_gate = nrm((N_MOE, N_EXPERTS, D_MODEL, D_FF), D_MODEL ** -0.5)
    moe_w_up = nrm((N_MOE, N_EXPERTS, D_MODEL, D_FF), D_MODEL ** -0.5)
    moe_w_down = nrm((N_MOE, N_EXPERTS, D_FF, D_MODEL), D_FF ** -0.5)
    norm_final = gain((D_MODEL,))
    return {"x": x, "mem": mem, "positions": positions, "norm_mix": norm_mix, "w_in": w_in,
            "ssm_a_re": ssm_a_re, "ssm_a_im": ssm_a_im, "ssm_log_dt": ssm_log_dt,
            "ssm_b_re": ssm_b_re, "ssm_b_im": ssm_b_im, "ssm_c_re": ssm_c_re, "ssm_c_im": ssm_c_im,
            "ssm_d": ssm_d, "ssm_w_glu": ssm_w_glu, "gdn_conv": gdn_conv, "gdn_a_log": gdn_a_log,
            "gdn_dt_bias": gdn_dt_bias, "gdn_norm": gdn_norm, "w_up_moba": w_up_moba,
            "w_up_gdn": w_up_gdn, "w_out": w_out, "norm_xa": norm_xa, "norm_mem": norm_mem,
            "xa_wq": xa_wq, "xa_wk": xa_wk, "xa_wv": xa_wv, "xa_wo": xa_wo, "norm_ffn": norm_ffn,
            "ffn_w_gate": ffn_w_gate, "ffn_w_up": ffn_w_up, "ffn_w_down": ffn_w_down,
            "moe_w_router": moe_w_router, "moe_w_gate": moe_w_gate, "moe_w_up": moe_w_up,
            "moe_w_down": moe_w_down, "norm_final": norm_final}

def reference(x, mem, positions, norm_mix, w_in, ssm_a_re, ssm_a_im, ssm_log_dt, ssm_b_re, ssm_b_im,
              ssm_c_re, ssm_c_im, ssm_d, ssm_w_glu, gdn_conv, gdn_a_log, gdn_dt_bias, gdn_norm,
              w_up_moba, w_up_gdn, w_out, norm_xa, norm_mem, xa_wq, xa_wk, xa_wv, xa_wo, norm_ffn,
              ffn_w_gate, ffn_w_up, ffn_w_down, moe_w_router, moe_w_gate, moe_w_up, moe_w_down,
              norm_final):
    b_, s_, _ = x.shape
    cos, sin = rope_tables(positions)
    for l in range(DEPTH):
        h = rms_norm(x, norm_mix[l])
        (q_m, k_m, v_m, u_s, q_g, k_g, v_g, a_g, b_g, z_g,
         gate_a, gate_b, gate_c) = split_columns(h @ w_in[l])
        q_m = apply_rope(q_m.reshape(b_, s_, MOBA_HEADS, MOBA_HEAD_DIM), cos, sin)
        k_m = apply_rope(k_m.reshape(b_, s_, MOBA_HEADS, MOBA_HEAD_DIM), cos, sin)
        v_m = v_m.reshape(b_, s_, MOBA_HEADS, MOBA_HEAD_DIM)
        y_a = moba_attention(q_m, k_m, v_m) @ w_up_moba[l]
        y_s = jax.nn.gelu(s5_ssm(u_s, ssm_a_re[l], ssm_a_im[l], ssm_log_dt[l], ssm_b_re[l], ssm_b_im[l],
                                 ssm_c_re[l], ssm_c_im[l], ssm_d[l]))
        glu_a, glu_b = jnp.split(y_s @ ssm_w_glu[l], 2, axis=-1)
        y_b = glu_a * jax.nn.sigmoid(glu_b)
        qkv = jax.nn.silu(causal_conv(jnp.concatenate([q_g, k_g, v_g], axis=-1), gdn_conv[l]))
        q_g, k_g, v_g = jnp.split(qkv, 3, axis=-1)
        q_g = l2_norm(q_g.reshape(b_, s_, GDN_HEADS, GDN_HEAD_DIM))
        k_g = l2_norm(k_g.reshape(b_, s_, GDN_HEADS, GDN_HEAD_DIM))
        v_g = v_g.reshape(b_, s_, GDN_HEADS, GDN_HEAD_DIM)
        beta = jax.nn.sigmoid(b_g.astype(jnp.float32))
        log_decay = -jnp.exp(gdn_a_log[l].astype(jnp.float32)) * jax.nn.softplus(
            a_g.astype(jnp.float32) + gdn_dt_bias[l].astype(jnp.float32))
        o_g = gated_delta_rule(q_g, k_g, v_g, log_decay, beta).astype(h.dtype)
        o_g = rms_norm(o_g, gdn_norm[l]) * jax.nn.silu(z_g.reshape(b_, s_, GDN_HEADS, GDN_HEAD_DIM))
        y_c = o_g.reshape(b_, s_, GDN_WIDTH) @ w_up_gdn[l]
        merged = (jax.nn.sigmoid(gate_a) * y_a + jax.nn.sigmoid(gate_b) * y_b
                  + jax.nn.sigmoid(gate_c) * y_c)
        x = x + merged @ w_out[l]
        x = x + cross_attention(rms_norm(x, norm_xa[l]), rms_norm(mem, norm_mem[l]),
                                xa_wq[l], xa_wk[l], xa_wv[l], xa_wo[l])
        h = rms_norm(x, norm_ffn[l])
        if l % 2 == 0:
            x = x + swiglu(h, ffn_w_gate[l // 2], ffn_w_up[l // 2], ffn_w_down[l // 2])
        else:
            x = x + moe_swiglu(h, moe_w_router[l // 2], moe_w_gate[l // 2], moe_w_up[l // 2],
                               moe_w_down[l // 2])
    return rms_norm(x, norm_final)


_drawn_inputs = setup_inputs


def setup_inputs(seed=0):
    import zlib

    import numpy as np

    out = dict(_drawn_inputs(seed))
    spreads = {}
    factors = {'ssm_a_re': 42.881,
     'gdn_norm': 5.074,
     'norm_xa': 8.0,
     'norm_mem': 7.779,
     'norm_final': 8.654,
     'norm_ffn': 4.378}
    for name, (base, spread) in spreads.items():
        noise = np.random.default_rng([zlib.crc32(name.encode()), seed]).standard_normal(out[name].shape)
        drawn = base * np.exp(spread * noise) if base else spread * noise
        out[name] = __import__('jax').numpy.asarray(drawn.astype(out[name].dtype))
    for name, factor in factors.items():
        out[name] = (out[name] * factor).astype(out[name].dtype)
    return out
```

```python
import math
from contextlib import ExitStack

import concourse.bass as bass
from concourse import mybir


def hybrid_trunk(nc: bass.Bass, x_d, mem_d, positions_d, norm_mix_d, w_in_d, a_re_d, a_im_d, log_dt_d,
                 b_re_d, b_im_d, c_re_d, c_im_d, ssm_d_d, w_glu_d, conv_d, a_log_d, dt_bias_d,
                 gdn_norm_d, w_up_moba_d, w_up_gdn_d, w_out_d, norm_xa_d, norm_mem_d, wq_d, wk_d, wv_d,
                 wo_d, norm_ffn_d, ffn_gate_d, ffn_up_d, ffn_down_d, router_d, moe_gate_d, moe_up_d,
                 moe_down_d, norm_final_d, out_d):
    F32 = mybir.dt.float32
    I32 = mybir.dt.int32
    ALU = mybir.AluOpType
    ACT = mybir.ActivationFunctionType
    AX = mybir.AxisListType

    P = 128
    SEQ, D = x_d.shape[1], x_d.shape[2]
    DEPTH = w_in_d.shape[0]
    NT = SEQ // P
    KD = D // P
    W = w_up_moba_d.shape[1]
    KW = W // P
    EPS = 1e-6
    NEG = -1e30
    MH, MD = 8, 64
    GH, GD, GL = 4, 128, 64
    NCHUNK = SEQ // GL
    XH, XD = 4, 128
    NS5 = 16
    NQ = 4
    D_FF = ffn_gate_d.shape[2]
    FC = 256
    NCH = D_FF // FC
    NE = moe_gate_d.shape[1]
    THETA = 10000.0
    TWO_PI = 2.0 * math.pi
    C1 = 6.28125
    C2 = TWO_PI - C1
    MAGIC = 1.5 * 2.0 ** 23
    PI_IN = 3.141592
    GELU_C = math.sqrt(2.0 / math.pi)
    NSLOT = 3
    SLOT = 6144
    IN_U, IN_QG, IN_KG, IN_VG, IN_AB, IN_Z, IN_GATE = 1536, 2048, 2560, 3072, 3584, 3592, 4104

    def in_cols(l, c0):
        return [(w_in_d[l].rearrange("(k p) n -> p k n", p=P)[:, :, c0:c0 + 512], 0, 512)]

    def half_width(w, l):
        return [(w[l].rearrange("(k p) n -> p k n", p=P), 0, D)]

    def glu_cols(l, n):
        v = w_glu_d[l].rearrange("(k p) (s n) -> s p k n", p=P, s=2)
        return [(v[s, :, :, n * 512:(n + 1) * 512], s * 512, D) for s in range(2)]

    def out_cols(l, n):
        return [(w_out_d[l].rearrange("(k p) n -> p k n", p=P)[:, :, n * 512:(n + 1) * 512], 0, 512)]

    def full_width(w, l):
        return [(w[l].rearrange("(k p) n -> p k n", p=P), 0, 512)]

    def mixer_units(l):
        return ([in_cols(l, c) for c in (IN_U, 0, 512, 1024, IN_Z)]
                + [in_cols(l, IN_GATE + 512 * g) for g in range(6)]
                + [in_cols(l, c) for c in (IN_QG, IN_KG, IN_VG)]
                + [half_width(w_up_moba_d, l), glu_cols(l, 0), glu_cols(l, 1), half_width(w_up_gdn_d, l),
                   out_cols(l, 0), out_cols(l, 1), full_width(wk_d, l), full_width(wv_d, l),
                   full_width(wq_d, l), half_width(wo_d, l)])

    U_U, U_Q, U_CONV = 0, 1, 11
    U_UPM, U_GLU, U_UPG, U_OUT, U_WK, U_WV, U_WQ, U_WO = 14, 15, 17, 18, 20, 21, 22, 23
    NUNIT = 24

    def experts(l):
        return 1 if l % 2 == 0 else NE

    def unit_base(l):
        return sum(NUNIT + NCH * experts(m) for m in range(l))

    def glu_extra(j):
        return 2 if j in (U_GLU, U_GLU + 1) else 1

    def slot_before(l, s):
        n = 0
        for m in range(l):
            n += sum(glu_extra(j) for j in range(NUNIT) if j % NSLOT == s)
            n += 3 * experts(m) * len([c for c in range(NCH) if c % NSLOT == s])
        return n

    def slot_after_unit(l, j):
        s = j % NSLOT
        return 16 * (slot_before(l, s) + sum(glu_extra(i) for i in range(j + 1) if i % NSLOT == s))

    def slot_after_chunk(l, e, c_in_slot, s):
        per_expert = 3 * len([c for c in range(NCH) if c % NSLOT == s])
        start = slot_before(l, s) + sum(glu_extra(i) for i in range(NUNIT) if i % NSLOT == s)
        return 16 * start + e * (16 * per_expert) + 48 * c_in_slot + 48

    ctx = ExitStack()
    with ctx:
        def sb(name, shape, dt=F32):
            return ctx.enter_context(nc.sbuf_tensor(name, shape, dt))

        def sem(name):
            return ctx.enter_context(nc.semaphore(name))

        class Region:

            def __init__(self, buf, end):
                self.buf, self.at, self.end = buf, 0, end

            def take(self, *shape):
                n = int(math.prod(shape))
                v = self.buf[:, self.at:self.at + n]
                self.at += n
                assert self.at <= self.end, (self.at, self.end)
                if len(shape) > 1:
                    names = "abcd"[:len(shape)]
                    v = v.rearrange(f"p ({' '.join(names)}) -> p {' '.join(names)}",
                                    **{n_: s for n_, s in zip(names, shape)})
                return v

        ring = sb("ring", [P, NSLOT * SLOT])
        x = sb("x", [P, NT, D])
        hT = sb("hT", [P, KD, SEQ])
        memT = sb("memT", [P, KD, SEQ])
        qk = sb("qk", [P, 2, NT, W])
        v_tok = sb("v_tok", [P, NT, W])
        z_tok = sb("z_tok", [P, NT, W])
        gates = sb("gates", [P, NT, 3 * D])
        uT = sb("uT", [P, NQ, SEQ])
        yT = sb("yT", [P, NQ, SEQ])
        RAW = SEQ + 3
        PH = 11776
        phase = sb("phase", [P, PH])
        raw = phase[:, 8192:8192 + 12 * RAW].rearrange("p (j n) -> p j n", n=RAW)
        merged = qk[:, :, :, :].rearrange("p a t n -> p (a t n)").rearrange("p (t n) -> p t n", t=NT)
        h_tok = gates[:, :, :].rearrange("p t n -> p (t n)")[:, 0:NT * D].rearrange("p (t n) -> p t n", t=NT)
        gain_out = gates[:, :, :].rearrange("p t n -> p (t n)")[:, NT * D:NT * D + D]
        spare = [ring[:, s * SLOT + 4096:(s + 1) * SLOT] for s in range(NSLOT)]

        def spare_half(s, i):
            return spare[s][:, i * 1024:(i + 1) * 1024]

        ident = sb("ident", [P, P])
        ones = sb("ones", [P, P])
        cum_mask = sb("cum_mask", [P, P])
        level_mask = sb("level_mask", [P, 6, P])
        causal = sb("causal", [P, 3 * P])
        b_mask = sb("b_mask", [P, NQ, 8, 16])
        c_mask = sb("c_mask", [P, NQ, 2, 64])
        steps = sb("steps", [P, SEQ])
        inv_freq = sb("inv_freq", [P, MD // 2])
        params = sb("params", [P, 3 * P])
        small_bc = sb("small_bc", [P, DEPTH, 2, GH])
        gnorm_bc = sb("gnorm_bc", [P, DEPTH, GD])
        cosr = sb("cosr", [P, NT, MD // 2])
        sinr = sb("sinr", [P, NT, MD // 2])
        pos_i = sb("pos_i", [P, NT], I32)
        pos_f = sb("pos_f", [P, NT])
        s5c = sb("s5c", [P, 14, DEPTH * NS5])
        idx8 = sb("idx8", [P, 8])
        eps_col = sb("eps_col", [P, 3])
        router_w = sb("router_w", [P, KD, NE])
        ab_w = sb("ab_w", [P, KD, 2 * GH])
        st = sb("st", [P, 96])

        NG = DEPTH * KD
        gain_mix, gain_xa, gain_mem, gain_ffn = (params[:, i * NG:(i + 1) * NG] for i in range(4))
        p_are = params[:, 64:96]
        p_aim = params[:, 96:128]
        p_conv = params[:, 128:224]
        p_dt = params[:, 224:256]
        p_d = params[:, 256:264]
        DEC, THR, BCR, BCI = (s5c[:, i, :] for i in range(4))

        ss, rstd = st[:, 0:2], st[:, 2:4]
        mx, nm, rs = st[:, 4:8], st[:, 8:12], st[:, 12:16]
        ab = st[:, 16:32]
        gate_z, gate_e = st[:, 32:40], st[:, 40:48]
        gcum, beta = st[:, 48:56], st[:, 56:64]
        bexp = st[:, 64:72]
        kds = st[:, 72:80]
        gstep = st[:, 80:88]
        ealog = st[:, 88:92]

        r5 = Region(phase, PH)
        tab = [r5.take(NQ, 2, SEQ) for _ in range(2)]
        bct = [[r5.take(NQ, P) for _ in range(4)] for _ in range(2)]
        c_nat = r5.take(2, NQ, 64)
        b_bar = r5.take(2, NS5, 16)
        wk5 = [r5.take(2, SEQ) for _ in range(5)]
        ang, turns = spare_half(0, 0), spare_half(0, 1)
        s_half = spare_half(1, 0)
        pads = spare_half(1, 1).rearrange("p (c n) -> p c n", c=2)
        y5 = yT[:, :, :]
        b_nat = spare_half(2, 0)[:, 0:2 * NS5 * 16].rearrange("p (c t n) -> p c t n", c=2, t=NS5)
        y5b = spare_half(2, 1).rearrange("p (c n) -> p c n", n=SEQ)

        rm = Region(phase, PH)
        mqT, mkT = rm.take(KW, SEQ), rm.take(KW, SEQ)
        m_oT = rm.take(KW, SEQ)
        mp_ = [rm.take(3 * P) for _ in range(2)]
        mpT = [rm.take(3 * P) for _ in range(2)]
        glu_t = [rm.take(512) for _ in range(2)]
        glu_y = [rm.take(512) for _ in range(2)]
        gl_tmp = [rm.take(512) for _ in range(2)]

        rg = Region(phase, PH)
        cv = rg.take(12, SEQ)
        k_tok = rg.take(NT, GH, GD)
        kbeg = rg.take(NT, GH, GD)
        vbeta = rg.take(NT, GH, GD)
        kdec = rg.take(NT, GH, GD)
        e_row = rg.take(NT, GH, P)
        dec = rg.take(NT, GH, P)
        decT = rg.take(NT, GH, P)
        qkT = rg.take(NT, GH, P)
        vn = rg.take(GH, GD)
        wT, u_tok = dec, decT
        o_tok, g_oT = k_tok, kbeg.rearrange("p t h d -> p (t h d)").rearrange("p (k n) -> p k n", k=KW)
        Xi = uT[:, :, :].rearrange("p q n -> p (q n)").rearrange("p (t h n) -> p t h n", t=NT, h=GH)
        Zi = yT[:, :, :].rearrange("p q n -> p (q n)").rearrange("p (t h n) -> p t h n", t=NT, h=GH)
        state = v_tok[:, :, :].rearrange("p t (h n) -> p t h n", h=GH)
        rq = [kbeg, vbeta, kdec, qkT]
        A_low, M_lvl, W_lvl, DTm, Dcl, gdiag = (
            spare_half(i // 2, i % 2).rearrange("p (t h n) -> p t h n", t=NT, h=GH) for i in range(6))

        rx = Region(phase, PH)
        memnT = rx.take(KD, SEQ)
        xkT, xqT, x_oT = rx.take(XH, SEQ), rx.take(XH, SEQ), rx.take(XH, SEQ)
        x_v = rx.take(NT, W)
        xp = [rx.take(NT, SEQ) for _ in range(2)]
        xpT = [rx.take(NT, SEQ) for _ in range(2)]

        rf = Region(phase, PH)
        f_th = [rf.take(FC) for _ in range(NT)]
        f_a = [rf.take(FC) for _ in range(NT)]
        f_act = [rf.take(FC) for _ in range(NT)]
        f_actT = rf.take(FC // P, SEQ)
        comb = rf.take(NT, NE)
        r_log = rf.take(NT, NE)
        r_max = rf.take(NT, NE)
        r_w = rf.take(NT, 4)
        r_eq = rf.take(2, NT, NE)
        r_idx = sb("r_idx", [P, NT, NE], mybir.dt.uint32)
        r_idf = rf.take(NT, NE)

        B = [ctx.enter_context(nc.psum_tensor(f"bank{i}", [P, 512], F32)) for i in range(8)]

        x_in, mem_in, par_in, bc_in, rout_in = sem("x_in"), sem("mem_in"), sem("par_in"), sem("bc_in"), sem("rout_in")
        pos_in, fin_in, out_done = sem("pos_in"), sem("fin_in"), sem("out_done")
        slot_full = [sem(f"slot_full{s}") for s in range(NSLOT)]
        chunk_used = sem("chunk_used")
        ab_in, bc_nat_in = sem("ab_in"), sem("bc_nat_in")
        consts = sem("consts")
        pool_chain, act_chain, dve_chain = sem("pool_chain"), sem("act_chain"), sem("dve_chain")
        par_ps, par_ready = sem("par_ps"), sem("par_ready")
        norm_sq, norm_ss, norm_h, norm_ps, hT_ready = sem("norm_sq"), sem("norm_ss"), sem("norm_h"), sem("norm_ps"), sem("hT_ready")
        s5_dt, s5_ang, s5_sin, s5_const = sem("s5_dt"), sem("s5_ang"), sem("s5_sin"), sem("s5_const")
        rot_ang, rot_sin = sem("rot_ang"), sem("rot_sin")
        ws_ready, ws_evac = sem("ws_ready"), sem("ws_evac")
        ab_ps, ab_sb = sem("ab_ps"), sem("ab_sb")
        fill_ready, rope_done, fill_evac = sem("fill_ready"), sem("rope_done"), sem("fill_evac")
        tab_ang, tab_ready, tab_sin = sem("tab_ang"), sem("tab_ready"), sem("tab_sin")
        b_bar_ready, pad_ready, pad_ps, bct_ready = sem("b_bar_ready"), sem("pad_ready"), sem("pad_ps"), sem("bct_ready")
        bu_ready, bu_read, h_rot, y_read = sem("bu_ready"), sem("bu_read"), sem("h_rot"), sem("y_read")
        gel_in, gel_t, y_ready = sem("gel_in"), sem("gel_t"), sem("y_ready")
        mtr_ps, mtr_ready = sem("mtr_ps"), sem("mtr_ready")
        ms_ready, ms_neg, ms_exp, ms_norm, ms_tr, ms_pT, ms_o, ms_oT = (
            sem(n) for n in ("ms_ready", "ms_neg", "ms_exp", "ms_norm", "ms_tr", "ms_pT", "ms_o", "ms_oT"))
        up_ps, up_used = sem("up_ps"), sem("up_used")
        glu_ps, glu_th, glu_used = sem("glu_ps"), sem("glu_th"), sem("glu_used")
        cv_tap, cv_pre, cv_th, cv_ready, cv_sq, cv_ss, cv_rs, kq_ready = (
            sem(n) for n in ("cv_tap", "cv_pre", "cv_th", "cv_ready", "cv_sq", "cv_ss", "cv_rs", "kq_ready"))
        g_z, g_exp, g_ln, g_step, gc_ps, gc_sb, g_bexp, g_diag, row_ps = (
            sem(n) for n in ("g_z", "g_exp", "g_ln", "g_step", "gc_ps", "gc_sb", "g_bexp", "g_diag", "row_ps"))
        dec_in, dec_ready, kv_ps, kv_evac, kk_ps, a_ready, qk_ready = (
            sem(n) for n in ("dec_in", "dec_ready", "kv_ps", "kv_evac", "kk_ps", "a_ready", "qk_ready"))
        xz_init, m_ready, w_ps, w_evac, xz_ps, xz_ready = (
            sem(n) for n in ("xz_init", "m_ready", "w_ps", "w_evac", "xz_ps", "xz_ready"))
        uw_in, uw_ps, w_done, u_done, qd_ready = (sem(n) for n in ("uw_in", "uw_ps", "w_done", "u_done", "qd_ready"))
        s_init, vn_ps, vn_ready, o_ps, su_ps, s_ready, o_evac = (
            sem(n) for n in ("s_init", "vn_ps", "vn_ready", "o_ps", "su_ps", "s_ready", "o_evac"))
        og_ss, og_rs, og_ready, og_ps, og_T = sem("og_ss"), sem("og_rs"), sem("og_ready"), sem("og_ps"), sem("og_T")
        mg_ready, mg_ps, mg_T, wo_ps, wo_used = sem("mg_ready"), sem("mg_ps"), sem("mg_T"), sem("wo_ps"), sem("wo_used")
        memn_ready, xk_ps, xk_sb = sem("memn_ready"), sem("xk_ps"), sem("xk_sb")
        xs_ps, xs_neg, xs_exp, xs_norm, xs_tr, xs_pT, xs_o, xs_oT = (
            sem(n) for n in ("xs_ps", "xs_neg", "xs_exp", "xs_norm", "xs_tr", "xs_pT", "xs_o", "xs_oT"))
        xo_ps, xo_used = sem("xo_ps"), sem("xo_used")
        rl_ps, rl_sb, rl_d, rl_e, comb_ready = (sem(n) for n in ("rl_ps", "rl_sb", "rl_d", "rl_e", "comb_ready"))
        gu_ps, gu_th, gu_a, act_ready, act_tr, actT_ready, y_added = (
            sem(n) for n in ("gu_ps", "gu_th", "gu_a", "act_ready", "act_tr", "actT_ready", "y_added"))
        fin_ready = sem("fin_ready")

        NNORM = 3 * DEPTH + 1

        def multiplied(l, j):
            if j == U_U:
                return ws_ready, 8 * l + 2
            if j < U_CONV:
                return fill_ready, 20 * l + 2 * (j - U_Q) + 2
            if j < U_UPM:
                return ws_ready, 8 * l + 2 * (j - U_CONV) + 4
            return {U_UPM: (up_ps, 8 * l + 4), U_GLU: (glu_ps, 4 * l + 2), U_GLU + 1: (glu_ps, 4 * l + 4),
                    U_UPG: (up_ps, 8 * l + 8), U_OUT: (wo_ps, 4 * l + 2), U_OUT + 1: (wo_ps, 4 * l + 4),
                    U_WK: (xk_ps, 6 * l + 2), U_WV: (xk_ps, 6 * l + 4), U_WQ: (xk_ps, 6 * l + 6),
                    U_WO: (xo_ps, 4 * l + 4)}[j]

        def slot(j):
            return ring[:, (j % NSLOT) * SLOT:(j % NSLOT) * SLOT + SLOT]

        def experts_before(l):
            return sum(experts(m) for m in range(l))

        def chunks_of_expert(eng, chunk):
            chunk(0, 0, 0, True)
            loops = (NCH - 1) // NSLOT
            with eng.Fori(0, loops) as r:
                for i in range(NSLOT):
                    c = 1 + i
                    chunk(r * NSLOT + c, (r + c // NSLOT), c % NSLOT, False)
            for c in range(1 + loops * NSLOT, NCH):
                chunk(c, c // NSLOT, c % NSLOT, False)

        def over_experts(eng, l, body):
            if experts(l) == 1:
                body(0)
            else:
                with eng.Fori(0, experts(l)) as e:
                    body(e)

        block = ctx.enter_context(nc.Block())

        @block.sync
        def _(sp):
            x_v_ = x_d[0].rearrange("(t p) n -> p t n", p=P)
            sp.dma_start(x[:, :, :], x_v_).then_inc(x_in, 16)

            def load(pieces, l, j):
                for src, at, width in pieces:
                    n = src.shape[2]
                    dst = slot(j)[:, 0:4096].rearrange("p (k w) -> p k w", w=width)[:, :, at:at + n]
                    sp.dma_start(dst, src).then_inc(slot_full[j % NSLOT], 16)

            def layer_units(l):
                for j, pieces in enumerate(mixer_units(l)):
                    if j >= NSLOT:
                        sp.wait_ge(*multiplied(l, j - NSLOT))
                    elif l > 0:
                        sp.wait_ge(chunk_used, NCH * experts_before(l) - (1, 0, 2)[j])
                    load(pieces, l, j)

            def expert_chunks(l):
                if l % 2 == 0:
                    gate, up, down = (w[l // 2:l // 2 + 1] for w in (ffn_gate_d, ffn_up_d, ffn_down_d))
                else:
                    gate, up, down = (w[l // 2] for w in (moe_gate_d, moe_up_d, moe_down_d))
                gate = gate.rearrange("e (k p) (c f) -> e c p k f", p=P, f=FC)
                up = up.rearrange("e (k p) (c f) -> e c p k f", p=P, f=FC)
                down = down.rearrange("e (c k p) n -> e c p k n", p=P, k=FC // P)
                before = NCH * experts_before(l)

                def expert(e):
                    def chunk(c, s):
                        v = ring[:, s * SLOT:(s + 1) * SLOT]
                        gu = v[:, 0:4096].rearrange("p (k b f) -> p k b f", b=2, f=FC)
                        sp.dma_start(gu[:, :, 0, :], gate[e, c]).then_inc(slot_full[s], 16)
                        sp.dma_start(gu[:, :, 1, :], up[e, c]).then_inc(slot_full[s], 16)
                        sp.dma_start(v[:, 4096:6144].rearrange("p (k n) -> p k n", n=D),
                                     down[e, c]).then_inc(slot_full[s], 16)

                    for c in range(NSLOT):
                        sp.wait_ge(*multiplied(l, NUNIT - NSLOT + c))
                        if not isinstance(e, int):
                            sp.wait_ge(chunk_used, e * NCH + (before + c - (2, 2, 5)[c] + 1))
                        chunk(c, c)
                    loops = NCH // NSLOT - 1
                    with sp.Fori(0, loops) as r:
                        for i in range(NSLOT):
                            sp.wait_ge(chunk_used, e * NCH + r * NSLOT + (before + i + 1))
                            chunk(r * NSLOT + (NSLOT + i), i)
                    for c in range(NSLOT * (loops + 1), NCH):
                        sp.wait_ge(chunk_used, e * NCH + (before + c - NSLOT + 1))
                        chunk(c, c % NSLOT)
                if l % 2 == 0:
                    expert(0)
                else:
                    with sp.Fori(0, NE) as e:
                        expert(e)

            for l in range(DEPTH):
                layer_units(l)
                expert_chunks(l)
            sp.wait_ge(fin_ready, 1)
            sp.dma_start(out_d[0].rearrange("(t p) n -> p t n", p=P), x[:, :, :]).then_inc(out_done, 16)
            sp.wait_ge(out_done, 16)

        @block.gpsimd
        def _(pool):
            chain = [0]

            def link(ins):
                chain[0] += 1
                ins.then_inc(pool_chain, 1)
                pool.wait_ge(pool_chain, chain[0])

            def keep(v, pattern, base, cm):
                link(nc.gpsimd.affine_select(out=v, in_=v, pattern=pattern, base=base, channel_multiplier=cm,
                                             compare_op=ALU.is_ge, fill=0.0))

            link(nc.gpsimd.memset(ident[:, :], 0.0))
            nc.gpsimd.affine_select(out=ident[:, :], in_=ident[:, :], pattern=[[-1, P]], base=0,
                                    channel_multiplier=1, compare_op=ALU.not_equal,
                                    fill=1.0).then_inc(consts, 1)
            rows = phase[:, 0:3 * P].rearrange("p (a n) -> p a n", a=3)
            for i, w in enumerate((norm_mix_d, norm_xa_d, norm_mem_d, norm_ffn_d)):
                pool.dma_start(rows[i * NG:(i + 1) * NG, 0, :],
                               w.rearrange("l (k p) -> (l k) p", p=P)).then_inc(par_in, 16)
            pool.dma_start(rows[64:96, 0, :], a_re_d.rearrange("l (t g) s -> (l t) (g s)", g=2)).then_inc(par_in, 16)
            pool.dma_start(rows[96:128, 0, :], a_im_d.rearrange("l (t g) s -> (l t) (g s)", g=2)).then_inc(par_in, 16)
            pool.dma_start(rows[0:96, 1, :], conv_d.rearrange("l i (j p) -> (l i j) p", p=P)).then_inc(par_in, 16)
            dtr = phase[:, 3 * P:3 * P + 2]
            pool.dma_start(dtr[96:128, :], log_dt_d.rearrange("l (t g) -> (l t) g", g=2)).then_inc(par_in, 16)
            pool.dma_start(rows[0:8, 2, :], ssm_d_d.rearrange("l (k p) -> (l k) p", p=P)).then_inc(par_in, 16)
            link(nc.gpsimd.memset(ones[:, :], 1.0))
            for i, e in enumerate((EPS, 4.0 * EPS, 1.0)):
                nc.gpsimd.memset(eps_col[:, i:i + 1], e)
            for j in range(MD // 2):
                nc.gpsimd.memset(inv_freq[:, j:j + 1], THETA ** (-2.0 * j / MD))
            link(nc.gpsimd.iota(steps[:, :], pattern=[[1, SEQ]], base=0, channel_multiplier=0,
                                allow_small_or_imprecise_dtypes=True))
            link(nc.gpsimd.iota(idx8[:, :], pattern=[[1, 8]], base=0, channel_multiplier=0,
                                allow_small_or_imprecise_dtypes=True))
            pool.wait_ge(par_in, 16 * 9)
            link(nc.gpsimd.tensor_copy(rows[96:128, 1, :].rearrange("p (g s) -> p g s", g=2),
                                       dtr[96:128, :].unsqueeze(2).to_broadcast([32, 2, 64])))
            nc.gpsimd.memset(st[:, :], 0.0).then_inc(consts, 1)
            for m in (b_mask, c_mask):
                link(nc.gpsimd.memset(m[:, :, :, :], 1.0))
            keep(b_mask[:, :, :, :], [[128, NQ], [-64, 8], [0, 16]], 0, 1)
            keep(b_mask[:, :, :, :], [[-128, NQ], [64, 8], [0, 16]], 63, -1)
            keep(c_mask[:, :, :, :], [[-32, NQ], [-16, 2], [0, 64]], 0, 1)
            keep(c_mask[:, :, :, :], [[32, NQ], [16, 2], [0, 64]], 15, -1)
            link(nc.gpsimd.memset(cum_mask[:, :], 1.0))
            keep(cum_mask[:, :], [[1, P]], 0, -1)
            cm2 = cum_mask[:, :].rearrange("p (a b) -> p a b", b=GL)
            keep(cm2, [[-GL, P // GL], [0, GL]], 0, 1)
            keep(cm2, [[GL, P // GL], [0, GL]], GL - 1, -1)
            link(nc.gpsimd.memset(level_mask[:, :, :], 0.0))
            for k in range(6):
                b = 2 ** k
                q = level_mask[:, k, :].rearrange("p (a h b) -> p a h b", h=2, b=b)[:, :, 0, :]
                link(nc.gpsimd.memset(q, 1.0))
                keep(q, [[-2 * b, P // (2 * b)], [0, b]], -b, 1)
                keep(q, [[2 * b, P // (2 * b)], [0, b]], 2 * b - 1, -1)
            link(nc.gpsimd.memset(causal[:, :], 0.0))
            for at in (0, 2 * P):
                last = nc.gpsimd.affine_select(out=causal[:, at:at + P], in_=causal[:, at:at + P],
                                               pattern=[[-1, P]], base=0, channel_multiplier=1,
                                               compare_op=ALU.is_ge, fill=NEG)
            last.then_inc(consts, 1)

            def angle_table(l, q):
                n = NQ * l + q
                if n >= 1:
                    pool.wait_ge(tab_sin, n)
                a3 = ang.rearrange("p (c n) -> p c n", n=SEQ)
                th = THR[:, l * NS5 + NQ * q:l * NS5 + NQ * (q + 1)].unsqueeze(2).to_broadcast([P, NQ, SEQ])
                sx = steps[:, :].unsqueeze(1).to_broadcast([P, NQ, SEQ])
                link(nc.gpsimd.tensor_tensor(a3, th, sx, ALU.mult))
                link(nc.gpsimd.tensor_scalar(turns, ang, 1.0 / TWO_PI, MAGIC, ALU.mult, ALU.add))
                link(nc.gpsimd.tensor_scalar(turns, turns, -MAGIC, None, ALU.add))
                link(nc.gpsimd.tensor_scalar(s_half, turns, C1, None, ALU.mult))
                link(nc.gpsimd.tensor_tensor(ang, ang, s_half, ALU.subtract))
                link(nc.gpsimd.tensor_scalar(s_half, turns, C2, None, ALU.mult))
                link(nc.gpsimd.tensor_tensor(ang, ang, s_half, ALU.subtract))
                nc.gpsimd.tensor_scalar(ang, ang, PI_IN, -PI_IN, ALU.min, ALU.max).then_inc(tab_ang, 1)

            def pad_b(l, q):
                n = 2 * (NQ * l + q)
                if n >= 1:
                    pool.wait_ge(pad_ps, n)
                for c in range(2):
                    src = b_bar[:, c, NQ * q:NQ * (q + 1), :].unsqueeze(2).to_broadcast([P, NQ, 8, 16])
                    last = nc.gpsimd.tensor_tensor(pads[:, c, :].rearrange("p (t g n) -> p t g n", t=NQ, g=8),
                                                   src, b_mask[:, :, :, :], ALU.mult)
                    last.then_inc(pad_ready, 1)

            def pad_c(l, q):
                pool.wait_ge(pad_ps, 2 * (NQ * l + q) + 1)
                for c in range(2):
                    src = c_nat[:, c, q, :].unsqueeze(1).unsqueeze(1).to_broadcast([P, NQ, 2, 64])
                    last = nc.gpsimd.tensor_tensor(pads[:, c, :].rearrange("p (t g n) -> p t g n", t=NQ, g=2),
                                                   src, c_mask[:, :, :, :], ALU.mult)
                    last.then_inc(pad_ready, 1)

            for l in range(DEPTH):
                if l > 0:
                    pool.wait_ge(y_added, experts_before(l))
                if l > 0:
                    pool.wait_ge(hT_ready, 1 + 3 * l)
                pool.wait_ge(par_ready, 1)
                pool.dma_start(b_nat[:, 0], b_re_d[l].rearrange("(t g) s n -> (g s) t n", g=2)).then_inc(bc_nat_in, 16)
                pool.dma_start(b_nat[:, 1], b_im_d[l].rearrange("(t g) s n -> (g s) t n", g=2)).then_inc(bc_nat_in, 16)
                pool.dma_start(c_nat[:, 0], c_re_d[l].rearrange("(q g) n s -> (g n) q s", q=NQ)).then_inc(bc_nat_in, 16)
                pool.dma_start(c_nat[:, 1], c_im_d[l].rearrange("(q g) n s -> (g n) q s", q=NQ)).then_inc(bc_nat_in, 16)
                if l == 0:
                    pool.wait_ge(s5_const, 1)
                for q in range(NQ):
                    angle_table(l, q)
                    if q == 0:
                        pool.wait_ge(bc_nat_in, 64 * (l + 1))
                        pool.wait_ge(b_bar_ready, l + 1)
                    pad_b(l, q)
                    pad_c(l, q)
                for t in range(NT):
                    pool.wait_ge(a_ready, NT * l + t + 1)
                    for m in (Xi, Zi):
                        last = nc.gpsimd.tensor_copy(m[:, t], ident[:, :].unsqueeze(1).to_broadcast([P, GH, P]))
                        last.then_inc(xz_init, 1)
                for k in range(6):
                    for t in range(NT):
                        n = (6 * l + k) * NT + t
                        if k > 0:
                            pool.wait_ge(w_ps, n - NT + 1)
                        nc.gpsimd.tensor_tensor(M_lvl[:, t], A_low[:, t],
                                                level_mask[:, k, :].unsqueeze(1).to_broadcast([P, GH, P]),
                                                ALU.mult).then_inc(m_ready, 1)

        @block.scalar
        def _(act):
            chain = [0]

            def link(ins):
                chain[0] += 1
                ins.then_inc(act_chain, 1)
                act.wait_ge(act_chain, chain[0])

            act.dma_start(h_tok, mem_d[0].rearrange("(t p) n -> p t n", p=P)).then_inc(mem_in, 16)
            with nc.allow_non_contiguous_dma("one position per partition"):
                act.dma_start(pos_i[:, :], positions_d[0].rearrange("(t p) -> p t", p=P)).then_inc(pos_in, 16)
            for l in range(DEPTH):
                act.dma_start(small_bc[:, l, 0, :], a_log_d[l:l + 1, :].to_broadcast([P, GH])).then_inc(bc_in, 16)
                act.dma_start(small_bc[:, l, 1, :], dt_bias_d[l:l + 1, :].to_broadcast([P, GH])).then_inc(bc_in, 16)
                act.dma_start(gnorm_bc[:, l, :], gdn_norm_d[l:l + 1, :].to_broadcast([P, GD])).then_inc(bc_in, 16)
            act.dma_start(router_w[:, :, :], router_d[0].rearrange("(k p) n -> p k n", p=P)).then_inc(rout_in, 16)

            def load_ab(l):
                act.dma_start(ab_w[:, :, :], w_in_d[l].rearrange("(k p) n -> p k n", p=P)
                              [:, :, IN_AB:IN_AB + 2 * GH]).then_inc(ab_in, 16)

            load_ab(0)

            def sum_squares(src, n):
                for t in range(NT):
                    nc.scalar.activation(hT[:, :, :].rearrange("p k n -> p (k n)")[:, t * D:(t + 1) * D],
                                         src[:, t, :], ACT.Square,
                                         accum_out=ss[:, t:t + 1]).then_inc(norm_sq, 1)
                act.wait_ge(norm_sq, NT * (n + 1))
                link(nc.scalar.activation(ss, ss, ACT.Ln, scale=1.0 / D, bias=eps_col[:, 0:1]))
                nc.scalar.activation(rstd, ss, ACT.Exp, scale=-0.5).then_inc(norm_ss, 1)

            def evac_norm(n, dst, gain, at, done):
                for b in range(4):
                    act.wait_ge(norm_ps, 4 * n + b + 1)
                    for i in range(2):
                        k = 2 * b + i
                        if gain is None:
                            last = nc.scalar.activation(dst[:, k, :], B[4 + b][:, i * SEQ:(i + 1) * SEQ], ACT.Copy)
                        else:
                            last = nc.scalar.activation(dst[:, k, :], B[4 + b][:, i * SEQ:(i + 1) * SEQ], ACT.Copy,
                                                        scale=gain[:, at + k:at + k + 1])
                last.then_inc(done, 1)

            act.wait_ge(par_ps, 1)
            nc.scalar.activation(params[:, 0:2 * P + 8], B[0][:, 0:2 * P + 8], ACT.Copy).then_inc(par_ready, 1)
            act.wait_ge(mem_in, 16)
            act.wait_ge(consts, 2)
            sum_squares(h_tok, 0)
            evac_norm(0, memT[:, :, :], None, 0, hT_ready)

            act.wait_ge(par_ready, 1)
            nc.scalar.activation(s5c[:, 4, :], p_dt, ACT.Exp).then_inc(s5_dt, 1)
            act.wait_ge(s5_ang, 1)
            nc.scalar.activation(DEC, s5c[:, 5, :], ACT.Exp)
            nc.scalar.activation(s5c[:, 6, :], THR, ACT.Sin)
            nc.scalar.activation(s5c[:, 7, :], THR, ACT.Sin, scale=0.5).then_inc(s5_sin, 1)
            act.wait_ge(rot_ang, 1)
            link(nc.scalar.activation(sinr[:, :, :], cosr[:, :, :], ACT.Sin))
            nc.scalar.activation(cosr[:, :, :], cosr[:, :, :], ACT.Sin, scale=0.5).then_inc(rot_sin, 1)
            act.wait_ge(bc_in, 16 * 3 * DEPTH)

            def table(l, q):
                n = NQ * l + q
                if n >= 2:
                    act.wait_ge(h_rot, NS5 * l + NQ * (q - 2) + NQ if q >= 2 else NS5 * l)
                act.wait_ge(tab_ang, n + 1)
                T = tab[q % 2]
                nc.scalar.activation(T[:, :, 1, :], ang.rearrange("p (c n) -> p c n", n=SEQ), ACT.Sin)
                link(nc.scalar.activation(T[:, :, 0, :], ang.rearrange("p (c n) -> p c n", n=SEQ), ACT.Sin, scale=0.5))
                nc.scalar.activation(T[:, :, 0, :], T[:, :, 0, :], ACT.Square).then_inc(tab_sin, 1)

            def bct_evac(l, q):
                for half in range(2):
                    n = 2 * (NQ * l + q) + half
                    act.wait_ge(pad_ps, n + 1)
                    if NQ * l + q >= 2 and half == 0:
                        act.wait_ge(y_read, NQ * (NQ * l + q - 1))
                    for c in range(2):
                        last = nc.scalar.activation(bct[q % 2][2 * half + c].rearrange("p t n -> p (t n)"),
                                                    B[6 + c][:, :], ACT.Copy,
                                                    scale=-1.0 if (half == 1 and c == 1) else 1.0)
                    last.then_inc(bct_ready, 1)

            for l in range(DEPTH):
                n = 1 + 3 * l
                act.wait_ge(y_added, experts_before(l)) if l > 0 else act.wait_ge(x_in, 16)
                sum_squares(x[:, :, :], n)
                if l == 0:
                    act.wait_ge(par_ready, 1)
                evac_norm(n, hT[:, :, :], gain_mix, l * KD, hT_ready)
                table(l, 0)
                def ws_copy(w):
                    for b in range(2):
                        act.wait_ge(ws_ready, 8 * l + 2 * w + b + 1)
                        src = B[(2 if w == 2 else 0) + b][:, :].rearrange("p (c n) -> p c n", n=SEQ)
                        dst = (uT[:, 2 * b:2 * b + 2, :] if w == 0
                               else raw[:, 4 * (w - 1) + 2 * b:4 * (w - 1) + 2 * b + 2, 3:RAW])
                        nc.scalar.activation(dst, src, ACT.Copy).then_inc(ws_evac, 1)

                ws_copy(0)
                bct_evac(l, 0)
                act.wait_ge(ab_ps, l + 1)
                nc.scalar.activation(ab, B[4][:, 0:16], ACT.Copy).then_inc(ab_sb, 1)
                if l + 1 < DEPTH:
                    act.wait_ge(ab_ps, l + 1)
                    load_ab(l + 1)
                for f in range(4, 20):
                    i = f - 4
                    q, t = f // 2, f % 2
                    act.wait_ge(fill_ready, 20 * l + f + 1)
                    if q == 2:
                        nc.scalar.activation(v_tok[:, t, :], B[t][:, :], ACT.Copy).then_inc(fill_evac, 1)
                    elif q == 3:
                        nc.scalar.activation(z_tok[:, t, :], B[t][:, :], ACT.Copy).then_inc(fill_evac, 1)
                    else:
                        nc.scalar.activation(gates[:, t, (q - 4) * 512:(q - 3) * 512], B[t][:, :], ACT.Tanh,
                                             scale=0.5).then_inc(fill_evac, 1)
                    if i % NQ == 1 and i // NQ + 1 < NQ:
                        bct_evac(l, i // NQ + 1)
                    if i % NQ == 0 and i // NQ + 1 < NQ:
                        table(l, i // NQ + 1)
                for q in range(NQ):
                    act.wait_ge(gel_in, NQ * l + q + 1)
                    nc.scalar.activation(y5b[:, q, :], y5b[:, q, :], ACT.Tanh, scale=GELU_C).then_inc(gel_t, 1)
                act.wait_ge(y_ready, l + 1)
                for w in range(1, 4):
                    ws_copy(w)
                for i in range(4):
                    act.wait_ge(mtr_ps, 4 * l + i + 1)
                    dst = (mqT, mkT)[i // 2][:, :, (i % 2) * P:(i % 2 + 1) * P]
                    nc.scalar.activation(dst, B[4 + i][:, :].rearrange("p (k n) -> p k n", n=P),
                                         ACT.Copy).then_inc(mtr_ready, 1)

                def moba_exp(h):
                    n = MH * l + h
                    act.wait_ge(ms_neg, n + 1)
                    p = mp_[h % 2]
                    o = 2 * (h % 2)
                    nc.scalar.activation(p[:, 0:P], p[:, 0:P], ACT.Exp, bias=nm[:, o:o + 1], scale=MD ** -0.5,
                                         accum_out=rs[:, o:o + 1])
                    nc.scalar.activation(p[:, P:3 * P], p[:, P:3 * P], ACT.Exp, bias=nm[:, o + 1:o + 2],
                                         scale=MD ** -0.5, accum_out=rs[:, o + 1:o + 2]).then_inc(ms_exp, 1)

                def moba_pT(h):
                    n = MH * l + h
                    act.wait_ge(ms_tr, n + 1)
                    if n >= 2:
                        act.wait_ge(ms_o, n - 1)
                    nc.scalar.activation(mpT[h % 2], B[4 + h % 2][:, 0:3 * P], ACT.Copy).then_inc(ms_pT, 1)

                def moba_oT(j):
                    act.wait_ge(ms_o, MH * l + 2 * j + 2)
                    nc.scalar.activation(m_oT[:, j, :], B[6 + j % 2][:, 0:SEQ], ACT.Copy).then_inc(ms_oT, 1)

                for s in range(MH + 2):
                    if s < MH:
                        moba_exp(s)
                    if 1 <= s <= MH:
                        moba_pT(s - 1)
                    if s >= 3 and s % 2 == 1:
                        moba_oT((s - 3) // 2)
                for n_ in range(2):
                    for t in range(NT):
                        i = 2 * n_ + t
                        act.wait_ge(glu_ps, 4 * l + i + 1)
                        if i >= 2:
                            act.wait_ge(glu_used, 4 * l + i - 1)
                        nc.scalar.activation(glu_t[t], B[2 * t + 1][:, :], ACT.Tanh, scale=0.5).then_inc(glu_th, 1)
                act.wait_ge(glu_used, 4 * l + 4)
                for j in range(12):
                    last = nc.scalar.activation(cv[:, j, :], raw[:, j, 0:SEQ], ACT.Copy,
                                                scale=p_conv[:, 48 * l + j:48 * l + j + 1])
                    last.then_inc(cv_tap, 1)
                act.wait_ge(g_z, l + 1)
                nc.scalar.activation(ealog, small_bc[:, l, 0, :], ACT.Exp)
                link(nc.scalar.activation(gate_e, gate_e, ACT.Exp, scale=-1.0))
                nc.scalar.activation(gate_e, gate_e, ACT.Ln, bias=eps_col[:, 2:3]).then_inc(g_ln, 1)
                nc.scalar.activation(beta.rearrange("p (t h) -> p t h", t=NT),
                                     ab.rearrange("p (t c h) -> p t c h", t=NT, c=2)[:, :, 1, :],
                                     ACT.Tanh, scale=0.5).then_inc(g_exp, 1)
                for i in range(3):
                    act.wait_ge(cv_pre, 3 * l + i + 1)
                    tmp = (A_low, M_lvl, W_lvl)[i].rearrange("p t h n -> p (t h n)")
                    nc.scalar.activation(tmp, cv[:, 4 * i:4 * i + 4, :].rearrange("p c n -> p (c n)"), ACT.Tanh,
                                         scale=0.5).then_inc(cv_th, 1)
                for i in range(4):
                    act.wait_ge(cv_ready, 3 * l + i // 2 + 1)
                    tmp = (DTm, Dcl)[i // 2].rearrange("p t h n -> p (t h n)")[:, (i % 2) * 512:(i % 2 + 1) * 512]
                    nc.scalar.activation(tmp, cv[:, 2 * i:2 * i + 2, :].rearrange("p c n -> p (c n)"),
                                         ACT.Square).then_inc(cv_sq, 1)
                for i in range(4):
                    act.wait_ge(cv_ss, 4 * l + i + 1)
                    r_ = rq[i].rearrange("p t h n -> p (t h n)")[:, 0:512]
                    last = nc.scalar.activation(r_, B[4 + i][:, :], ACT.Ln, bias=eps_col[:, 1:2])
                link(last)
                for i in range(4):
                    r_ = rq[i].rearrange("p t h n -> p (t h n)")[:, 0:512]
                    nc.scalar.activation(r_, r_, ACT.Exp, scale=-0.5).then_inc(cv_rs, 1)
                act.wait_ge(gc_sb, l + 1)
                nc.scalar.activation(bexp, gcum, ACT.Exp).then_inc(g_bexp, 1)
                for t in range(NT):
                    act.wait_ge(dec_in, NT * l + t + 1)
                    nc.scalar.activation(e_row[:, t], B[2 + t][:, :].rearrange("p (h n) -> p h n", h=GH),
                                         ACT.Exp).then_inc(dec_ready, 1)
                    nc.scalar.activation(dec[:, t], Dcl[:, t], ACT.Exp, scale=-1.0).then_inc(dec_ready, 1)
                    nc.scalar.activation(decT[:, t], DTm[:, t], ACT.Exp).then_inc(dec_ready, 1)
                for t in range(NT):
                    act.wait_ge(kv_ps, 4 * l + t + 1)
                    nc.scalar.activation(k_tok[:, t], B[4 + t][:, :].rearrange("p (h n) -> p h n", h=GH),
                                         ACT.Copy).then_inc(kv_evac, 1)
                for k in range(6):
                    for t in range(NT):
                        n = (6 * l + k) * NT + t
                        act.wait_ge(w_ps, n + 1)
                        nc.scalar.activation(W_lvl[:, t], B[t][:, :].rearrange("p (h n) -> p h n", h=GH),
                                             ACT.Copy).then_inc(w_evac, 1)
                for t in range(NT):
                    act.wait_ge(uw_ps, NT * l + t + 1)
                    nc.scalar.activation(wT[:, t], B[t][:, :].rearrange("p (h n) -> p h n", h=GH),
                                         ACT.Copy).then_inc(w_done, 1)
                for c in range(NCHUNK):
                    rows_ = slice((c % 2) * GL, (c % 2 + 1) * GL)
                    act.wait_ge(o_ps, NCHUNK * l + c + 1)
                    nc.scalar.activation(o_tok[rows_, c // 2], B[5 + c % 2][rows_, :].rearrange("p (h n) -> p h n", h=GH),
                                         ACT.Copy).then_inc(o_evac, 1)
                nc.scalar.activation(gdiag.rearrange("p t h n -> p (t h n)"),
                                     z_tok[:, :, :].rearrange("p t n -> p (t n)"), ACT.Tanh,
                                     scale=0.5).then_inc(o_evac, 1)
                act.wait_ge(og_ss, l + 1)
                link(nc.scalar.activation(gate_z, gate_z, ACT.Ln, scale=1.0 / GD, bias=eps_col[:, 0:1]))
                nc.scalar.activation(gate_z, gate_z, ACT.Exp, scale=-0.5).then_inc(og_rs, 1)
                for t in range(NT):
                    act.wait_ge(og_ps, NT * l + t + 1)
                    nc.scalar.activation(g_oT[:, :, t * P:(t + 1) * P], B[4 + t][:, :].rearrange("p (k n) -> p k n", n=P),
                                         ACT.Copy).then_inc(og_T, 1)
                for b in range(4):
                    act.wait_ge(mg_ps, 4 * l + b + 1)
                    nc.scalar.activation(hT[:, 2 * b:2 * b + 2, :], B[4 + b][:, :].rearrange("p (c n) -> p c n", n=SEQ),
                                         ACT.Copy).then_inc(mg_T, 1)
                for k in range(KD):
                    last = nc.scalar.activation(memnT[:, k, :], memT[:, k, :], ACT.Copy,
                                                scale=gain_mem[:, l * KD + k:l * KD + k + 1])
                last.then_inc(memn_ready, 1)
                for b in range(2):
                    act.wait_ge(xk_ps, 6 * l + b + 1)
                    nc.scalar.activation(xkT[:, 2 * b:2 * b + 2, :], B[2 + b][:, :].rearrange("p (c n) -> p c n", n=SEQ),
                                         ACT.Copy).then_inc(xk_sb, 1)
                for b in range(2):
                    act.wait_ge(xk_ps, 6 * l + 2 + b + 1)
                    nc.scalar.activation(x_v[:, b, :], B[b][:, :], ACT.Copy).then_inc(xk_sb, 1)
                n = 2 + 3 * l
                act.wait_ge(wo_used, 4 * (l + 1))
                sum_squares(x[:, :, :], n)
                evac_norm(n, hT[:, :, :], gain_xa, l * KD, hT_ready)
                for b in range(2):
                    act.wait_ge(xk_ps, 6 * l + 4 + b + 1)
                    nc.scalar.activation(xqT[:, 2 * b:2 * b + 2, :], B[b][:, :].rearrange("p (c n) -> p c n", n=SEQ),
                                         ACT.Copy).then_inc(xk_sb, 1)

                def xa_exp(h):
                    n_ = XH * l + h
                    act.wait_ge(xs_neg, n_ + 1)
                    if n_ >= 2:
                        act.wait_ge(xs_tr, n_ - 1)
                    for t in range(NT):
                        o = 2 * (h % 2) + t
                        last = nc.scalar.activation(xp[h % 2][:, t, :], B[2 + h % 2][:, t * SEQ:(t + 1) * SEQ], ACT.Exp,
                                                    bias=nm[:, o:o + 1], scale=XD ** -0.5, accum_out=rs[:, o:o + 1])
                    last.then_inc(xs_exp, 1)

                def xa_pT(h):
                    n_ = XH * l + h
                    act.wait_ge(xs_tr, n_ + 1)
                    if n_ >= 2:
                        act.wait_ge(xs_o, n_ - 1)
                    nc.scalar.activation(xpT[h % 2], B[4 + h % 2][:, :].rearrange("p (c n) -> p c n", n=SEQ),
                                         ACT.Copy).then_inc(xs_pT, 1)

                def xa_oT(h):
                    act.wait_ge(xs_o, XH * l + h + 1)
                    nc.scalar.activation(x_oT[:, h, :], B[6 + h % 2][:, 0:SEQ], ACT.Copy).then_inc(xs_oT, 1)

                for s in range(XH + 2):
                    if s < XH:
                        xa_exp(s)
                    if 1 <= s <= XH:
                        xa_pT(s - 1)
                    if s >= 2:
                        xa_oT(s - 2)
                n = 3 + 3 * l
                act.wait_ge(xo_used, 4 * (l + 1))
                sum_squares(x[:, :, :], n)
                evac_norm(n, hT[:, :, :], gain_ffn, l * KD, hT_ready)
                if l % 2 == 1:
                    act.wait_ge(rl_d, l // 2 + 1)
                    nc.scalar.activation(r_w[:, :, 1:2], r_w[:, :, 0:1], ACT.Exp).then_inc(rl_e, 1)
                base = NCH * experts_before(l) * NT

                def expert(e):
                    def tail(c, t):
                        act.wait_ge(act_tr, e * (NCH * NT) + c * NT + (base + t + 1))
                        nc.scalar.activation(f_actT[:, :, t * P:(t + 1) * P],
                                             B[2 + t][:, 0:2 * P].rearrange("p (k n) -> p k n", n=P),
                                             ACT.Copy).then_inc(actT_ready, 1)

                    def chunk(c, in_slot, s, head):
                        for t in range(NT):
                            act.wait_ge(gu_ps, e * (NCH * NT) + c * NT + (base + t + 1))
                            if not (head and l == 0):
                                act.wait_ge(gu_a, e * (NCH * NT) + c * NT + (base + t + 1 - NT))
                            nc.scalar.activation(f_th[t], B[t][:, 0:FC], ACT.Tanh, scale=0.5).then_inc(gu_th, 1)
                            if t == 0 and not head:
                                tail(c - 1, 1)
                        tail(c, 0)
                    chunks_of_expert(act, chunk)
                    tail(NCH - 1, 1)
                over_experts(act, l, expert)
            act.wait_ge(y_added, experts_before(DEPTH))
            act.dma_start(gain_out, norm_final_d.rearrange("(a n) -> a n", a=1).to_broadcast([P, D])).then_inc(fin_in, 16)
            sum_squares(x[:, :, :], NNORM)

        @block.vector
        def _(dve):
            V = nc.vector
            chain = [0]

            def link(ins):
                chain[0] += 1
                ins.then_inc(dve_chain, 1)
                dve.wait_ge(dve_chain, chain[0])

            def normalise(src, dst, n):
                dve.wait_ge(norm_ss, n + 1)
                for t in range(NT):
                    V.tensor_scalar(dst[:, t, :], src[:, t, :], rstd[:, t:t + 1], None, ALU.mult).then_inc(norm_h, 1)

            def reduce_angle(a, tmp):
                link(V.tensor_scalar(tmp, a, 1.0 / TWO_PI, MAGIC, ALU.mult, ALU.add))
                link(V.tensor_scalar(tmp, tmp, -MAGIC, None, ALU.add))
                link(V.scalar_tensor_tensor(a, tmp, -C1, a, ALU.mult, ALU.add))
                link(V.scalar_tensor_tensor(a, tmp, -C2, a, ALU.mult, ALU.add))
                return V.tensor_scalar(a, a, PI_IN, -PI_IN, ALU.min, ALU.max)

            dve.wait_ge(mem_in, 16)
            normalise(h_tok, h_tok, 0)
            c_ = [s5c[:, i, :] for i in range(14)]
            dve.wait_ge(par_ready, 1)
            dve.wait_ge(s5_dt, 1)
            V.tensor_tensor(c_[5], c_[4], p_are, ALU.mult)
            link(V.tensor_tensor(THR, c_[4], p_aim, ALU.mult))
            reduce_angle(THR, c_[8]).then_inc(s5_ang, 1)
            dve.wait_ge(pos_in, 16)
            link(V.tensor_copy(pos_f[:, :], pos_i[:, :]))
            dve.wait_ge(consts, 2)
            for t in range(NT):
                link(V.tensor_scalar(cosr[:, t, :], inv_freq[:, :], pos_f[:, t:t + 1], None, ALU.mult))
            reduce_angle(cosr[:, :, :], sinr[:, :, :]).then_inc(rot_ang, 1)
            dve.wait_ge(s5_sin, 1)
            link(V.tensor_tensor(c_[7], c_[7], c_[7], ALU.mult))
            link(V.tensor_scalar(c_[7], c_[7], -2.0, 1.0, ALU.mult, ALU.add))
            link(V.tensor_tensor(c_[7], c_[7], DEC, ALU.mult))
            link(V.tensor_scalar(c_[7], c_[7], -1.0, None, ALU.add))
            link(V.tensor_tensor(c_[6], c_[6], DEC, ALU.mult))
            V.tensor_tensor(c_[8], p_are, p_are, ALU.mult)
            link(V.tensor_tensor(c_[9], p_aim, p_aim, ALU.mult))
            link(V.tensor_tensor(c_[8], c_[8], c_[9], ALU.add))
            link(V.reciprocal(c_[8], c_[8]))
            V.tensor_tensor(c_[9], c_[7], p_are, ALU.mult)
            V.tensor_tensor(c_[10], c_[6], p_aim, ALU.mult)
            V.tensor_tensor(c_[11], c_[6], p_are, ALU.mult)
            link(V.tensor_tensor(c_[12], c_[7], p_aim, ALU.mult))
            V.tensor_tensor(c_[9], c_[9], c_[10], ALU.add)
            link(V.tensor_tensor(c_[11], c_[11], c_[12], ALU.subtract))
            V.tensor_tensor(BCR, c_[9], c_[8], ALU.mult)
            V.tensor_tensor(BCI, c_[11], c_[8], ALU.mult).then_inc(s5_const, 1)
            dve.wait_ge(rot_sin, 1)
            link(V.tensor_tensor(cosr[:, :, :], cosr[:, :, :], cosr[:, :, :], ALU.mult))
            link(V.tensor_scalar(cosr[:, :, :], cosr[:, :, :], -2.0, 1.0, ALU.mult, ALU.add))
            dve.wait_ge(s5_const, 1)

            for l in range(DEPTH):
                if l == 0:
                    dve.wait_ge(x_in, 16)
                    dve.wait_ge(norm_ps, 4)
                normalise(x[:, :, :], h_tok, 1 + 3 * l)
                dve.wait_ge(bc_nat_in, 64 * (l + 1))
                cr = BCR[:, l * NS5:(l + 1) * NS5].unsqueeze(2).to_broadcast([P, NS5, 16])
                ci = BCI[:, l * NS5:(l + 1) * NS5].unsqueeze(2).to_broadcast([P, NS5, 16])
                tb = [wk5[i][:, 0, :].rearrange("p (t n) -> p t n", n=16) for i in range(4)]
                V.tensor_tensor(tb[0], b_nat[:, 0], cr, ALU.mult)
                V.tensor_tensor(tb[1], b_nat[:, 1], ci, ALU.mult)
                V.tensor_tensor(tb[2], b_nat[:, 0], ci, ALU.mult)
                link(V.tensor_tensor(tb[3], b_nat[:, 1], cr, ALU.mult))
                link(V.tensor_tensor(b_bar[:, 0], tb[0], tb[1], ALU.subtract))
                V.tensor_tensor(b_bar[:, 1], tb[2], tb[3], ALU.add).then_inc(b_bar_ready, 1)
                for f in range(4):
                    c, t = f // 2, f % 2
                    dve.wait_ge(fill_ready, 20 * l + f + 1)
                    src = B[t][:, :].rearrange("p (h c n) -> p h c n", c=2, n=MD // 2)
                    dst = qk[:, c, t, :].rearrange("p (h c n) -> p h c n", c=2, n=MD // 2)
                    cs = cosr[:, t, :].unsqueeze(1).to_broadcast([P, MH, MD // 2])
                    sn = sinr[:, t, :].unsqueeze(1).to_broadcast([P, MH, MD // 2])
                    tmp = wk5[3 + f % 2].rearrange("p a b -> p (a b)").rearrange("p (h c n) -> p h c n", c=2, n=MD // 2)
                    for i in range(2):
                        V.tensor_tensor(dst[:, :, i, :], src[:, :, i, :], cs, ALU.mult)
                    V.tensor_tensor(tmp[:, :, 0, :], src[:, :, 1, :], sn, ALU.mult)
                    link(V.tensor_tensor(tmp[:, :, 1, :], src[:, :, 0, :], sn, ALU.mult))
                    V.tensor_tensor(dst[:, :, 0, :], dst[:, :, 0, :], tmp[:, :, 0, :], ALU.subtract)
                    V.tensor_tensor(dst[:, :, 1, :], dst[:, :, 1, :], tmp[:, :, 1, :], ALU.add).then_inc(rope_done, 1)
                dve.wait_ge(rope_done, 4 * (l + 1))
                for i in range(NS5):
                    q, n = i // NQ, NS5 * l + i
                    T = tab[q % 2][:, i % NQ]
                    if i % NQ == 0:
                        dve.wait_ge(tab_sin, NQ * l + q + 1)
                        cosn = tab[q % 2][:, :, 0, :]
                        link(V.tensor_scalar(cosn, cosn, -2.0, 1.0, ALU.mult, ALU.add))
                    dve.wait_ge(bu_ready, n + 1)
                    bu = B[2 + n % 2][:, :].rearrange("p (c n) -> p c n", n=SEQ)
                    cs2 = T[:, 0, :].unsqueeze(1).to_broadcast([P, 2, SEQ])
                    sn = T[:, 1, :]
                    m1, m2, gin = wk5[0], wk5[1], wk5[2]
                    if n >= 1:
                        dve.wait_ge(h_rot, n)
                    V.tensor_tensor(m1, bu, cs2, ALU.mult)
                    V.tensor_tensor(m2[:, 0, :], bu[:, 1, :], sn, ALU.mult)
                    V.tensor_tensor(m2[:, 1, :], bu[:, 0, :], sn, ALU.mult).then_inc(bu_read, 1)
                    dve.wait_ge(bu_read, n + 1)
                    V.tensor_tensor(gin[:, 0, :], m1[:, 0, :], m2[:, 0, :], ALU.add)
                    link(V.tensor_tensor(gin[:, 1, :], m1[:, 1, :], m2[:, 1, :], ALU.subtract))
                    dc = DEC[:, NS5 * l + i:NS5 * l + i + 1].to_broadcast([P, SEQ])
                    for c in range(2):
                        last = V.tensor_tensor_scan(m1[:, c, :], dc, gin[:, c, :], 0.0, ALU.mult, ALU.add)
                    link(last)
                    hr = wk5[3 + n % 2]
                    if n >= 2:
                        dve.wait_ge(y_read, n - 1)
                    V.tensor_tensor(m2, m1, cs2, ALU.mult)
                    V.tensor_tensor(gin[:, 0, :], m1[:, 1, :], sn, ALU.mult)
                    link(V.tensor_tensor(gin[:, 1, :], m1[:, 0, :], sn, ALU.mult))
                    V.tensor_tensor(hr[:, 0, :], m2[:, 0, :], gin[:, 0, :], ALU.subtract)
                    V.tensor_tensor(hr[:, 1, :], m2[:, 1, :], gin[:, 1, :], ALU.add).then_inc(h_rot, 1)
                    if i % NQ == 0:
                        dve.wait_ge(h_rot, n + 1)
                    if i % NQ == NQ - 1:
                        dve.wait_ge(h_rot, n + 1)
                        dve.wait_ge(y_read, n + 1)
                        link(V.scalar_tensor_tensor(y5[:, q, :], uT[:, q, :], p_d[:, l * NQ + q:l * NQ + q + 1],
                                                    B[4 + q % 2][:, 0:SEQ], ALU.mult, ALU.add))
                        link(V.tensor_tensor(y5b[:, q, :], y5[:, q, :], y5[:, q, :], ALU.mult))
                        link(V.tensor_scalar(y5b[:, q, :], y5b[:, q, :], 0.044715, 1.0, ALU.mult, ALU.add))
                        V.tensor_tensor(y5b[:, q, :], y5b[:, q, :], y5[:, q, :], ALU.mult).then_inc(gel_in, 1)
                dve.wait_ge(gel_t, NQ * (l + 1))
                yflat = yT[:, :, :].rearrange("p q n -> p (q n)")
                link(V.scalar_tensor_tensor(yflat, y5b.rearrange("p q n -> p (q n)"), 1.0,
                                            y5.rearrange("p q n -> p (q n)"), ALU.add, ALU.mult))
                V.tensor_scalar(yflat, yflat, 0.5, None, ALU.mult).then_inc(y_ready, 1)
                link(V.memset(raw[:, :, 0:3], 0.0))
                def moba_max(h):
                    n = MH * l + h
                    p, o = mp_[h % 2], 2 * (h % 2)
                    dve.wait_ge(ms_ready, n + 1)
                    if n >= 2:
                        dve.wait_ge(ms_tr, n - 1)
                    link(V.tensor_tensor(p, B[2 + h % 2][:, 0:3 * P], causal[:, :], ALU.add))
                    V.tensor_reduce(mx[:, o:o + 1], p[:, 0:P], AX.X, ALU.max)
                    link(V.tensor_reduce(mx[:, o + 1:o + 2], p[:, P:3 * P], AX.X, ALU.max))
                    V.tensor_scalar(nm[:, o:o + 2], mx[:, o:o + 2], -MD ** -0.5, None, ALU.mult).then_inc(ms_neg, 1)

                def moba_norm(h):
                    n = MH * l + h
                    p, o = mp_[h % 2], 2 * (h % 2)
                    dve.wait_ge(ms_exp, n + 1)
                    link(V.reciprocal(rs[:, o:o + 2], rs[:, o:o + 2]))
                    V.tensor_scalar(p[:, 0:P], p[:, 0:P], rs[:, o:o + 1], None, ALU.mult)
                    V.tensor_scalar(p[:, P:3 * P], p[:, P:3 * P], rs[:, o + 1:o + 2], None, ALU.mult).then_inc(ms_norm, 1)

                if l == 0:
                    dve.wait_ge(consts, 3)
                moba_max(0)
                for h in range(MH):
                    if h + 1 < MH:
                        moba_max(h + 1)
                    moba_norm(h)
                for i in range(4):
                    n_, t = i // 2, i % 2
                    dve.wait_ge(up_ps, 8 * l + i + 1)
                    V.scalar_tensor_tensor(merged[:, t, n_ * 512:(n_ + 1) * 512], gates[:, t, n_ * 512:(n_ + 1) * 512],
                                           1.0, B[i % 2][:, :], ALU.add, ALU.mult).then_inc(up_used, 1)
                for i in range(4):
                    n_, t = i // 2, i % 2
                    dve.wait_ge(glu_th, 4 * l + i + 1)
                    V.scalar_tensor_tensor(glu_y[t], glu_t[t], 1.0, B[2 * t][:, :], ALU.add, ALU.mult).then_inc(glu_used, 1)
                    dve.wait_ge(glu_used, 4 * l + i + 1)
                    g = gates[:, t, D + n_ * 512:D + (n_ + 1) * 512]
                    m = merged[:, t, n_ * 512:(n_ + 1) * 512]
                    link(V.scalar_tensor_tensor(gl_tmp[t], g, 1.0, glu_y[t], ALU.add, ALU.mult))
                    link(V.scalar_tensor_tensor(m, gl_tmp[t], 0.5, m, ALU.mult, ALU.add))
                ab4 = ab.rearrange("p (t c h) -> p t c h", t=NT, c=2)
                z4 = gate_z.rearrange("p (t h) -> p t h", t=NT)
                dve.wait_ge(ab_sb, l + 1)
                for t in range(NT):
                    last = V.tensor_tensor(z4[:, t, :], ab4[:, t, 0, :], small_bc[:, l, 1, :], ALU.add)
                link(last)
                V.scalar_tensor_tensor(gate_e, gate_z, -1.0, gate_z, ALU.mult, ALU.max).then_inc(g_z, 1)
                for w in range(1, 4):
                    for j in range(12):
                        if w == 1:
                            dve.wait_ge(cv_tap, 12 * l + j + 1)
                        k = 48 * l + 12 * w + j
                        last = V.scalar_tensor_tensor(cv[:, j, :], raw[:, j, w:w + SEQ], p_conv[:, k:k + 1],
                                                      cv[:, j, :], ALU.mult, ALU.add)
                        if w == 3 and j % 4 == 3:
                            last.then_inc(cv_pre, 1)
                    if w < 3:
                        link(last)
                dve.wait_ge(g_ln, l + 1)
                link(V.scalar_tensor_tensor(gate_z, gate_z, 0.0, gate_e, ALU.max, ALU.add))
                for t in range(NT):
                    last = V.scalar_tensor_tensor(gstep.rearrange("p (t h) -> p t h", t=NT)[:, t, :], z4[:, t, :],
                                                  -1.0, ealog, ALU.mult, ALU.mult)
                last.then_inc(g_step, 1)
                dve.wait_ge(g_exp, l + 1)
                link(V.tensor_scalar(beta, beta, 0.5, 0.5, ALU.mult, ALU.add))
                for i in range(3):
                    dve.wait_ge(cv_th, 3 * l + i + 1)
                    tmp = (A_low, M_lvl, W_lvl)[i].rearrange("p t h n -> p (t h n)")
                    c4 = cv[:, 4 * i:4 * i + 4, :].rearrange("p c n -> p (c n)")
                    V.scalar_tensor_tensor(c4, tmp, 1.0, c4, ALU.add, ALU.mult).then_inc(cv_ready, 1)
                for i in range(4):
                    dve.wait_ge(cv_rs, 4 * l + i + 1)
                    r_ = rq[i].rearrange("p t h n -> p (t h n)")[:, 0:512]
                    c2 = cv[:, 2 * i:2 * i + 2, :].rearrange("p c n -> p (c n)")
                    V.scalar_tensor_tensor(c2, r_, GD ** -0.5 if i < 2 else 1.0, c2, ALU.mult, ALU.mult).then_inc(kq_ready, 1)
                dve.wait_ge(gc_ps, l + 1)
                V.tensor_copy(gcum, B[1][:, 0:NT * GH]).then_inc(gc_sb, 1)
                dve.wait_ge(gc_sb, l + 1)
                gc3 = gcum.rearrange("p (t h) -> p t h", t=NT)
                be3 = beta.rearrange("p (t h) -> p t h", t=NT)
                bx3 = bexp.rearrange("p (t h) -> p t h", t=NT)
                kd3 = kds.rearrange("p (t h) -> p t h", t=NT)
                for t in range(NT):
                    V.tensor_tensor(gdiag[:, t], ident[:, :].unsqueeze(1).to_broadcast([P, GH, P]),
                                    gc3[:, t, :].unsqueeze(2).to_broadcast([P, GH, P]), ALU.mult).then_inc(g_diag, 1)
                for t in range(NT):
                    dve.wait_ge(row_ps, NT * l + t + 1)
                    link(V.tensor_tensor(DTm[:, t], B[2 + t][:, :].rearrange("p (h n) -> p h n", h=GH),
                                         gc3[:, t, :].unsqueeze(2).to_broadcast([P, GH, P]), ALU.subtract))
                    link(V.tensor_scalar(Dcl[:, t], DTm[:, t], 0.0, None, ALU.max))
                    V.tensor_scalar(DTm[:, t], DTm[:, t], 0.0, None, ALU.min).then_inc(dec_in, 1)
                dve.wait_ge(g_bexp, l + 1)
                link(V.tensor_tensor(bexp, bexp, beta, ALU.mult))
                for t in range(NT):
                    dve.wait_ge(dec_ready, 3 * NT * l + 3 * t + 3)
                    link(V.tensor_tensor(decT[:, t], decT[:, t], cum_mask[:, :].unsqueeze(1).to_broadcast([P, GH, P]),
                                         ALU.mult))
                    link(V.tensor_tensor(kd3[:, t, :], decT[:, t, :, GL - 1], decT[:, t, :, 2 * GL - 1], ALU.add))

                def per_token(s3, t):
                    return s3[:, t, :].unsqueeze(2).to_broadcast([P, GH, GD])

                for t in range(NT):
                    dve.wait_ge(kv_evac, NT * l + t + 1)
                    V.tensor_tensor(kbeg[:, t], k_tok[:, t], per_token(bx3, t), ALU.mult)
                    V.tensor_tensor(kdec[:, t], k_tok[:, t], per_token(kd3, t), ALU.mult)
                    dve.wait_ge(kv_ps, 4 * l + 2 + t + 1)
                    V.scalar_tensor_tensor(vbeta[:, t], B[6 + t][:, :].rearrange("p (h n) -> p h n", h=GH), 0.5,
                                           per_token(be3, t), ALU.mult, ALU.mult).then_inc(uw_in, 1)
                for t in range(NT):
                    dve.wait_ge(kk_ps, 2 * NT * l + t + 1)
                    link(V.tensor_tensor(A_low[:, t], B[4 + t][:, :].rearrange("p (h n) -> p h n", h=GH), dec[:, t], ALU.mult))
                    V.tensor_tensor(A_low[:, t], A_low[:, t], per_token(be3, t), ALU.mult).then_inc(a_ready, 1)
                for t in range(NT):
                    dve.wait_ge(kk_ps, 2 * NT * l + NT + t + 1)
                    V.tensor_tensor(qkT[:, t], B[6 + t][:, :].rearrange("p (h n) -> p h n", h=GH), decT[:, t], ALU.mult)
                    qc = cv[:, 0:4, t * P:(t + 1) * P]
                    V.tensor_tensor(qc, qc, e_row[:, t], ALU.mult).then_inc(qd_ready, 1)
                for k in range(6):
                    for t in range(NT):
                        n = (6 * l + k) * NT + t
                        if k == 0:
                            dve.wait_ge(xz_init, 2 * NT * l + 2 * t + 2)
                        dve.wait_ge(xz_ps, n + 1)
                        V.tensor_tensor(Xi[:, t], Xi[:, t], B[2 + t][:, :].rearrange("p (h n) -> p h n", h=GH), ALU.subtract)
                        V.tensor_tensor(Zi[:, t], Zi[:, t], B[4 + t][:, :].rearrange("p (h n) -> p h n", h=GH),
                                        ALU.subtract).then_inc(xz_ready, 1)
                    for t in range(NT):
                        dve.wait_ge(xz_ready, (6 * l + k) * NT + t + 1)
                V.memset(state[:, 0], 0.0).then_inc(s_init, 1)
                for t in range(NT):
                    dve.wait_ge(uw_ps, NT * l + t + 1)
                    V.tensor_copy(u_tok[:, t], B[2 + t][:, :].rearrange("p (h n) -> p h n", h=GH)).then_inc(u_done, 1)
                dve.wait_ge(u_done, NT * (l + 1))
                for c in range(NCHUNK):
                    n, t, off = NCHUNK * l + c, c // 2, (c % 2) * GL
                    rows_ = slice(off, off + GL)
                    dve.wait_ge(vn_ps, n + 1)
                    V.tensor_tensor(vn[rows_], u_tok[rows_, t], B[4][rows_, :].rearrange("p (h n) -> p h n", h=GH),
                                    ALU.subtract).then_inc(vn_ready, 1)
                    if c < NCHUNK - 1:
                        new, old = state[:, (c + 1) % 2], state[:, c % 2]
                        eg = e_row[:, t, :, off + GL - 1].unsqueeze(2).to_broadcast([P, GH, GD])
                        if c == 0:
                            dve.wait_ge(s_init, l + 1)
                        dve.wait_ge(s_ready, n - l) if c > 0 else None
                        link(V.tensor_tensor(new, old, eg, ALU.mult))
                        dve.wait_ge(su_ps, (NCHUNK - 1) * l + c + 1)
                        V.tensor_tensor(new, new, B[7][:, :].rearrange("p (h n) -> p h n", h=GH), ALU.add).then_inc(s_ready, 1)
                dve.wait_ge(o_evac, (NCHUNK + 1) * (l + 1))
                o_all = o_tok.rearrange("p t h n -> p (t h) n")
                sq = DTm.rearrange("p t h n -> p (t h) n")
                link(V.tensor_tensor(sq, o_all, o_all, ALU.mult))
                V.tensor_reduce(gate_z, sq, AX.X, ALU.add).then_inc(og_ss, 1)
                dve.wait_ge(og_rs, l + 1)
                link(V.tensor_tensor(o_all, o_all, gate_z.unsqueeze(2).to_broadcast([P, NT * GH, GD]), ALU.mult))
                link(V.tensor_tensor(o_all, o_all, gnorm_bc[:, l, :].unsqueeze(1).to_broadcast([P, NT * GH, GD]), ALU.mult))
                zf = z_tok[:, :, :].rearrange("p t n -> p (t n)")
                gz = gdiag.rearrange("p t h n -> p (t h n)")
                of = o_tok.rearrange("p t h n -> p (t h n)")
                link(V.scalar_tensor_tensor(gz, gz, 1.0, zf, ALU.add, ALU.mult))
                V.scalar_tensor_tensor(of, gz, 0.5, of, ALU.mult, ALU.mult).then_inc(og_ready, 1)
                for i in range(4):
                    n_, t = i // 2, i % 2
                    dve.wait_ge(up_ps, 8 * l + 4 + i + 1)
                    tmp = (DTm if t == 0 else Dcl).rearrange("p t h n -> p (t h n)")[:, 0:512]
                    V.scalar_tensor_tensor(tmp, gates[:, t, 2 * D + n_ * 512:2 * D + (n_ + 1) * 512], 1.0, B[i % 2][:, :],
                                           ALU.add, ALU.mult).then_inc(up_used, 1)
                    dve.wait_ge(up_used, 8 * l + 4 + i + 1)
                    m = merged[:, t, n_ * 512:(n_ + 1) * 512]
                    last = V.tensor_tensor(m, m, tmp, ALU.add)
                last.then_inc(mg_ready, 1)
                for i in range(4):
                    n_, t = i // 2, i % 2
                    dve.wait_ge(wo_ps, 4 * l + i + 1)
                    xs = x[:, t, n_ * 512:(n_ + 1) * 512]
                    V.scalar_tensor_tensor(xs, B[i % 2][:, :], 0.5, xs, ALU.mult, ALU.add).then_inc(wo_used, 1)
                normalise(x[:, :, :], h_tok, 2 + 3 * l)
                for h in range(XH):
                    n_, o = XH * l + h, 2 * (h % 2)
                    dve.wait_ge(xs_ps, n_ + 1)
                    if n_ >= 2:
                        dve.wait_ge(xs_exp, n_ - 1)
                    link(V.tensor_reduce(mx[:, o:o + 2], B[2 + h % 2][:, :].rearrange("p (t n) -> p t n", t=NT), AX.X, ALU.max))
                    V.tensor_scalar(nm[:, o:o + 2], mx[:, o:o + 2], -XD ** -0.5, None, ALU.mult).then_inc(xs_neg, 1)
                    dve.wait_ge(xs_exp, n_ + 1)
                    link(V.reciprocal(rs[:, o:o + 2], rs[:, o:o + 2]))
                    for t in range(NT):
                        last = V.tensor_scalar(xp[h % 2][:, t, :], xp[h % 2][:, t, :], rs[:, o + t:o + t + 1], None, ALU.mult)
                    last.then_inc(xs_norm, 1)
                for i in range(4):
                    n_, t = i // 2, i % 2
                    dve.wait_ge(xo_ps, 4 * l + i + 1)
                    xs = x[:, t, n_ * 512:(n_ + 1) * 512]
                    V.tensor_tensor(xs, xs, B[i % 2][:, :], ALU.add).then_inc(xo_used, 1)
                normalise(x[:, :, :], h_tok, 3 + 3 * l)
                if l % 2 == 0:
                    V.memset(comb, 0.5).then_inc(comb_ready, 1)
                else:
                    dve.wait_ge(rl_ps, l // 2 + 1)
                    link(V.tensor_copy(r_log, B[0][:, 0:NT * NE].rearrange("p (t e) -> p t e", t=NT)))
                    for t in range(NT):
                        link(V.max(r_max[:, t, :], r_log[:, t, :]))
                        link(V.max_index(r_idx[:, t, :], r_max[:, t, :], r_log[:, t, :]))
                    link(V.tensor_copy(r_idf, r_idx[:, :, :]))
                    V.tensor_tensor(r_w[:, :, 0:1], r_max[:, :, 1:2], r_max[:, :, 0:1], ALU.subtract).then_inc(rl_d, 1)
                    dve.wait_ge(rl_e, l // 2 + 1)
                    link(V.tensor_scalar(r_w[:, :, 2:3], r_w[:, :, 1:2], 1.0, None, ALU.add))
                    link(V.reciprocal(r_w[:, :, 2:3], r_w[:, :, 2:3]))
                    link(V.tensor_tensor(r_w[:, :, 3:4], r_w[:, :, 1:2], r_w[:, :, 2:3], ALU.mult))
                    for t in range(NT):
                        for i in range(2):
                            last = V.tensor_scalar(r_eq[:, i, t, :], idx8[:, :], r_idf[:, t, i:i + 1],
                                                   r_w[:, t, 2 + i:3 + i], ALU.is_equal, ALU.mult)
                    link(last)
                    link(V.tensor_tensor(comb, r_eq[:, 0], r_eq[:, 1], ALU.add))
                    V.tensor_scalar(comb, comb, 0.5, None, ALU.mult).then_inc(comb_ready, 1)
                dve.wait_ge(comb_ready, l + 1)
                base = NCH * experts_before(l) * NT
                eb = experts_before(l)

                def expert(e):
                    def chunk(c, in_slot, s, head):
                        for t in range(NT):
                            v = e * (NCH * NT) + c * NT + (base + t + 1)
                            dve.wait_ge(gu_th, v)
                            V.scalar_tensor_tensor(f_a[t], f_th[t], 1.0, B[t][:, 0:FC], ALU.add, ALU.mult).then_inc(gu_a, 1)
                            dve.wait_ge(gu_a, v)
                            if not (head and l == 0):
                                dve.wait_ge(act_tr, e * (NCH * NT) + c * NT + (base + t + 1 - NT))
                            V.scalar_tensor_tensor(f_act[t], f_a[t], comb[:, t, bass.ds(e, 1)], B[t][:, FC:2 * FC],
                                                   ALU.mult, ALU.mult).then_inc(act_ready, 1)
                    chunks_of_expert(dve, chunk)
                    dve.wait_ge(chunk_used, e * NCH + (NCH * eb + NCH))
                    for i in range(4):
                        n_, t = i // 2, i % 2
                        xs = x[:, t, n_ * 512:(n_ + 1) * 512]
                        last = V.tensor_tensor(xs, xs, B[4 + i][:, :], ALU.add)
                    last.then_inc(y_added, 1)
                    dve.wait_ge(y_added, e + (eb + 1))
                over_experts(dve, l, expert)
            n = NNORM
            dve.wait_ge(norm_ss, n + 1)
            dve.wait_ge(fin_in, 16)
            for t in range(NT):
                last = V.scalar_tensor_tensor(x[:, t, :], x[:, t, :], rstd[:, t:t + 1], gain_out, ALU.mult, ALU.mult)
            last.then_inc(fin_ready, 1)

        @block.tensor
        def _(pe):
            mm = nc.tensor.matmul
            tr = nc.tensor.transpose
            pe.wait_ge(consts, 1)
            pe.wait_ge(consts, 2)
            pe.wait_ge(par_in, 16 * 9)
            rows = phase[:, 0:3 * P].rearrange("p (a n) -> p a n", a=3)
            tr(B[0][:, 0:P], rows[:, 0, :], ident[:, :])
            tr(B[0][:, P:2 * P], rows[:, 1, :], ident[:, :])
            tr(B[0][:, 2 * P:2 * P + 8], rows[0:8, 2, :], ident[0:8, 0:8]).then_inc(par_ps, 1)

            def transpose_rows(src, n):
                pe.wait_ge(norm_h, NT * (n + 1))
                for b in range(4):
                    for i in range(2):
                        for t in range(NT):
                            k = 2 * b + i
                            last = tr(B[4 + b][:, i * SEQ + t * P:i * SEQ + (t + 1) * P],
                                      src[:, t, k * P:(k + 1) * P], ident[:, :])
                    last.then_inc(norm_ps, 1)

            def arrived(l, j):
                pe.wait_ge(slot_full[j % NSLOT], slot_after_unit(l, j))

            def features_out(l, j, src, banks, ready, free):
                arrived(l, j)
                w = slot(j)[:, 0:4096].rearrange("p (k w) -> p k w", w=512)
                for m in range(4):
                    if m % 2 == 0 and free is not None:
                        free(m // 2)
                    for k in range(KD):
                        last = mm(B[banks[m // 2]][:, (m % 2) * SEQ:(m % 2 + 1) * SEQ],
                                  w[:, k, m * P:(m + 1) * P], src[:, k, :], start=k == 0, stop=k == KD - 1)
                    if m % 2 == 1:
                        last.then_inc(ready, 1)

            def tokens_out(bank, src, t, w, kt, n0):
                for k in range(kt):
                    last = mm(B[bank][:, :], src[:, k, t * P:(t + 1) * P], w[:, k, n0:n0 + 512],
                              start=k == 0, stop=k == kt - 1)
                return last

            transpose_rows(h_tok, 0)

            for l in range(DEPTH):
                if l == 0:
                    pe.wait_ge(hT_ready, 1)
                transpose_rows(h_tok, 1 + 3 * l)
                pe.wait_ge(hT_ready, 2 + 3 * l)
                if l == 0:
                    pe.wait_ge(par_ready, 1)

                features_out(l, U_U, hT[:, :, :], (0, 1), ws_ready, None)

                def pad_tr(q, half):
                    n = 2 * (NQ * l + q) + half
                    pe.wait_ge(pad_ready, 2 * n + 2)
                    if n >= 1:
                        pe.wait_ge(bct_ready, n)
                    for c in range(2):
                        for j in range(NQ):
                            last = tr(B[6 + c][:, j * P:(j + 1) * P], pads[:, c, j * P:(j + 1) * P], ident[:, :])
                    last.then_inc(pad_ps, 1)

                pad_tr(0, 0)
                pad_tr(0, 1)
                pe.wait_ge(ab_in, 16 * (l + 1))
                for t in range(NT):
                    for k in range(KD):
                        last = mm(B[4][:, t * 8:(t + 1) * 8], hT[:, k, t * P:(t + 1) * P], ab_w[:, k, :],
                                  start=k == 0, stop=k == KD - 1)
                last.then_inc(ab_ps, 1)

                def fill(f):
                    j, t = U_Q + f // 2, f % 2
                    if t == 0:
                        arrived(l, j)
                    if f < 2:
                        pe.wait_ge(ws_evac, 8 * l + 1 + f)
                    elif f < 6:
                        pe.wait_ge(rope_done, 4 * l + f - 1)
                    else:
                        pe.wait_ge(fill_evac, 16 * l + f - 5)
                    w = slot(j)[:, 0:4096].rearrange("p (k w) -> p k w", w=512)
                    tokens_out(t, hT[:, :, :], t, w, KD, 0).then_inc(fill_ready, 1)

                def s5_in(i):
                    q, n = i // NQ, NS5 * l + i
                    if i % NQ == 0:
                        pe.wait_ge(bct_ready, 2 * (NQ * l + q) + 2)
                    if i == 0:
                        pe.wait_ge(ws_evac, 8 * l + 2)
                    if n >= 2:
                        pe.wait_ge(bu_read, n - 1)
                    for c in range(2):
                        last = mm(B[2 + n % 2][:, c * SEQ:(c + 1) * SEQ], bct[q % 2][c][:, i % NQ, :], uT[:, q, :],
                                  start=True, stop=True)
                    last.then_inc(bu_ready, 1)

                def s5_out(i):
                    q, n = i // NQ, NS5 * l + i
                    if i == 0:
                        pe.wait_ge(ab_sb, l + 1)
                    if i % NQ == 0 and q >= 2:
                        pe.wait_ge(gel_in, NQ * l + q - 1)
                    pe.wait_ge(h_rot, n + 1)
                    hr = wk5[3 + n % 2]
                    for c in range(2):
                        last = mm(B[4 + q % 2][:, 0:SEQ], bct[q % 2][2 + c][:, i % NQ, :], hr[:, c, :],
                                  start=(i % NQ == 0 and c == 0), stop=(i % NQ == NQ - 1 and c == 1))
                    last.then_inc(y_read, 1)

                for f in range(4):
                    fill(f)
                for i in range(NS5):
                    s5_in(i)
                    fill(4 + i)
                    if i > 0:
                        s5_out(i - 1)
                    if i % NQ == 1 and i // NQ + 1 < NQ:
                        pad_tr(i // NQ + 1, 0)
                        pad_tr(i // NQ + 1, 1)
                s5_out(NS5 - 1)

                pe.wait_ge(fill_evac, 16 * (l + 1))
                features_out(l, U_CONV, hT[:, :, :], (0, 1), ws_ready, None)
                pe.wait_ge(bu_read, NS5 * (l + 1))
                features_out(l, U_CONV + 1, hT[:, :, :], (2, 3), ws_ready, None)
                features_out(l, U_CONV + 2, hT[:, :, :], (0, 1), ws_ready,
                             lambda b: pe.wait_ge(ws_evac, 8 * l + 3 + b))

                pe.wait_ge(gel_in, NQ * (l + 1))
                pe.wait_ge(bct_ready, 2 * NQ * (l + 1))
                for i in range(4):
                    for k in range(KW):
                        last = tr(B[4 + i][:, k * P:(k + 1) * P], qk[:, i // 2, i % 2, k * P:(k + 1) * P], ident[:, :])
                    last.then_inc(mtr_ps, 1)
                pe.wait_ge(mtr_ready, 4 * (l + 1))

                def m_scores(h):
                    n = MH * l + h
                    if h >= 2:
                        pe.wait_ge(ms_neg, n - 1)
                    else:
                        pe.wait_ge(ws_evac, 8 * l + 5 + h)
                    ps = slice((h % 2) * MD, (h % 2 + 1) * MD)
                    mm(B[2 + h % 2][:, 0:P], mqT[ps, h // 2, 0:P], mkT[ps, h // 2, 0:P], start=True, stop=True)
                    mm(B[2 + h % 2][:, P:3 * P], mqT[ps, h // 2, P:2 * P], mkT[ps, h // 2, :], start=True,
                       stop=True).then_inc(ms_ready, 1)

                def m_tr(h):
                    n = MH * l + h
                    pe.wait_ge(ms_norm, n + 1)
                    if h >= 2:
                        pe.wait_ge(ms_pT, n - 1)
                    for b in range(3):
                        last = tr(B[4 + h % 2][:, b * P:(b + 1) * P], mp_[h % 2][:, b * P:(b + 1) * P], ident[:, :])
                    last.then_inc(ms_tr, 1)

                def m_out(h):
                    n = MH * l + h
                    pe.wait_ge(ms_pT, n + 1)
                    if h >= 4 and h % 2 == 0:
                        pe.wait_ge(ms_oT, 4 * l + h // 2 - 1)
                    ps = slice((h % 2) * MD, (h % 2 + 1) * MD)
                    o = B[6 + (h // 2) % 2]
                    pT, vh = mpT[h % 2], v_tok[:, :, h * MD:(h + 1) * MD]
                    mm(o[ps, 0:P], vh[:, 0, :], pT[:, 0:P], start=True, stop=True)
                    mm(o[ps, P:2 * P], vh[:, 0, :], pT[:, P:2 * P], start=True, stop=False)
                    mm(o[ps, P:2 * P], vh[:, 1, :], pT[:, 2 * P:3 * P], start=False, stop=True).then_inc(ms_o, 1)

                for s in range(MH + 2):
                    if s < MH:
                        m_scores(s)
                    if 1 <= s <= MH:
                        m_tr(s - 1)
                    if s >= 2:
                        m_out(s - 2)

                def up(j, src, first, n):
                    arrived(l, j)
                    w = slot(j)[:, 0:4096].rearrange("p (k w) -> p k w", w=D)
                    for i in range(4):
                        if i >= 2:
                            pe.wait_ge(up_used, n + i - 1)
                        last = tokens_out(i % 2, src, i % 2, w, KW, (i // 2) * 512)
                        last.then_inc(up_ps, 1)

                pe.wait_ge(ms_oT, 4 * (l + 1))
                pe.wait_ge(ws_evac, 8 * (l + 1))
                up(U_UPM, m_oT, True, 8 * l)
                pe.wait_ge(y_ready, l + 1)
                pe.wait_ge(up_used, 8 * l + 4)
                for n_ in range(2):
                    j = U_GLU + n_
                    arrived(l, j)
                    w = slot(j)[:, 0:4096].rearrange("p (k w) -> p k w", w=D)
                    for t in range(NT):
                        if n_ == 1:
                            pe.wait_ge(glu_used, 4 * l + t + 1)
                        tokens_out(2 * t, yT[:, :, :], t, w, KW, 0)
                        tokens_out(2 * t + 1, yT[:, :, :], t, w, KW, 512).then_inc(glu_ps, 1)
                pe.wait_ge(glu_used, 4 * l + 4)
                pe.wait_ge(g_step, l + 1)
                mm(B[1][:, 0:NT * GH], cum_mask[:, :], gstep, start=True, stop=True).then_inc(gc_ps, 1)
                for i in range(4):
                    pe.wait_ge(cv_sq, 4 * l + i + 1)
                    tmp = (DTm, Dcl)[i // 2].rearrange("p t h n -> p (t h n)")[:, (i % 2) * 512:(i % 2 + 1) * 512]
                    mm(B[4 + i][:, :], ones[:, :], tmp, start=True, stop=True).then_inc(cv_ss, 1)
                for t in range(NT):
                    pe.wait_ge(g_diag, NT * l + t + 1)
                    mm(B[2 + t][:, :], ones[:, :], gdiag[:, t].rearrange("p h n -> p (h n)"), start=True,
                       stop=True).then_inc(row_ps, 1)
                pe.wait_ge(kq_ready, 4 * (l + 1))
                for t in range(NT):
                    for h in range(GH):
                        last = tr(B[4 + t][:, h * P:(h + 1) * P], cv[:, 4 + h, t * P:(t + 1) * P], ident[:, :])
                    last.then_inc(kv_ps, 1)
                pe.wait_ge(cv_ready, 3 * (l + 1))
                for t in range(NT):
                    for h in range(GH):
                        last = tr(B[6 + t][:, h * P:(h + 1) * P], cv[:, 8 + h, t * P:(t + 1) * P], ident[:, :])
                    last.then_inc(kv_ps, 1)
                for t in range(NT):
                    pe.wait_ge(kv_evac, NT * l + t + 1)
                    for h in range(GH):
                        kh = cv[:, 4 + h, t * P:(t + 1) * P]
                        last = mm(B[4 + t][:, h * P:(h + 1) * P], kh, kh, start=True, stop=True)
                    last.then_inc(kk_ps, 1)
                for t in range(NT):
                    pe.wait_ge(uw_in, NT * l + t + 1)
                    for h in range(GH):
                        last = mm(B[6 + t][:, h * P:(h + 1) * P], cv[:, 4 + h, t * P:(t + 1) * P],
                                  cv[:, h, t * P:(t + 1) * P], start=True, stop=True)
                    last.then_inc(kk_ps, 1)
                for k in range(6):
                    for t in range(NT):
                        n = (6 * l + k) * NT + t
                        pe.wait_ge(m_ready, n + 1)
                        if k == 0:
                            pe.wait_ge(xz_init, 2 * NT * l + 2 * t + 2)
                            pe.wait_ge(dec_in, NT * (l + 1))
                            pe.wait_ge(dec_ready, 3 * NT * (l + 1))
                        else:
                            pe.wait_ge(xz_ready, n - NT + 1)
                        for h in range(GH):
                            last = mm(B[t][:, h * P:(h + 1) * P], M_lvl[:, t, h, :], Zi[:, t, h, :], start=True, stop=True)
                        last.then_inc(w_ps, 1)
                    for t in range(NT):
                        n = (6 * l + k) * NT + t
                        pe.wait_ge(w_evac, n + 1)
                        for h in range(GH):
                            mm(B[2 + t][:, h * P:(h + 1) * P], W_lvl[:, t, h, :], Xi[:, t, h, :], start=True, stop=True)
                        for h in range(GH):
                            last = mm(B[4 + t][:, h * P:(h + 1) * P], Xi[:, t, h, :], W_lvl[:, t, h, :], start=True, stop=True)
                        last.then_inc(xz_ps, 1)
                for t in range(NT):
                    pe.wait_ge(xz_ready, (6 * l + 5) * NT + t + 1)
                    pe.wait_ge(qd_ready, NT * l + t + 1)
                    for h in range(GH):
                        mm(B[t][:, h * P:(h + 1) * P], kbeg[:, t, h, :], Zi[:, t, h, :], start=True, stop=True)
                    for h in range(GH):
                        last = mm(B[2 + t][:, h * P:(h + 1) * P], Zi[:, t, h, :], vbeta[:, t, h, :], start=True, stop=True)
                    last.then_inc(uw_ps, 1)
                pe.wait_ge(w_done, NT * (l + 1))
                pe.wait_ge(s_init, l + 1)
                pe.wait_ge(xz_ready, 6 * NT * (l + 1))
                for c in range(NCHUNK):
                    n, t, off = NCHUNK * l + c, c // 2, (c % 2) * GL
                    rows_ = slice(off, off + GL)
                    if c > 0:
                        pe.wait_ge(s_ready, (NCHUNK - 1) * l + c)
                    S = state[:, c % 2]
                    for h in range(GH):
                        last = mm(B[4][rows_, h * P:(h + 1) * P], wT[:, t, h, rows_], S[:, h, :], start=True, stop=True)
                    last.then_inc(vn_ps, 1)
                    pe.wait_ge(vn_ready, n + 1)
                    if c < NCHUNK - 1:
                        for h in range(GH):
                            last = mm(B[7][:, h * P:(h + 1) * P], kdec[rows_, t, h, :], vn[rows_, h, :], start=True, stop=True)
                        last.then_inc(su_ps, 1)
                    if c >= 2:
                        pe.wait_ge(o_evac, (NCHUNK + 1) * l + c - 1)
                    for h in range(GH):
                        o = B[5 + c % 2][rows_, h * P:(h + 1) * P]
                        mm(o, cv[:, h, t * P + off:t * P + off + GL], S[:, h, :], start=True, stop=False)
                        last = mm(o, qkT[rows_, t, h, rows_], vn[rows_, h, :], start=False, stop=True)
                    last.then_inc(o_ps, 1)
                pe.wait_ge(og_ready, l + 1)
                for t in range(NT):
                    for h in range(GH):
                        last = tr(B[4 + t][:, h * P:(h + 1) * P], o_tok[:, t, h, :], ident[:, :])
                    last.then_inc(og_ps, 1)
                pe.wait_ge(og_T, NT * (l + 1))
                up(U_UPG, g_oT, False, 8 * l + 4)
                pe.wait_ge(up_used, 8 * (l + 1))
                pe.wait_ge(mg_ready, l + 1)
                for b in range(4):
                    for i in range(2):
                        for t in range(NT):
                            k = 2 * b + i
                            last = tr(B[4 + b][:, i * SEQ + t * P:i * SEQ + (t + 1) * P], merged[:, t, k * P:(k + 1) * P], ident[:, :])
                    last.then_inc(mg_ps, 1)
                pe.wait_ge(mg_T, 4 * (l + 1))
                for n_ in range(2):
                    arrived(l, U_OUT + n_)
                    w = slot(U_OUT + n_)[:, 0:4096].rearrange("p (k w) -> p k w", w=512)
                    for t in range(NT):
                        if n_ == 1:
                            pe.wait_ge(wo_used, 4 * l + t + 1)
                        tokens_out(t, hT[:, :, :], t, w, KD, 0).then_inc(wo_ps, 1)
                pe.wait_ge(memn_ready, l + 1)
                features_out(l, U_WK, memnT, (2, 3), xk_ps, None)
                pe.wait_ge(wo_used, 4 * (l + 1))
                arrived(l, U_WV)
                w = slot(U_WV)[:, 0:4096].rearrange("p (k w) -> p k w", w=512)
                for t in range(NT):
                    tokens_out(t, memnT, t, w, KD, 0).then_inc(xk_ps, 1)
                transpose_rows(h_tok, 2 + 3 * l)
                pe.wait_ge(hT_ready, 3 + 3 * l)
                pe.wait_ge(xk_sb, 6 * l + 4)
                features_out(l, U_WQ, hT[:, :, :], (0, 1), xk_ps, None)
                pe.wait_ge(xk_sb, 6 * l + 6)

                def x_scores(h):
                    n = XH * l + h
                    if h >= 2:
                        pe.wait_ge(xs_exp, n - 1)
                    for t in range(NT):
                        last = mm(B[2 + h % 2][:, t * SEQ:(t + 1) * SEQ], xqT[:, h, t * P:(t + 1) * P], xkT[:, h, :],
                                  start=True, stop=True)
                    last.then_inc(xs_ps, 1)

                def x_tr(h):
                    n = XH * l + h
                    pe.wait_ge(xs_norm, n + 1)
                    if h >= 2:
                        pe.wait_ge(xs_pT, n - 1)
                    for m in range(NT):
                        for t in range(NT):
                            last = tr(B[4 + h % 2][:, m * SEQ + t * P:m * SEQ + (t + 1) * P],
                                      xp[h % 2][:, t, m * P:(m + 1) * P], ident[:, :])
                    last.then_inc(xs_tr, 1)

                def x_out(h):
                    n = XH * l + h
                    pe.wait_ge(xs_pT, n + 1)
                    if h >= 2:
                        pe.wait_ge(xs_oT, n - 1)
                    for m in range(NT):
                        last = mm(B[6 + h % 2][:, 0:SEQ], x_v[:, m, h * XD:(h + 1) * XD], xpT[h % 2][:, m, :],
                                  start=m == 0, stop=m == NT - 1)
                    last.then_inc(xs_o, 1)

                for s in range(XH + 2):
                    if s < XH:
                        x_scores(s)
                    if 1 <= s <= XH:
                        x_tr(s - 1)
                    if s >= 2:
                        x_out(s - 2)
                pe.wait_ge(xs_oT, XH * (l + 1))
                arrived(l, U_WO)
                w = slot(U_WO)[:, 0:4096].rearrange("p (k w) -> p k w", w=D)
                for i in range(4):
                    if i >= 2:
                        pe.wait_ge(xo_used, 4 * l + i - 1)
                    tokens_out(i % 2, x_oT, i % 2, w, KW, (i // 2) * 512).then_inc(xo_ps, 1)
                transpose_rows(h_tok, 3 + 3 * l)
                pe.wait_ge(hT_ready, 4 + 3 * l)
                if l % 2 == 1:
                    pe.wait_ge(rout_in, 16)
                    for t in range(NT):
                        for k in range(KD):
                            last = mm(B[0][:, t * NE:(t + 1) * NE], hT[:, k, t * P:(t + 1) * P], router_w[:, k, :],
                                      start=k == 0, stop=k == KD - 1)
                    last.then_inc(rl_ps, 1)
                pe.wait_ge(comb_ready, l + 1)
                base = NCH * experts_before(l) * NT
                eb = experts_before(l)

                def expert(e):
                    def at(c, t):
                        return e * (NCH * NT) + c * NT + (base + t + 1)

                    def gate_up(c, t, s, head):
                        w = ring[:, s * SLOT:s * SLOT + 4096].rearrange("p (k w) -> p k w", w=512)
                        if not (head and l == 0):
                            pe.wait_ge(act_ready, at(c, t) - NT)
                        tokens_out(t, hT[:, :, :], t, w, KD, 0).then_inc(gu_ps, 1)

                    def flip(c, t, head):
                        pe.wait_ge(act_ready, at(c, t))
                        if not (head and l == 0):
                            pe.wait_ge(actT_ready, at(c, t) - NT)
                        for k in range(FC // P):
                            last = tr(B[2 + t][:, k * P:(k + 1) * P], f_act[t][:, k * P:(k + 1) * P], ident[:, :])
                        last.then_inc(act_tr, 1)

                    def down(c, s, first, last_one):
                        w = ring[:, s * SLOT + 4096:(s + 1) * SLOT].rearrange("p (k n) -> p k n", n=D)
                        pe.wait_ge(actT_ready, at(c, NT - 1))
                        if first and not (l == 0):
                            pe.wait_ge(y_added, e + eb)
                        for t in range(NT):
                            for n_ in range(2):
                                for k in range(FC // P):
                                    last = mm(B[4 + 2 * n_ + t][:, :], f_actT[:, k, t * P:(t + 1) * P],
                                              w[:, k, n_ * 512:(n_ + 1) * 512], start=first and k == 0,
                                              stop=last_one and k == FC // P - 1)
                        last.then_inc(chunk_used, 1)

                    def chunk(c, in_slot, s, head):
                        pe.wait_ge(slot_full[s], slot_after_chunk(l, e, in_slot, s))
                        gate_up(c, 0, s, head)
                        if not head:
                            flip(c - 1, 1, False)
                        gate_up(c, 1, s, head)
                        if not head:
                            down(c - 1, (s - 1) % NSLOT, isinstance(c, int) and c == 1, False)
                        flip(c, 0, head)

                    chunk(0, 0, 0, True)
                    chunk(1, 0, 1, False)
                    loops = (NCH - 2) // NSLOT
                    with pe.Fori(0, loops) as r:
                        for i in range(NSLOT):
                            c = 2 + i
                            chunk(r * NSLOT + c, r + c // NSLOT, c % NSLOT, False)
                    for c in range(2 + loops * NSLOT, NCH):
                        chunk(c, c // NSLOT, c % NSLOT, False)
                    flip(NCH - 1, 1, False)
                    down(NCH - 1, (NCH - 1) % NSLOT, False, True)
                over_experts(pe, l, expert)


_INS = ["x", "mem", "positions", "norm_mix", "w_in", "ssm_a_re", "ssm_a_im", "ssm_log_dt", "ssm_b_re",
        "ssm_b_im", "ssm_c_re", "ssm_c_im", "ssm_d", "ssm_w_glu", "gdn_conv", "gdn_a_log", "gdn_dt_bias",
        "gdn_norm", "w_up_moba", "w_up_gdn", "w_out", "norm_xa", "norm_mem", "xa_wq", "xa_wk", "xa_wv",
        "xa_wo", "norm_ffn", "ffn_w_gate", "ffn_w_up", "ffn_w_down", "moe_w_router", "moe_w_gate",
        "moe_w_up", "moe_w_down", "norm_final"]


def kernel(**inputs):
    import numpy as _np
    import concourse.bacc as _bacc
    from concourse import mybir as _mybir
    from concourse.bass_utils import run_bass_kernel_spmd as _run

    nc = _bacc.Bacc("TRN2", target_bir_lowering=False, num_devices=1)
    arrays, args = {}, []
    for name in _INS:
        a = _np.ascontiguousarray(inputs[name])
        arrays[f"in_{name}"] = a
        args.append(nc.dram_tensor(f"in_{name}", a.shape, _mybir.dt.from_np(a.dtype), kind="ExternalInput").ap())
    shape = inputs["x"].shape
    args.append(nc.dram_tensor("out", shape, _mybir.dt.float32, kind="ExternalOutput").ap())
    hybrid_trunk(nc, *args)
    r = _run(nc, [arrays], core_ids=[0])
    return r.results[0]["out"]
```

```python
import math
from contextlib import ExitStack

import concourse.bass as bass
from concourse import mybir


def hybrid_trunk(nc: bass.Bass, x_d, mem_d, positions_d, norm_mix_d, w_in_d, a_re_d, a_im_d, log_dt_d,
                 b_re_d, b_im_d, c_re_d, c_im_d, ssm_d_d, w_glu_d, conv_d, a_log_d, dt_bias_d,
                 gdn_norm_d, w_up_moba_d, w_up_gdn_d, w_out_d, norm_xa_d, norm_mem_d, wq_d, wk_d, wv_d,
                 wo_d, norm_ffn_d, ffn_gate_d, ffn_up_d, ffn_down_d, router_d, moe_gate_d, moe_up_d,
                 moe_down_d, norm_final_d, out_d):
    F32 = mybir.dt.float32
    I32 = mybir.dt.int32
    ALU = mybir.AluOpType
    ACT = mybir.ActivationFunctionType
    AX = mybir.AxisListType

    P = 128
    SEQ, D = x_d.shape[1], x_d.shape[2]
    DEPTH = w_in_d.shape[0]
    NT = SEQ // P
    KD = D // P
    W = w_up_moba_d.shape[1]
    KW = W // P
    EPS = 1e-6
    NEG = -1e30
    MH, MD = 8, 64
    GH, GD, GL = 4, 128, 64
    NCHUNK = SEQ // GL
    XH, XD = 4, 128
    NS5 = 16
    NQ = 4
    D_FF = ffn_gate_d.shape[2]
    FC = 256
    NCH = D_FF // FC
    NE = moe_gate_d.shape[1]
    THETA = 10000.0
    TWO_PI = 2.0 * math.pi
    C1 = 6.28125
    C2 = TWO_PI - C1
    MAGIC = 1.5 * 2.0 ** 23
    PI_IN = 3.141592
    GELU_C = math.sqrt(2.0 / math.pi)
    NSLOT = 3
    SLOT = 6144
    IN_U, IN_QG, IN_KG, IN_VG, IN_AB, IN_Z, IN_GATE = 1536, 2048, 2560, 3072, 3584, 3592, 4104

    def in_cols(l, c0):
        return [(w_in_d[l].rearrange("(k p) n -> p k n", p=P)[:, :, c0:c0 + 512], 0, 512)]

    def half_width(w, l):
        return [(w[l].rearrange("(k p) n -> p k n", p=P), 0, D)]

    def glu_cols(l, n):
        v = w_glu_d[l].rearrange("(k p) (s n) -> s p k n", p=P, s=2)
        return [(v[s, :, :, n * 512:(n + 1) * 512], s * 512, D) for s in range(2)]

    def out_cols(l, n):
        return [(w_out_d[l].rearrange("(k p) n -> p k n", p=P)[:, :, n * 512:(n + 1) * 512], 0, 512)]

    def full_width(w, l):
        return [(w[l].rearrange("(k p) n -> p k n", p=P), 0, 512)]

    def mixer_units(l):
        return ([in_cols(l, c) for c in (IN_U, 0, 512, 1024, IN_Z)]
                + [in_cols(l, IN_GATE + 512 * g) for g in range(6)]
                + [in_cols(l, c) for c in (IN_QG, IN_KG, IN_VG)]
                + [half_width(w_up_moba_d, l), glu_cols(l, 0), glu_cols(l, 1), half_width(w_up_gdn_d, l),
                   out_cols(l, 0), out_cols(l, 1), full_width(wk_d, l), full_width(wv_d, l),
                   full_width(wq_d, l), half_width(wo_d, l)])

    U_U, U_Q, U_CONV = 0, 1, 11
    U_UPM, U_GLU, U_UPG, U_OUT, U_WK, U_WV, U_WQ, U_WO = 14, 15, 17, 18, 20, 21, 22, 23
    NUNIT = 24

    def experts(l):
        return 1 if l % 2 == 0 else NE

    def unit_base(l):
        return sum(NUNIT + NCH * experts(m) for m in range(l))

    def glu_extra(j):
        return 2 if j in (U_GLU, U_GLU + 1) else 1

    def slot_before(l, s):
        n = 0
        for m in range(l):
            n += sum(glu_extra(j) for j in range(NUNIT) if j % NSLOT == s)
            n += 3 * experts(m) * len([c for c in range(NCH) if c % NSLOT == s])
        return n

    def slot_after_unit(l, j):
        s = j % NSLOT
        return 16 * (slot_before(l, s) + sum(glu_extra(i) for i in range(j + 1) if i % NSLOT == s))

    def slot_after_chunk(l, e, c_in_slot, s):
        per_expert = 3 * len([c for c in range(NCH) if c % NSLOT == s])
        start = slot_before(l, s) + sum(glu_extra(i) for i in range(NUNIT) if i % NSLOT == s)
        return 16 * start + e * (16 * per_expert) + 48 * c_in_slot + 48

    ctx = ExitStack()
    with ctx:
        def sb(name, shape, dt=F32):
            return ctx.enter_context(nc.sbuf_tensor(name, shape, dt))

        def sem(name):
            return ctx.enter_context(nc.semaphore(name))

        class Region:

            def __init__(self, buf, end):
                self.buf, self.at, self.end = buf, 0, end

            def take(self, *shape):
                n = int(math.prod(shape))
                v = self.buf[:, self.at:self.at + n]
                self.at += n
                assert self.at <= self.end, (self.at, self.end)
                if len(shape) > 1:
                    names = "abcd"[:len(shape)]
                    v = v.rearrange(f"p ({' '.join(names)}) -> p {' '.join(names)}",
                                    **{n_: s for n_, s in zip(names, shape)})
                return v

        ring = sb("ring", [P, NSLOT * SLOT])
        x = sb("x", [P, NT, D])
        hT = sb("hT", [P, KD, SEQ])
        memT = sb("memT", [P, KD, SEQ])
        qk = sb("qk", [P, 2, NT, W])
        v_tok = sb("v_tok", [P, NT, W])
        z_tok = sb("z_tok", [P, NT, W])
        gates = sb("gates", [P, NT, 3 * D])
        uT = sb("uT", [P, NQ, SEQ])
        yT = sb("yT", [P, NQ, SEQ])
        RAW = SEQ + 3
        PH = 11776
        phase = sb("phase", [P, PH])
        raw = phase[:, 8192:8192 + 12 * RAW].rearrange("p (j n) -> p j n", n=RAW)
        merged = qk[:, :, :, :].rearrange("p a t n -> p (a t n)").rearrange("p (t n) -> p t n", t=NT)
        h_tok = gates[:, :, :].rearrange("p t n -> p (t n)")[:, 0:NT * D].rearrange("p (t n) -> p t n", t=NT)
        gain_out = gates[:, :, :].rearrange("p t n -> p (t n)")[:, NT * D:NT * D + D]
        spare = [ring[:, s * SLOT + 4096:(s + 1) * SLOT] for s in range(NSLOT)]

        def spare_half(s, i):
            return spare[s][:, i * 1024:(i + 1) * 1024]

        ident = sb("ident", [P, P])
        ones = sb("ones", [P, P])
        cum_mask = sb("cum_mask", [P, P])
        level_mask = sb("level_mask", [P, 6, P])
        causal = sb("causal", [P, 3 * P])
        b_mask = sb("b_mask", [P, NQ, 8, 16])
        c_mask = sb("c_mask", [P, NQ, 2, 64])
        steps = sb("steps", [P, SEQ])
        before = sb("before", [P, P])
        inv_freq = sb("inv_freq", [P, MD // 2])
        params = sb("params", [P, 3 * P])
        small_bc = sb("small_bc", [P, DEPTH, 2, GH])
        gnorm_bc = sb("gnorm_bc", [P, DEPTH, GD])
        cosr = sb("cosr", [P, NT, MD // 2])
        sinr = sb("sinr", [P, NT, MD // 2])
        pos_i = sb("pos_i", [P, NT], I32)
        pos_f = sb("pos_f", [P, NT])
        s5c = sb("s5c", [P, 14, DEPTH * NS5])
        idx8 = sb("idx8", [P, 8])
        eps_col = sb("eps_col", [P, 3])
        router_w = sb("router_w", [P, KD, NE])
        ab_w = sb("ab_w", [P, KD, 2 * GH])
        st = sb("st", [P, 96])

        NG = DEPTH * KD
        gain_mix, gain_xa, gain_mem, gain_ffn = (params[:, i * NG:(i + 1) * NG] for i in range(4))
        p_are = params[:, 64:96]
        p_aim = params[:, 96:128]
        p_conv = params[:, 128:224]
        p_dt = params[:, 224:256]
        p_d = params[:, 256:264]
        DEC, THR, BCR, BCI = (s5c[:, i, :] for i in range(4))

        ss, rstd = st[:, 0:2], st[:, 2:4]
        mx, nm, rs = st[:, 4:8], st[:, 8:12], st[:, 12:16]
        ab = st[:, 16:32]
        gate_z, gate_e = st[:, 32:40], st[:, 40:48]
        gcum, beta = st[:, 48:56], st[:, 56:64]
        bexp = st[:, 64:72]
        kds = st[:, 72:80]
        gstep = st[:, 80:88]
        ealog = st[:, 88:92]

        r5 = Region(phase, PH)
        tab = [r5.take(NQ, 2, SEQ) for _ in range(2)]
        bct = [[r5.take(NQ, P) for _ in range(4)] for _ in range(2)]
        c_nat = r5.take(2, NQ, 64)
        b_bar = r5.take(2, NS5, 16)
        wk5 = [r5.take(2, SEQ) for _ in range(5)]
        ang, turns = spare_half(0, 0), spare_half(0, 1)
        s_half = spare_half(1, 0)
        pads = spare_half(1, 1).rearrange("p (c n) -> p c n", c=2)
        y5 = yT[:, :, :]
        b_nat = spare_half(2, 0)[:, 0:2 * NS5 * 16].rearrange("p (c t n) -> p c t n", c=2, t=NS5)
        y5b = spare_half(2, 1).rearrange("p (c n) -> p c n", n=SEQ)

        rm = Region(phase, PH)
        mqT, mkT = rm.take(KW, SEQ), rm.take(KW, SEQ)
        m_oT = rm.take(KW, SEQ)
        mp_ = [rm.take(3 * P) for _ in range(2)]
        mpT = [rm.take(3 * P) for _ in range(2)]
        glu_t = [rm.take(512) for _ in range(2)]
        glu_y = [rm.take(512) for _ in range(2)]
        gl_tmp = [rm.take(512) for _ in range(2)]

        rg = Region(phase, PH)
        cv = rg.take(12, SEQ)
        k_tok = rg.take(NT, GH, GD)
        kbeg = rg.take(NT, GH, GD)
        vbeta = rg.take(NT, GH, GD)
        kdec = rg.take(NT, GH, GD)
        e_row = rg.take(NT, GH, P)
        dec = rg.take(NT, GH, P)
        decT = rg.take(NT, GH, P)
        qkT = rg.take(NT, GH, P)
        vn = rg.take(GH, GD)
        wT, u_tok = dec, decT
        o_tok, g_oT = k_tok, kbeg.rearrange("p t h d -> p (t h d)").rearrange("p (k n) -> p k n", k=KW)
        Xi = uT[:, :, :].rearrange("p q n -> p (q n)").rearrange("p (t h n) -> p t h n", t=NT, h=GH)
        Zi = yT[:, :, :].rearrange("p q n -> p (q n)").rearrange("p (t h n) -> p t h n", t=NT, h=GH)
        state = v_tok[:, :, :].rearrange("p t (h n) -> p t h n", h=GH)
        rq = [kbeg, vbeta, kdec, qkT]
        A_low, M_lvl, W_lvl, DTm, Dcl, gdiag = (
            spare_half(i // 2, i % 2).rearrange("p (t h n) -> p t h n", t=NT, h=GH) for i in range(6))

        rx = Region(phase, PH)
        memnT = rx.take(KD, SEQ)
        xkT, xqT, x_oT = rx.take(XH, SEQ), rx.take(XH, SEQ), rx.take(XH, SEQ)
        x_v = rx.take(NT, W)
        xp = [rx.take(NT, SEQ) for _ in range(2)]
        xpT = [rx.take(NT, SEQ) for _ in range(2)]

        rf = Region(phase, PH)
        f_th = [rf.take(FC) for _ in range(NT)]
        f_a = [rf.take(FC) for _ in range(NT)]
        f_act = [rf.take(FC) for _ in range(NT)]
        f_actT = rf.take(FC // P, SEQ)
        r_log = rf.take(NT, NE)
        r_max = rf.take(NT, NE)
        r_w = rf.take(NT, 4)
        r_eq = rf.take(2, NT, NE)
        r_idx = sb("r_idx", [P, NT, NE], mybir.dt.uint32)
        r_idf = rf.take(NT, NE)
        comb, chosen, place = (rf.take(NT, NE + 1) for _ in range(3))
        e_count = rf.take(NE)
        e_most = rf.take(1)
        over_i = sb("over_i", [P, 1], I32)
        gather_m = rf.take(NT, P)
        weight_m = rf.take(NT, P)
        scatter_m = rf.take(NT * P)
        h_e = rf.take(KD, P)
        y_e = rf.take(D)
        gain_bc = gates[:, :, :].rearrange("p t n -> p (t n)")[:, 3 * D:4 * D]

        B = [ctx.enter_context(nc.psum_tensor(f"bank{i}", [P, 512], F32)) for i in range(8)]

        x_in, mem_in, par_in, bc_in, rout_in = sem("x_in"), sem("mem_in"), sem("par_in"), sem("bc_in"), sem("rout_in")
        pos_in, fin_in, out_done = sem("pos_in"), sem("fin_in"), sem("out_done")
        slot_full = [sem(f"slot_full{s}") for s in range(NSLOT)]
        chunk_used = sem("chunk_used")
        ab_in, bc_nat_in = sem("ab_in"), sem("bc_nat_in")
        consts = sem("consts")
        pool_chain, act_chain, dve_chain = sem("pool_chain"), sem("act_chain"), sem("dve_chain")
        par_ps, par_ready = sem("par_ps"), sem("par_ready")
        norm_sq, norm_ss, norm_h, norm_ps, hT_ready = sem("norm_sq"), sem("norm_ss"), sem("norm_h"), sem("norm_ps"), sem("hT_ready")
        s5_dt, s5_ang, s5_sin, s5_const = sem("s5_dt"), sem("s5_ang"), sem("s5_sin"), sem("s5_const")
        rot_ang, rot_sin = sem("rot_ang"), sem("rot_sin")
        ws_ready, ws_evac = sem("ws_ready"), sem("ws_evac")
        ab_ps, ab_sb = sem("ab_ps"), sem("ab_sb")
        fill_ready, rope_done, fill_evac = sem("fill_ready"), sem("rope_done"), sem("fill_evac")
        tab_ang, tab_ready, tab_sin = sem("tab_ang"), sem("tab_ready"), sem("tab_sin")
        b_bar_ready, pad_ready, pad_ps, bct_ready = sem("b_bar_ready"), sem("pad_ready"), sem("pad_ps"), sem("bct_ready")
        bu_ready, bu_read, h_rot, y_read = sem("bu_ready"), sem("bu_read"), sem("h_rot"), sem("y_read")
        gel_in, gel_t, y_ready = sem("gel_in"), sem("gel_t"), sem("y_ready")
        mtr_ps, mtr_ready = sem("mtr_ps"), sem("mtr_ready")
        ms_ready, ms_neg, ms_exp, ms_norm, ms_tr, ms_pT, ms_o, ms_oT = (
            sem(n) for n in ("ms_ready", "ms_neg", "ms_exp", "ms_norm", "ms_tr", "ms_pT", "ms_o", "ms_oT"))
        up_ps, up_used = sem("up_ps"), sem("up_used")
        glu_ps, glu_th, glu_used = sem("glu_ps"), sem("glu_th"), sem("glu_used")
        cv_tap, cv_pre, cv_th, cv_ready, cv_sq, cv_ss, cv_rs, kq_ready = (
            sem(n) for n in ("cv_tap", "cv_pre", "cv_th", "cv_ready", "cv_sq", "cv_ss", "cv_rs", "kq_ready"))
        g_z, g_exp, g_ln, g_step, gc_ps, gc_sb, g_bexp, g_diag, row_ps = (
            sem(n) for n in ("g_z", "g_exp", "g_ln", "g_step", "gc_ps", "gc_sb", "g_bexp", "g_diag", "row_ps"))
        dec_in, dec_ready, kv_ps, kv_evac, kk_ps, a_ready, qk_ready = (
            sem(n) for n in ("dec_in", "dec_ready", "kv_ps", "kv_evac", "kk_ps", "a_ready", "qk_ready"))
        xz_init, m_ready, w_ps, w_evac, xz_ps, xz_ready = (
            sem(n) for n in ("xz_init", "m_ready", "w_ps", "w_evac", "xz_ps", "xz_ready"))
        uw_in, uw_ps, w_done, u_done, qd_ready = (sem(n) for n in ("uw_in", "uw_ps", "w_done", "u_done", "qd_ready"))
        s_init, vn_ps, vn_ready, o_ps, su_ps, s_ready, o_evac = (
            sem(n) for n in ("s_init", "vn_ps", "vn_ready", "o_ps", "su_ps", "s_ready", "o_evac"))
        og_ss, og_rs, og_ready, og_ps, og_T = sem("og_ss"), sem("og_rs"), sem("og_ready"), sem("og_ps"), sem("og_T")
        mg_ready, mg_ps, mg_T, wo_ps, wo_used = sem("mg_ready"), sem("mg_ps"), sem("mg_T"), sem("wo_ps"), sem("wo_used")
        memn_ready, xk_ps, xk_sb = sem("memn_ready"), sem("xk_ps"), sem("xk_sb")
        xs_ps, xs_neg, xs_exp, xs_norm, xs_tr, xs_pT, xs_o, xs_oT = (
            sem(n) for n in ("xs_ps", "xs_neg", "xs_exp", "xs_norm", "xs_tr", "xs_pT", "xs_o", "xs_oT"))
        xo_ps, xo_used = sem("xo_ps"), sem("xo_used")
        rl_ps, rl_d, rl_e, comb_ready = (sem(n) for n in ("rl_ps", "rl_d", "rl_e", "comb_ready"))
        gain_in, h_gain, place_ps, place_ready = (sem(n) for n in ("gain_in", "h_gain", "place_ps", "place_ready"))
        gm_ready, wm_ready, he_ps, he_ready, sm_ps, sm_ready, ye_ready, sc_ps, sc_used = (
            sem(n) for n in ("gm_ready", "wm_ready", "he_ps", "he_ready", "sm_ps", "sm_ready", "ye_ready", "sc_ps",
                             "sc_used"))
        gu_ps, gu_th, gu_a, act_ready, act_tr, actT_ready, y_added = (
            sem(n) for n in ("gu_ps", "gu_th", "gu_a", "act_ready", "act_tr", "actT_ready", "y_added"))
        fin_ready = sem("fin_ready")

        NNORM = 3 * DEPTH + 1

        def multiplied(l, j):
            if j == U_U:
                return ws_ready, 8 * l + 2
            if j < U_CONV:
                return fill_ready, 20 * l + 2 * (j - U_Q) + 2
            if j < U_UPM:
                return ws_ready, 8 * l + 2 * (j - U_CONV) + 4
            return {U_UPM: (up_ps, 8 * l + 4), U_GLU: (glu_ps, 4 * l + 2), U_GLU + 1: (glu_ps, 4 * l + 4),
                    U_UPG: (up_ps, 8 * l + 8), U_OUT: (wo_ps, 4 * l + 2), U_OUT + 1: (wo_ps, 4 * l + 4),
                    U_WK: (xk_ps, 6 * l + 2), U_WV: (xk_ps, 6 * l + 4), U_WQ: (xk_ps, 6 * l + 6),
                    U_WO: (xo_ps, 4 * l + 4)}[j]

        def slot(j):
            return ring[:, (j % NSLOT) * SLOT:(j % NSLOT) * SLOT + SLOT]

        def experts_before(l):
            return sum(experts(m) for m in range(l))

        def chunks_of_expert(eng, chunk):
            chunk(0, 0)
            loops = (NCH - 1) // NSLOT
            with eng.Fori(0, loops) as r:
                for i in range(NSLOT):
                    chunk(r * NSLOT + (1 + i), (1 + i) % NSLOT)
            for c in range(1 + loops * NSLOT, NCH):
                chunk(c, c % NSLOT)

        def moe_passes(eng, one_pass):
            one_pass(0)
            eng.wait_ge(place_ready, 1)
            more = eng.value_load(over_i[0:1, 0:1], min_val=0, max_val=1)
            with eng.If(more > 0):
                one_pass(1)

        def acts_before(l):
            return sum(NCH * (NT if m % 2 == 0 else NE) for m in range(l))

        block = ctx.enter_context(nc.Block())

        @block.sync
        def _(sp):
            x_v_ = x_d[0].rearrange("(t p) n -> p t n", p=P)
            sp.dma_start(x[:, :, :], x_v_).then_inc(x_in, 16)

            def load(pieces, l, j):
                for src, at, width in pieces:
                    n = src.shape[2]
                    dst = slot(j)[:, 0:4096].rearrange("p (k w) -> p k w", w=width)[:, :, at:at + n]
                    sp.dma_start(dst, src).then_inc(slot_full[j % NSLOT], 16)

            def layer_units(l):
                for j, pieces in enumerate(mixer_units(l)):
                    if j >= NSLOT:
                        sp.wait_ge(*multiplied(l, j - NSLOT))
                    elif l > 0:
                        sp.wait_ge(chunk_used, NCH * experts_before(l) - (1, 0, 2)[j])
                    load(pieces, l, j)

            def expert_chunks(l):
                if l % 2 == 0:
                    gate, up, down = (w[l // 2:l // 2 + 1] for w in (ffn_gate_d, ffn_up_d, ffn_down_d))
                else:
                    gate, up, down = (w[l // 2] for w in (moe_gate_d, moe_up_d, moe_down_d))
                gate = gate.rearrange("e (k p) (c f) -> e c p k f", p=P, f=FC)
                up = up.rearrange("e (k p) (c f) -> e c p k f", p=P, f=FC)
                down = down.rearrange("e (c k p) n -> e c p k n", p=P, k=FC // P)

                def expert(e, first):
                    def chunk(c, s):
                        v = ring[:, s * SLOT:(s + 1) * SLOT]
                        gu = v[:, 0:4096].rearrange("p (k b f) -> p k b f", b=2, f=FC)
                        sp.dma_start(gu[:, :, 0, :], gate[e, c]).then_inc(slot_full[s], 16)
                        sp.dma_start(gu[:, :, 1, :], up[e, c]).then_inc(slot_full[s], 16)
                        sp.dma_start(v[:, 4096:6144].rearrange("p (k n) -> p k n", n=D),
                                     down[e, c]).then_inc(slot_full[s], 16)

                    for c in range(NSLOT):
                        sp.wait_ge(*multiplied(l, NUNIT - NSLOT + c))
                        if not isinstance(e, int):
                            sp.wait_ge(chunk_used, e * NCH + (first + c - (2, 2, 5)[c] + 1))
                        chunk(c, c)
                    loops = NCH // NSLOT - 1
                    with sp.Fori(0, loops) as r:
                        for i in range(NSLOT):
                            sp.wait_ge(chunk_used, e * NCH + r * NSLOT + (first + i + 1))
                            chunk(r * NSLOT + (NSLOT + i), i)
                    for c in range(NSLOT * (loops + 1), NCH):
                        sp.wait_ge(chunk_used, e * NCH + (first + c - NSLOT + 1))
                        chunk(c, c % NSLOT)

                def one_pass(p):
                    with sp.Fori(0, NE) as e:
                        expert(e, NCH * (experts_before(l) + p * NE))

                if l % 2 == 0:
                    expert(0, NCH * experts_before(l))
                else:
                    moe_passes(sp, one_pass)

            for l in range(DEPTH):
                layer_units(l)
                expert_chunks(l)
            sp.wait_ge(fin_ready, 1)
            sp.dma_start(out_d[0].rearrange("(t p) n -> p t n", p=P), x[:, :, :]).then_inc(out_done, 16)
            sp.wait_ge(out_done, 16)

        @block.gpsimd
        def _(pool):
            chain = [0]

            def link(ins):
                chain[0] += 1
                ins.then_inc(pool_chain, 1)
                pool.wait_ge(pool_chain, chain[0])

            def keep(v, pattern, base, cm):
                link(nc.gpsimd.affine_select(out=v, in_=v, pattern=pattern, base=base, channel_multiplier=cm,
                                             compare_op=ALU.is_ge, fill=0.0))

            link(nc.gpsimd.memset(ident[:, :], 0.0))
            nc.gpsimd.affine_select(out=ident[:, :], in_=ident[:, :], pattern=[[-1, P]], base=0,
                                    channel_multiplier=1, compare_op=ALU.not_equal,
                                    fill=1.0).then_inc(consts, 1)
            rows = phase[:, 0:3 * P].rearrange("p (a n) -> p a n", a=3)
            for i, w in enumerate((norm_mix_d, norm_xa_d, norm_mem_d, norm_ffn_d)):
                pool.dma_start(rows[i * NG:(i + 1) * NG, 0, :],
                               w.rearrange("l (k p) -> (l k) p", p=P)).then_inc(par_in, 16)
            pool.dma_start(rows[64:96, 0, :], a_re_d.rearrange("l (t g) s -> (l t) (g s)", g=2)).then_inc(par_in, 16)
            pool.dma_start(rows[96:128, 0, :], a_im_d.rearrange("l (t g) s -> (l t) (g s)", g=2)).then_inc(par_in, 16)
            pool.dma_start(rows[0:96, 1, :], conv_d.rearrange("l i (j p) -> (l i j) p", p=P)).then_inc(par_in, 16)
            dtr = phase[:, 3 * P:3 * P + 2]
            pool.dma_start(dtr[96:128, :], log_dt_d.rearrange("l (t g) -> (l t) g", g=2)).then_inc(par_in, 16)
            pool.dma_start(rows[0:8, 2, :], ssm_d_d.rearrange("l (k p) -> (l k) p", p=P)).then_inc(par_in, 16)
            link(nc.gpsimd.memset(ones[:, :], 1.0))
            for i, e in enumerate((EPS, 4.0 * EPS, 1.0)):
                nc.gpsimd.memset(eps_col[:, i:i + 1], e)
            for j in range(MD // 2):
                nc.gpsimd.memset(inv_freq[:, j:j + 1], THETA ** (-2.0 * j / MD))
            link(nc.gpsimd.iota(steps[:, :], pattern=[[1, SEQ]], base=0, channel_multiplier=0,
                                allow_small_or_imprecise_dtypes=True))
            link(nc.gpsimd.iota(idx8[:, :], pattern=[[1, 8]], base=0, channel_multiplier=0,
                                allow_small_or_imprecise_dtypes=True))
            pool.wait_ge(par_in, 16 * 9)
            link(nc.gpsimd.tensor_copy(rows[96:128, 1, :].rearrange("p (g s) -> p g s", g=2),
                                       dtr[96:128, :].unsqueeze(2).to_broadcast([32, 2, 64])))
            nc.gpsimd.memset(st[:, :], 0.0).then_inc(consts, 1)
            for m in (b_mask, c_mask):
                link(nc.gpsimd.memset(m[:, :, :, :], 1.0))
            keep(b_mask[:, :, :, :], [[128, NQ], [-64, 8], [0, 16]], 0, 1)
            keep(b_mask[:, :, :, :], [[-128, NQ], [64, 8], [0, 16]], 63, -1)
            keep(c_mask[:, :, :, :], [[-32, NQ], [-16, 2], [0, 64]], 0, 1)
            keep(c_mask[:, :, :, :], [[32, NQ], [16, 2], [0, 64]], 15, -1)
            link(nc.gpsimd.memset(cum_mask[:, :], 1.0))
            keep(cum_mask[:, :], [[1, P]], 0, -1)
            cm2 = cum_mask[:, :].rearrange("p (a b) -> p a b", b=GL)
            keep(cm2, [[-GL, P // GL], [0, GL]], 0, 1)
            keep(cm2, [[GL, P // GL], [0, GL]], GL - 1, -1)
            link(nc.gpsimd.memset(before[:, :], 1.0))
            keep(before[:, :], [[1, P]], -1, -1)
            link(nc.gpsimd.memset(level_mask[:, :, :], 0.0))
            for k in range(6):
                b = 2 ** k
                q = level_mask[:, k, :].rearrange("p (a h b) -> p a h b", h=2, b=b)[:, :, 0, :]
                link(nc.gpsimd.memset(q, 1.0))
                keep(q, [[-2 * b, P // (2 * b)], [0, b]], -b, 1)
                keep(q, [[2 * b, P // (2 * b)], [0, b]], 2 * b - 1, -1)
            link(nc.gpsimd.memset(causal[:, :], 0.0))
            for at in (0, 2 * P):
                last = nc.gpsimd.affine_select(out=causal[:, at:at + P], in_=causal[:, at:at + P],
                                               pattern=[[-1, P]], base=0, channel_multiplier=1,
                                               compare_op=ALU.is_ge, fill=NEG)
            last.then_inc(consts, 1)

            def angle_table(l, q):
                n = NQ * l + q
                if n >= 1:
                    pool.wait_ge(tab_sin, n)
                a3 = ang.rearrange("p (c n) -> p c n", n=SEQ)
                th = THR[:, l * NS5 + NQ * q:l * NS5 + NQ * (q + 1)].unsqueeze(2).to_broadcast([P, NQ, SEQ])
                sx = steps[:, :].unsqueeze(1).to_broadcast([P, NQ, SEQ])
                link(nc.gpsimd.tensor_tensor(a3, th, sx, ALU.mult))
                link(nc.gpsimd.tensor_scalar(turns, ang, 1.0 / TWO_PI, MAGIC, ALU.mult, ALU.add))
                link(nc.gpsimd.tensor_scalar(turns, turns, -MAGIC, None, ALU.add))
                link(nc.gpsimd.tensor_scalar(s_half, turns, C1, None, ALU.mult))
                link(nc.gpsimd.tensor_tensor(ang, ang, s_half, ALU.subtract))
                link(nc.gpsimd.tensor_scalar(s_half, turns, C2, None, ALU.mult))
                link(nc.gpsimd.tensor_tensor(ang, ang, s_half, ALU.subtract))
                nc.gpsimd.tensor_scalar(ang, ang, PI_IN, -PI_IN, ALU.min, ALU.max).then_inc(tab_ang, 1)

            def pad_b(l, q):
                n = 2 * (NQ * l + q)
                if n >= 1:
                    pool.wait_ge(pad_ps, n)
                for c in range(2):
                    src = b_bar[:, c, NQ * q:NQ * (q + 1), :].unsqueeze(2).to_broadcast([P, NQ, 8, 16])
                    last = nc.gpsimd.tensor_tensor(pads[:, c, :].rearrange("p (t g n) -> p t g n", t=NQ, g=8),
                                                   src, b_mask[:, :, :, :], ALU.mult)
                    last.then_inc(pad_ready, 1)

            def pad_c(l, q):
                pool.wait_ge(pad_ps, 2 * (NQ * l + q) + 1)
                for c in range(2):
                    src = c_nat[:, c, q, :].unsqueeze(1).unsqueeze(1).to_broadcast([P, NQ, 2, 64])
                    last = nc.gpsimd.tensor_tensor(pads[:, c, :].rearrange("p (t g n) -> p t g n", t=NQ, g=2),
                                                   src, c_mask[:, :, :, :], ALU.mult)
                    last.then_inc(pad_ready, 1)

            for l in range(DEPTH):
                if l > 0:
                    pool.wait_ge(y_added, (l + 1) // 2)
                if l > 0:
                    pool.wait_ge(hT_ready, 1 + 3 * l)
                pool.wait_ge(par_ready, 1)
                pool.dma_start(b_nat[:, 0], b_re_d[l].rearrange("(t g) s n -> (g s) t n", g=2)).then_inc(bc_nat_in, 16)
                pool.dma_start(b_nat[:, 1], b_im_d[l].rearrange("(t g) s n -> (g s) t n", g=2)).then_inc(bc_nat_in, 16)
                pool.dma_start(c_nat[:, 0], c_re_d[l].rearrange("(q g) n s -> (g n) q s", q=NQ)).then_inc(bc_nat_in, 16)
                pool.dma_start(c_nat[:, 1], c_im_d[l].rearrange("(q g) n s -> (g n) q s", q=NQ)).then_inc(bc_nat_in, 16)
                if l == 0:
                    pool.wait_ge(s5_const, 1)
                for q in range(NQ):
                    angle_table(l, q)
                    if q == 0:
                        pool.wait_ge(bc_nat_in, 64 * (l + 1))
                        pool.wait_ge(b_bar_ready, l + 1)
                    pad_b(l, q)
                    pad_c(l, q)
                for t in range(NT):
                    pool.wait_ge(a_ready, NT * l + t + 1)
                    for m in (Xi, Zi):
                        last = nc.gpsimd.tensor_copy(m[:, t], ident[:, :].unsqueeze(1).to_broadcast([P, GH, P]))
                        last.then_inc(xz_init, 1)
                for k in range(6):
                    for t in range(NT):
                        n = (6 * l + k) * NT + t
                        if k > 0:
                            pool.wait_ge(w_ps, n - NT + 1)
                        nc.gpsimd.tensor_tensor(M_lvl[:, t], A_low[:, t],
                                                level_mask[:, k, :].unsqueeze(1).to_broadcast([P, GH, P]),
                                                ALU.mult).then_inc(m_ready, 1)

        @block.scalar
        def _(act):
            chain = [0]

            def link(ins):
                chain[0] += 1
                ins.then_inc(act_chain, 1)
                act.wait_ge(act_chain, chain[0])

            act.dma_start(h_tok, mem_d[0].rearrange("(t p) n -> p t n", p=P)).then_inc(mem_in, 16)
            with nc.allow_non_contiguous_dma("one position per partition"):
                act.dma_start(pos_i[:, :], positions_d[0].rearrange("(t p) -> p t", p=P)).then_inc(pos_in, 16)
            for l in range(DEPTH):
                act.dma_start(small_bc[:, l, 0, :], a_log_d[l:l + 1, :].to_broadcast([P, GH])).then_inc(bc_in, 16)
                act.dma_start(small_bc[:, l, 1, :], dt_bias_d[l:l + 1, :].to_broadcast([P, GH])).then_inc(bc_in, 16)
                act.dma_start(gnorm_bc[:, l, :], gdn_norm_d[l:l + 1, :].to_broadcast([P, GD])).then_inc(bc_in, 16)
            act.dma_start(router_w[:, :, :], router_d[0].rearrange("(k p) n -> p k n", p=P)).then_inc(rout_in, 16)

            def load_ab(l):
                act.dma_start(ab_w[:, :, :], w_in_d[l].rearrange("(k p) n -> p k n", p=P)
                              [:, :, IN_AB:IN_AB + 2 * GH]).then_inc(ab_in, 16)

            load_ab(0)

            def sum_squares(src, n):
                for t in range(NT):
                    nc.scalar.activation(hT[:, :, :].rearrange("p k n -> p (k n)")[:, t * D:(t + 1) * D],
                                         src[:, t, :], ACT.Square,
                                         accum_out=ss[:, t:t + 1]).then_inc(norm_sq, 1)
                act.wait_ge(norm_sq, NT * (n + 1))
                link(nc.scalar.activation(ss, ss, ACT.Ln, scale=1.0 / D, bias=eps_col[:, 0:1]))
                nc.scalar.activation(rstd, ss, ACT.Exp, scale=-0.5).then_inc(norm_ss, 1)

            def evac_norm(n, dst, gain, at, done):
                for b in range(4):
                    act.wait_ge(norm_ps, 4 * n + b + 1)
                    for i in range(2):
                        k = 2 * b + i
                        if gain is None:
                            last = nc.scalar.activation(dst[:, k, :], B[4 + b][:, i * SEQ:(i + 1) * SEQ], ACT.Copy)
                        else:
                            last = nc.scalar.activation(dst[:, k, :], B[4 + b][:, i * SEQ:(i + 1) * SEQ], ACT.Copy,
                                                        scale=gain[:, at + k:at + k + 1])
                last.then_inc(done, 1)

            act.wait_ge(par_ps, 1)
            nc.scalar.activation(params[:, 0:2 * P + 8], B[0][:, 0:2 * P + 8], ACT.Copy).then_inc(par_ready, 1)
            act.wait_ge(mem_in, 16)
            act.wait_ge(consts, 2)
            sum_squares(h_tok, 0)
            evac_norm(0, memT[:, :, :], None, 0, hT_ready)

            act.wait_ge(par_ready, 1)
            nc.scalar.activation(s5c[:, 4, :], p_dt, ACT.Exp).then_inc(s5_dt, 1)
            act.wait_ge(s5_ang, 1)
            nc.scalar.activation(DEC, s5c[:, 5, :], ACT.Exp)
            nc.scalar.activation(s5c[:, 6, :], THR, ACT.Sin)
            nc.scalar.activation(s5c[:, 7, :], THR, ACT.Sin, scale=0.5).then_inc(s5_sin, 1)
            act.wait_ge(rot_ang, 1)
            link(nc.scalar.activation(sinr[:, :, :], cosr[:, :, :], ACT.Sin))
            nc.scalar.activation(cosr[:, :, :], cosr[:, :, :], ACT.Sin, scale=0.5).then_inc(rot_sin, 1)
            act.wait_ge(bc_in, 16 * 3 * DEPTH)

            def table(l, q):
                n = NQ * l + q
                if n >= 2:
                    act.wait_ge(h_rot, NS5 * l + NQ * (q - 2) + NQ if q >= 2 else NS5 * l)
                act.wait_ge(tab_ang, n + 1)
                T = tab[q % 2]
                nc.scalar.activation(T[:, :, 1, :], ang.rearrange("p (c n) -> p c n", n=SEQ), ACT.Sin)
                link(nc.scalar.activation(T[:, :, 0, :], ang.rearrange("p (c n) -> p c n", n=SEQ), ACT.Sin, scale=0.5))
                nc.scalar.activation(T[:, :, 0, :], T[:, :, 0, :], ACT.Square).then_inc(tab_sin, 1)

            def bct_evac(l, q):
                for half in range(2):
                    n = 2 * (NQ * l + q) + half
                    act.wait_ge(pad_ps, n + 1)
                    if NQ * l + q >= 2 and half == 0:
                        act.wait_ge(y_read, NQ * (NQ * l + q - 1))
                    for c in range(2):
                        last = nc.scalar.activation(bct[q % 2][2 * half + c].rearrange("p t n -> p (t n)"),
                                                    B[6 + c][:, :], ACT.Copy,
                                                    scale=-1.0 if (half == 1 and c == 1) else 1.0)
                    last.then_inc(bct_ready, 1)

            for l in range(DEPTH):
                n = 1 + 3 * l
                act.wait_ge(x_in, 16)
                sum_squares(x[:, :, :], n)
                if l == 0:
                    act.wait_ge(par_ready, 1)
                evac_norm(n, hT[:, :, :], gain_mix, l * KD, hT_ready)
                table(l, 0)
                def ws_copy(w):
                    for b in range(2):
                        act.wait_ge(ws_ready, 8 * l + 2 * w + b + 1)
                        src = B[(2 if w == 2 else 0) + b][:, :].rearrange("p (c n) -> p c n", n=SEQ)
                        dst = (uT[:, 2 * b:2 * b + 2, :] if w == 0
                               else raw[:, 4 * (w - 1) + 2 * b:4 * (w - 1) + 2 * b + 2, 3:RAW])
                        nc.scalar.activation(dst, src, ACT.Copy).then_inc(ws_evac, 1)

                ws_copy(0)
                bct_evac(l, 0)
                act.wait_ge(ab_ps, l + 1)
                nc.scalar.activation(ab, B[4][:, 0:16], ACT.Copy).then_inc(ab_sb, 1)
                if l + 1 < DEPTH:
                    act.wait_ge(ab_ps, l + 1)
                    load_ab(l + 1)
                for f in range(4, 20):
                    i = f - 4
                    q, t = f // 2, f % 2
                    act.wait_ge(fill_ready, 20 * l + f + 1)
                    if q == 2:
                        nc.scalar.activation(v_tok[:, t, :], B[t][:, :], ACT.Copy).then_inc(fill_evac, 1)
                    elif q == 3:
                        nc.scalar.activation(z_tok[:, t, :], B[t][:, :], ACT.Copy).then_inc(fill_evac, 1)
                    else:
                        nc.scalar.activation(gates[:, t, (q - 4) * 512:(q - 3) * 512], B[t][:, :], ACT.Tanh,
                                             scale=0.5).then_inc(fill_evac, 1)
                    if i % NQ == 1 and i // NQ + 1 < NQ:
                        bct_evac(l, i // NQ + 1)
                    if i % NQ == 0 and i // NQ + 1 < NQ:
                        table(l, i // NQ + 1)
                for q in range(NQ):
                    act.wait_ge(gel_in, NQ * l + q + 1)
                    nc.scalar.activation(y5b[:, q, :], y5b[:, q, :], ACT.Tanh, scale=GELU_C).then_inc(gel_t, 1)
                act.wait_ge(y_ready, l + 1)
                for w in range(1, 4):
                    ws_copy(w)
                for i in range(4):
                    act.wait_ge(mtr_ps, 4 * l + i + 1)
                    dst = (mqT, mkT)[i // 2][:, :, (i % 2) * P:(i % 2 + 1) * P]
                    nc.scalar.activation(dst, B[4 + i][:, :].rearrange("p (k n) -> p k n", n=P),
                                         ACT.Copy).then_inc(mtr_ready, 1)

                def moba_exp(h):
                    n = MH * l + h
                    act.wait_ge(ms_neg, n + 1)
                    p = mp_[h % 2]
                    o = 2 * (h % 2)
                    nc.scalar.activation(p[:, 0:P], p[:, 0:P], ACT.Exp, bias=nm[:, o:o + 1], scale=MD ** -0.5,
                                         accum_out=rs[:, o:o + 1])
                    nc.scalar.activation(p[:, P:3 * P], p[:, P:3 * P], ACT.Exp, bias=nm[:, o + 1:o + 2],
                                         scale=MD ** -0.5, accum_out=rs[:, o + 1:o + 2]).then_inc(ms_exp, 1)

                def moba_pT(h):
                    n = MH * l + h
                    act.wait_ge(ms_tr, n + 1)
                    if n >= 2:
                        act.wait_ge(ms_o, n - 1)
                    nc.scalar.activation(mpT[h % 2], B[4 + h % 2][:, 0:3 * P], ACT.Copy).then_inc(ms_pT, 1)

                def moba_oT(j):
                    act.wait_ge(ms_o, MH * l + 2 * j + 2)
                    nc.scalar.activation(m_oT[:, j, :], B[6 + j % 2][:, 0:SEQ], ACT.Copy).then_inc(ms_oT, 1)

                for s in range(MH + 2):
                    if s < MH:
                        moba_exp(s)
                    if 1 <= s <= MH:
                        moba_pT(s - 1)
                    if s >= 3 and s % 2 == 1:
                        moba_oT((s - 3) // 2)
                for n_ in range(2):
                    for t in range(NT):
                        i = 2 * n_ + t
                        act.wait_ge(glu_ps, 4 * l + i + 1)
                        if i >= 2:
                            act.wait_ge(glu_used, 4 * l + i - 1)
                        nc.scalar.activation(glu_t[t], B[2 * t + 1][:, :], ACT.Tanh, scale=0.5).then_inc(glu_th, 1)
                act.wait_ge(glu_used, 4 * l + 4)
                for j in range(12):
                    last = nc.scalar.activation(cv[:, j, :], raw[:, j, 0:SEQ], ACT.Copy,
                                                scale=p_conv[:, 48 * l + j:48 * l + j + 1])
                    last.then_inc(cv_tap, 1)
                act.wait_ge(g_z, l + 1)
                nc.scalar.activation(ealog, small_bc[:, l, 0, :], ACT.Exp)
                link(nc.scalar.activation(gate_e, gate_e, ACT.Exp, scale=-1.0))
                nc.scalar.activation(gate_e, gate_e, ACT.Ln, bias=eps_col[:, 2:3]).then_inc(g_ln, 1)
                nc.scalar.activation(beta.rearrange("p (t h) -> p t h", t=NT),
                                     ab.rearrange("p (t c h) -> p t c h", t=NT, c=2)[:, :, 1, :],
                                     ACT.Tanh, scale=0.5).then_inc(g_exp, 1)
                for i in range(3):
                    act.wait_ge(cv_pre, 3 * l + i + 1)
                    tmp = (A_low, M_lvl, W_lvl)[i].rearrange("p t h n -> p (t h n)")
                    nc.scalar.activation(tmp, cv[:, 4 * i:4 * i + 4, :].rearrange("p c n -> p (c n)"), ACT.Tanh,
                                         scale=0.5).then_inc(cv_th, 1)
                for i in range(4):
                    act.wait_ge(cv_ready, 3 * l + i // 2 + 1)
                    tmp = (DTm, Dcl)[i // 2].rearrange("p t h n -> p (t h n)")[:, (i % 2) * 512:(i % 2 + 1) * 512]
                    nc.scalar.activation(tmp, cv[:, 2 * i:2 * i + 2, :].rearrange("p c n -> p (c n)"),
                                         ACT.Square).then_inc(cv_sq, 1)
                for i in range(4):
                    act.wait_ge(cv_ss, 4 * l + i + 1)
                    r_ = rq[i].rearrange("p t h n -> p (t h n)")[:, 0:512]
                    last = nc.scalar.activation(r_, B[4 + i][:, :], ACT.Ln, bias=eps_col[:, 1:2])
                link(last)
                for i in range(4):
                    r_ = rq[i].rearrange("p t h n -> p (t h n)")[:, 0:512]
                    nc.scalar.activation(r_, r_, ACT.Exp, scale=-0.5).then_inc(cv_rs, 1)
                act.wait_ge(gc_sb, l + 1)
                nc.scalar.activation(bexp, gcum, ACT.Exp).then_inc(g_bexp, 1)
                for t in range(NT):
                    act.wait_ge(dec_in, NT * l + t + 1)
                    nc.scalar.activation(e_row[:, t], B[2 + t][:, :].rearrange("p (h n) -> p h n", h=GH),
                                         ACT.Exp).then_inc(dec_ready, 1)
                    nc.scalar.activation(dec[:, t], Dcl[:, t], ACT.Exp, scale=-1.0).then_inc(dec_ready, 1)
                    nc.scalar.activation(decT[:, t], DTm[:, t], ACT.Exp).then_inc(dec_ready, 1)
                for t in range(NT):
                    act.wait_ge(kv_ps, 4 * l + t + 1)
                    nc.scalar.activation(k_tok[:, t], B[4 + t][:, :].rearrange("p (h n) -> p h n", h=GH),
                                         ACT.Copy).then_inc(kv_evac, 1)
                for k in range(6):
                    for t in range(NT):
                        n = (6 * l + k) * NT + t
                        act.wait_ge(w_ps, n + 1)
                        nc.scalar.activation(W_lvl[:, t], B[t][:, :].rearrange("p (h n) -> p h n", h=GH),
                                             ACT.Copy).then_inc(w_evac, 1)
                for t in range(NT):
                    act.wait_ge(uw_ps, NT * l + t + 1)
                    nc.scalar.activation(wT[:, t], B[t][:, :].rearrange("p (h n) -> p h n", h=GH),
                                         ACT.Copy).then_inc(w_done, 1)
                for c in range(NCHUNK):
                    rows_ = slice((c % 2) * GL, (c % 2 + 1) * GL)
                    act.wait_ge(o_ps, NCHUNK * l + c + 1)
                    nc.scalar.activation(o_tok[rows_, c // 2], B[5 + c % 2][rows_, :].rearrange("p (h n) -> p h n", h=GH),
                                         ACT.Copy).then_inc(o_evac, 1)
                nc.scalar.activation(gdiag.rearrange("p t h n -> p (t h n)"),
                                     z_tok[:, :, :].rearrange("p t n -> p (t n)"), ACT.Tanh,
                                     scale=0.5).then_inc(o_evac, 1)
                act.wait_ge(og_ss, l + 1)
                link(nc.scalar.activation(gate_z, gate_z, ACT.Ln, scale=1.0 / GD, bias=eps_col[:, 0:1]))
                nc.scalar.activation(gate_z, gate_z, ACT.Exp, scale=-0.5).then_inc(og_rs, 1)
                for t in range(NT):
                    act.wait_ge(og_ps, NT * l + t + 1)
                    nc.scalar.activation(g_oT[:, :, t * P:(t + 1) * P], B[4 + t][:, :].rearrange("p (k n) -> p k n", n=P),
                                         ACT.Copy).then_inc(og_T, 1)
                for b in range(4):
                    act.wait_ge(mg_ps, 4 * l + b + 1)
                    nc.scalar.activation(hT[:, 2 * b:2 * b + 2, :], B[4 + b][:, :].rearrange("p (c n) -> p c n", n=SEQ),
                                         ACT.Copy).then_inc(mg_T, 1)
                for k in range(KD):
                    last = nc.scalar.activation(memnT[:, k, :], memT[:, k, :], ACT.Copy,
                                                scale=gain_mem[:, l * KD + k:l * KD + k + 1])
                last.then_inc(memn_ready, 1)
                for b in range(2):
                    act.wait_ge(xk_ps, 6 * l + b + 1)
                    nc.scalar.activation(xkT[:, 2 * b:2 * b + 2, :], B[2 + b][:, :].rearrange("p (c n) -> p c n", n=SEQ),
                                         ACT.Copy).then_inc(xk_sb, 1)
                for b in range(2):
                    act.wait_ge(xk_ps, 6 * l + 2 + b + 1)
                    nc.scalar.activation(x_v[:, b, :], B[b][:, :], ACT.Copy).then_inc(xk_sb, 1)
                n = 2 + 3 * l
                act.wait_ge(wo_used, 4 * (l + 1))
                sum_squares(x[:, :, :], n)
                evac_norm(n, hT[:, :, :], gain_xa, l * KD, hT_ready)
                for b in range(2):
                    act.wait_ge(xk_ps, 6 * l + 4 + b + 1)
                    nc.scalar.activation(xqT[:, 2 * b:2 * b + 2, :], B[b][:, :].rearrange("p (c n) -> p c n", n=SEQ),
                                         ACT.Copy).then_inc(xk_sb, 1)

                def xa_exp(h):
                    n_ = XH * l + h
                    act.wait_ge(xs_neg, n_ + 1)
                    if n_ >= 2:
                        act.wait_ge(xs_tr, n_ - 1)
                    for t in range(NT):
                        o = 2 * (h % 2) + t
                        last = nc.scalar.activation(xp[h % 2][:, t, :], B[2 + h % 2][:, t * SEQ:(t + 1) * SEQ], ACT.Exp,
                                                    bias=nm[:, o:o + 1], scale=XD ** -0.5, accum_out=rs[:, o:o + 1])
                    last.then_inc(xs_exp, 1)

                def xa_pT(h):
                    n_ = XH * l + h
                    act.wait_ge(xs_tr, n_ + 1)
                    if n_ >= 2:
                        act.wait_ge(xs_o, n_ - 1)
                    nc.scalar.activation(xpT[h % 2], B[4 + h % 2][:, :].rearrange("p (c n) -> p c n", n=SEQ),
                                         ACT.Copy).then_inc(xs_pT, 1)

                def xa_oT(h):
                    act.wait_ge(xs_o, XH * l + h + 1)
                    nc.scalar.activation(x_oT[:, h, :], B[6 + h % 2][:, 0:SEQ], ACT.Copy).then_inc(xs_oT, 1)

                for s in range(XH + 2):
                    if s < XH:
                        xa_exp(s)
                    if 1 <= s <= XH:
                        xa_pT(s - 1)
                    if s >= 2:
                        xa_oT(s - 2)
                n = 3 + 3 * l
                act.wait_ge(xo_used, 4 * (l + 1))
                sum_squares(x[:, :, :], n)
                evac_norm(n, hT[:, :, :], gain_ffn, l * KD, hT_ready)
                if l % 2 == 1:
                    act.wait_ge(rl_d, l // 2 + 1)
                    nc.scalar.activation(r_w[:, :, 1:2], r_w[:, :, 0:1], ACT.Exp).then_inc(rl_e, 1)
                base = acts_before(l)
                if l % 2 == 0:
                    def tail(c, t):
                        act.wait_ge(act_tr, c * NT + (base + t + 1))
                        nc.scalar.activation(f_actT[:, :, t * P:(t + 1) * P],
                                             B[2 + t][:, 0:2 * P].rearrange("p (k n) -> p k n", n=P),
                                             ACT.Copy).then_inc(actT_ready, 1)

                    def chunk(c, s):
                        first = isinstance(c, int) and c == 0 and l == 0
                        for t in range(NT):
                            act.wait_ge(gu_ps, c * NT + (base + t + 1))
                            if not first:
                                act.wait_ge(gu_a, c * NT + (base + t + 1 - NT))
                            nc.scalar.activation(f_th[t], B[t][:, 0:FC], ACT.Tanh, scale=0.5).then_inc(gu_th, 1)
                            if t == 0 and not (isinstance(c, int) and c == 0):
                                tail(c - 1, 1)
                        tail(c, 0)

                    chunks_of_expert(act, chunk)
                    tail(NCH - 1, 1)
                    act.wait_ge(y_added, l // 2 + 1)
                else:
                    act.dma_start(gain_bc, norm_ffn_d[l:l + 1, :].to_broadcast([P, D])).then_inc(gain_in, 16)

                    def take_he(k):
                        act.wait_ge(he_ps, k)
                        for b in range(2):
                            last = nc.scalar.activation(h_e[:, 4 * b:4 * b + 4, :],
                                                        B[6 + b][:, :].rearrange("p (k n) -> p k n", n=P), ACT.Copy)
                        last.then_inc(he_ready, 1)

                    def one_pass(p):
                        ab_, kb = base + p * NE * NCH, p * (NE + 1)
                        take_he(kb + 1)
                        with act.Fori(0, NE) as e:
                            def tail(c):
                                act.wait_ge(act_tr, e * NCH + c + (ab_ + 1))
                                nc.scalar.activation(f_actT[:, :, 0:P], B[3][:, 0:2 * P].rearrange("p (k n) -> p k n", n=P),
                                                     ACT.Copy).then_inc(actT_ready, 1)

                            def chunk(c, s):
                                if isinstance(c, int) and c == 0:
                                    act.wait_ge(gu_ps, e * NCH + (ab_ + 1))
                                else:
                                    tail(c - 1)
                                    act.wait_ge(gu_ps, e * NCH + c + (ab_ + 1))
                                act.wait_ge(gu_a, e * NCH + c + ab_)
                                nc.scalar.activation(f_th[0], B[s][:, 0:FC], ACT.Tanh, scale=0.5).then_inc(gu_th, 1)
                                if isinstance(c, int) and c == 0:
                                    act.wait_ge(sm_ps, e + (NE * p + 1))
                                    nc.scalar.activation(scatter_m, B[3][:, 2 * P:4 * P], ACT.Copy).then_inc(sm_ready, 1)
                                if isinstance(c, int) and c == NCH - 1:
                                    take_he(e + (kb + 2))
                            chunks_of_expert(act, chunk)
                            tail(NCH - 1)
                            act.wait_ge(chunk_used, e * NCH + (NCH * (experts_before(l) + p * NE) + NCH))
                            act.wait_ge(sc_ps, 4 * e + (4 * kb + 4))
                            for b in range(2):
                                last = nc.scalar.activation(y_e[:, b * 512:(b + 1) * 512], B[4 + b][:, :], ACT.Copy)
                            last.then_inc(ye_ready, 1)
                        act.wait_ge(sc_used, 4 * (NE + 1) * (p + 1))
                    moe_passes(act, one_pass)
            act.dma_start(gain_out, norm_final_d.rearrange("(a n) -> a n", a=1).to_broadcast([P, D])).then_inc(fin_in, 16)
            sum_squares(x[:, :, :], NNORM)

        @block.vector
        def _(dve):
            V = nc.vector
            chain = [0]

            def link(ins):
                chain[0] += 1
                ins.then_inc(dve_chain, 1)
                dve.wait_ge(dve_chain, chain[0])

            def normalise(src, dst, n):
                dve.wait_ge(norm_ss, n + 1)
                for t in range(NT):
                    V.tensor_scalar(dst[:, t, :], src[:, t, :], rstd[:, t:t + 1], None, ALU.mult).then_inc(norm_h, 1)

            def reduce_angle(a, tmp):
                link(V.tensor_scalar(tmp, a, 1.0 / TWO_PI, MAGIC, ALU.mult, ALU.add))
                link(V.tensor_scalar(tmp, tmp, -MAGIC, None, ALU.add))
                link(V.scalar_tensor_tensor(a, tmp, -C1, a, ALU.mult, ALU.add))
                link(V.scalar_tensor_tensor(a, tmp, -C2, a, ALU.mult, ALU.add))
                return V.tensor_scalar(a, a, PI_IN, -PI_IN, ALU.min, ALU.max)

            dve.wait_ge(mem_in, 16)
            normalise(h_tok, h_tok, 0)
            c_ = [s5c[:, i, :] for i in range(14)]
            dve.wait_ge(par_ready, 1)
            dve.wait_ge(s5_dt, 1)
            V.tensor_tensor(c_[5], c_[4], p_are, ALU.mult)
            link(V.tensor_tensor(THR, c_[4], p_aim, ALU.mult))
            reduce_angle(THR, c_[8]).then_inc(s5_ang, 1)
            dve.wait_ge(pos_in, 16)
            link(V.tensor_copy(pos_f[:, :], pos_i[:, :]))
            dve.wait_ge(consts, 2)
            for t in range(NT):
                link(V.tensor_scalar(cosr[:, t, :], inv_freq[:, :], pos_f[:, t:t + 1], None, ALU.mult))
            reduce_angle(cosr[:, :, :], sinr[:, :, :]).then_inc(rot_ang, 1)
            dve.wait_ge(s5_sin, 1)
            link(V.tensor_tensor(c_[7], c_[7], c_[7], ALU.mult))
            link(V.tensor_scalar(c_[7], c_[7], -2.0, 1.0, ALU.mult, ALU.add))
            link(V.tensor_tensor(c_[7], c_[7], DEC, ALU.mult))
            link(V.tensor_scalar(c_[7], c_[7], -1.0, None, ALU.add))
            link(V.tensor_tensor(c_[6], c_[6], DEC, ALU.mult))
            V.tensor_tensor(c_[8], p_are, p_are, ALU.mult)
            link(V.tensor_tensor(c_[9], p_aim, p_aim, ALU.mult))
            link(V.tensor_tensor(c_[8], c_[8], c_[9], ALU.add))
            link(V.reciprocal(c_[8], c_[8]))
            V.tensor_tensor(c_[9], c_[7], p_are, ALU.mult)
            V.tensor_tensor(c_[10], c_[6], p_aim, ALU.mult)
            V.tensor_tensor(c_[11], c_[6], p_are, ALU.mult)
            link(V.tensor_tensor(c_[12], c_[7], p_aim, ALU.mult))
            V.tensor_tensor(c_[9], c_[9], c_[10], ALU.add)
            link(V.tensor_tensor(c_[11], c_[11], c_[12], ALU.subtract))
            V.tensor_tensor(BCR, c_[9], c_[8], ALU.mult)
            V.tensor_tensor(BCI, c_[11], c_[8], ALU.mult).then_inc(s5_const, 1)
            dve.wait_ge(rot_sin, 1)
            link(V.tensor_tensor(cosr[:, :, :], cosr[:, :, :], cosr[:, :, :], ALU.mult))
            link(V.tensor_scalar(cosr[:, :, :], cosr[:, :, :], -2.0, 1.0, ALU.mult, ALU.add))
            dve.wait_ge(s5_const, 1)

            for l in range(DEPTH):
                if l == 0:
                    dve.wait_ge(x_in, 16)
                    dve.wait_ge(norm_ps, 4)
                normalise(x[:, :, :], h_tok, 1 + 3 * l)
                dve.wait_ge(bc_nat_in, 64 * (l + 1))
                cr = BCR[:, l * NS5:(l + 1) * NS5].unsqueeze(2).to_broadcast([P, NS5, 16])
                ci = BCI[:, l * NS5:(l + 1) * NS5].unsqueeze(2).to_broadcast([P, NS5, 16])
                tb = [wk5[i][:, 0, :].rearrange("p (t n) -> p t n", n=16) for i in range(4)]
                V.tensor_tensor(tb[0], b_nat[:, 0], cr, ALU.mult)
                V.tensor_tensor(tb[1], b_nat[:, 1], ci, ALU.mult)
                V.tensor_tensor(tb[2], b_nat[:, 0], ci, ALU.mult)
                link(V.tensor_tensor(tb[3], b_nat[:, 1], cr, ALU.mult))
                link(V.tensor_tensor(b_bar[:, 0], tb[0], tb[1], ALU.subtract))
                V.tensor_tensor(b_bar[:, 1], tb[2], tb[3], ALU.add).then_inc(b_bar_ready, 1)
                for f in range(4):
                    c, t = f // 2, f % 2
                    dve.wait_ge(fill_ready, 20 * l + f + 1)
                    src = B[t][:, :].rearrange("p (h c n) -> p h c n", c=2, n=MD // 2)
                    dst = qk[:, c, t, :].rearrange("p (h c n) -> p h c n", c=2, n=MD // 2)
                    cs = cosr[:, t, :].unsqueeze(1).to_broadcast([P, MH, MD // 2])
                    sn = sinr[:, t, :].unsqueeze(1).to_broadcast([P, MH, MD // 2])
                    tmp = wk5[3 + f % 2].rearrange("p a b -> p (a b)").rearrange("p (h c n) -> p h c n", c=2, n=MD // 2)
                    for i in range(2):
                        V.tensor_tensor(dst[:, :, i, :], src[:, :, i, :], cs, ALU.mult)
                    V.tensor_tensor(tmp[:, :, 0, :], src[:, :, 1, :], sn, ALU.mult)
                    link(V.tensor_tensor(tmp[:, :, 1, :], src[:, :, 0, :], sn, ALU.mult))
                    V.tensor_tensor(dst[:, :, 0, :], dst[:, :, 0, :], tmp[:, :, 0, :], ALU.subtract)
                    V.tensor_tensor(dst[:, :, 1, :], dst[:, :, 1, :], tmp[:, :, 1, :], ALU.add).then_inc(rope_done, 1)
                dve.wait_ge(rope_done, 4 * (l + 1))
                for i in range(NS5):
                    q, n = i // NQ, NS5 * l + i
                    T = tab[q % 2][:, i % NQ]
                    if i % NQ == 0:
                        dve.wait_ge(tab_sin, NQ * l + q + 1)
                        cosn = tab[q % 2][:, :, 0, :]
                        link(V.tensor_scalar(cosn, cosn, -2.0, 1.0, ALU.mult, ALU.add))
                    dve.wait_ge(bu_ready, n + 1)
                    bu = B[2 + n % 2][:, :].rearrange("p (c n) -> p c n", n=SEQ)
                    cs2 = T[:, 0, :].unsqueeze(1).to_broadcast([P, 2, SEQ])
                    sn = T[:, 1, :]
                    m1, m2, gin = wk5[0], wk5[1], wk5[2]
                    if n >= 1:
                        dve.wait_ge(h_rot, n)
                    V.tensor_tensor(m1, bu, cs2, ALU.mult)
                    V.tensor_tensor(m2[:, 0, :], bu[:, 1, :], sn, ALU.mult)
                    V.tensor_tensor(m2[:, 1, :], bu[:, 0, :], sn, ALU.mult).then_inc(bu_read, 1)
                    dve.wait_ge(bu_read, n + 1)
                    V.tensor_tensor(gin[:, 0, :], m1[:, 0, :], m2[:, 0, :], ALU.add)
                    link(V.tensor_tensor(gin[:, 1, :], m1[:, 1, :], m2[:, 1, :], ALU.subtract))
                    dc = DEC[:, NS5 * l + i:NS5 * l + i + 1].to_broadcast([P, SEQ])
                    for c in range(2):
                        last = V.tensor_tensor_scan(m1[:, c, :], dc, gin[:, c, :], 0.0, ALU.mult, ALU.add)
                    link(last)
                    hr = wk5[3 + n % 2]
                    if n >= 2:
                        dve.wait_ge(y_read, n - 1)
                    V.tensor_tensor(m2, m1, cs2, ALU.mult)
                    V.tensor_tensor(gin[:, 0, :], m1[:, 1, :], sn, ALU.mult)
                    link(V.tensor_tensor(gin[:, 1, :], m1[:, 0, :], sn, ALU.mult))
                    V.tensor_tensor(hr[:, 0, :], m2[:, 0, :], gin[:, 0, :], ALU.subtract)
                    V.tensor_tensor(hr[:, 1, :], m2[:, 1, :], gin[:, 1, :], ALU.add).then_inc(h_rot, 1)
                    if i % NQ == 0:
                        dve.wait_ge(h_rot, n + 1)
                    if i % NQ == NQ - 1:
                        dve.wait_ge(h_rot, n + 1)
                        dve.wait_ge(y_read, n + 1)
                        link(V.scalar_tensor_tensor(y5[:, q, :], uT[:, q, :], p_d[:, l * NQ + q:l * NQ + q + 1],
                                                    B[4 + q % 2][:, 0:SEQ], ALU.mult, ALU.add))
                        link(V.tensor_tensor(y5b[:, q, :], y5[:, q, :], y5[:, q, :], ALU.mult))
                        link(V.tensor_scalar(y5b[:, q, :], y5b[:, q, :], 0.044715, 1.0, ALU.mult, ALU.add))
                        V.tensor_tensor(y5b[:, q, :], y5b[:, q, :], y5[:, q, :], ALU.mult).then_inc(gel_in, 1)
                dve.wait_ge(gel_t, NQ * (l + 1))
                yflat = yT[:, :, :].rearrange("p q n -> p (q n)")
                link(V.scalar_tensor_tensor(yflat, y5b.rearrange("p q n -> p (q n)"), 1.0,
                                            y5.rearrange("p q n -> p (q n)"), ALU.add, ALU.mult))
                V.tensor_scalar(yflat, yflat, 0.5, None, ALU.mult).then_inc(y_ready, 1)
                link(V.memset(raw[:, :, 0:3], 0.0))
                def moba_max(h):
                    n = MH * l + h
                    p, o = mp_[h % 2], 2 * (h % 2)
                    dve.wait_ge(ms_ready, n + 1)
                    if n >= 2:
                        dve.wait_ge(ms_tr, n - 1)
                    link(V.tensor_tensor(p, B[2 + h % 2][:, 0:3 * P], causal[:, :], ALU.add))
                    V.tensor_reduce(mx[:, o:o + 1], p[:, 0:P], AX.X, ALU.max)
                    link(V.tensor_reduce(mx[:, o + 1:o + 2], p[:, P:3 * P], AX.X, ALU.max))
                    V.tensor_scalar(nm[:, o:o + 2], mx[:, o:o + 2], -MD ** -0.5, None, ALU.mult).then_inc(ms_neg, 1)

                def moba_norm(h):
                    n = MH * l + h
                    p, o = mp_[h % 2], 2 * (h % 2)
                    dve.wait_ge(ms_exp, n + 1)
                    link(V.reciprocal(rs[:, o:o + 2], rs[:, o:o + 2]))
                    V.tensor_scalar(p[:, 0:P], p[:, 0:P], rs[:, o:o + 1], None, ALU.mult)
                    V.tensor_scalar(p[:, P:3 * P], p[:, P:3 * P], rs[:, o + 1:o + 2], None, ALU.mult).then_inc(ms_norm, 1)

                if l == 0:
                    dve.wait_ge(consts, 3)
                moba_max(0)
                for h in range(MH):
                    if h + 1 < MH:
                        moba_max(h + 1)
                    moba_norm(h)
                for i in range(4):
                    n_, t = i // 2, i % 2
                    dve.wait_ge(up_ps, 8 * l + i + 1)
                    V.scalar_tensor_tensor(merged[:, t, n_ * 512:(n_ + 1) * 512], gates[:, t, n_ * 512:(n_ + 1) * 512],
                                           1.0, B[i % 2][:, :], ALU.add, ALU.mult).then_inc(up_used, 1)
                for i in range(4):
                    n_, t = i // 2, i % 2
                    dve.wait_ge(glu_th, 4 * l + i + 1)
                    V.scalar_tensor_tensor(glu_y[t], glu_t[t], 1.0, B[2 * t][:, :], ALU.add, ALU.mult).then_inc(glu_used, 1)
                    dve.wait_ge(glu_used, 4 * l + i + 1)
                    g = gates[:, t, D + n_ * 512:D + (n_ + 1) * 512]
                    m = merged[:, t, n_ * 512:(n_ + 1) * 512]
                    link(V.scalar_tensor_tensor(gl_tmp[t], g, 1.0, glu_y[t], ALU.add, ALU.mult))
                    link(V.scalar_tensor_tensor(m, gl_tmp[t], 0.5, m, ALU.mult, ALU.add))
                ab4 = ab.rearrange("p (t c h) -> p t c h", t=NT, c=2)
                z4 = gate_z.rearrange("p (t h) -> p t h", t=NT)
                dve.wait_ge(ab_sb, l + 1)
                for t in range(NT):
                    last = V.tensor_tensor(z4[:, t, :], ab4[:, t, 0, :], small_bc[:, l, 1, :], ALU.add)
                link(last)
                V.scalar_tensor_tensor(gate_e, gate_z, -1.0, gate_z, ALU.mult, ALU.max).then_inc(g_z, 1)
                for w in range(1, 4):
                    for j in range(12):
                        if w == 1:
                            dve.wait_ge(cv_tap, 12 * l + j + 1)
                        k = 48 * l + 12 * w + j
                        last = V.scalar_tensor_tensor(cv[:, j, :], raw[:, j, w:w + SEQ], p_conv[:, k:k + 1],
                                                      cv[:, j, :], ALU.mult, ALU.add)
                        if w == 3 and j % 4 == 3:
                            last.then_inc(cv_pre, 1)
                    if w < 3:
                        link(last)
                dve.wait_ge(g_ln, l + 1)
                link(V.scalar_tensor_tensor(gate_z, gate_z, 0.0, gate_e, ALU.max, ALU.add))
                for t in range(NT):
                    last = V.scalar_tensor_tensor(gstep.rearrange("p (t h) -> p t h", t=NT)[:, t, :], z4[:, t, :],
                                                  -1.0, ealog, ALU.mult, ALU.mult)
                last.then_inc(g_step, 1)
                dve.wait_ge(g_exp, l + 1)
                link(V.tensor_scalar(beta, beta, 0.5, 0.5, ALU.mult, ALU.add))
                for i in range(3):
                    dve.wait_ge(cv_th, 3 * l + i + 1)
                    tmp = (A_low, M_lvl, W_lvl)[i].rearrange("p t h n -> p (t h n)")
                    c4 = cv[:, 4 * i:4 * i + 4, :].rearrange("p c n -> p (c n)")
                    V.scalar_tensor_tensor(c4, tmp, 1.0, c4, ALU.add, ALU.mult).then_inc(cv_ready, 1)
                for i in range(4):
                    dve.wait_ge(cv_rs, 4 * l + i + 1)
                    r_ = rq[i].rearrange("p t h n -> p (t h n)")[:, 0:512]
                    c2 = cv[:, 2 * i:2 * i + 2, :].rearrange("p c n -> p (c n)")
                    V.scalar_tensor_tensor(c2, r_, GD ** -0.5 if i < 2 else 1.0, c2, ALU.mult, ALU.mult).then_inc(kq_ready, 1)
                dve.wait_ge(gc_ps, l + 1)
                V.tensor_copy(gcum, B[1][:, 0:NT * GH]).then_inc(gc_sb, 1)
                dve.wait_ge(gc_sb, l + 1)
                gc3 = gcum.rearrange("p (t h) -> p t h", t=NT)
                be3 = beta.rearrange("p (t h) -> p t h", t=NT)
                bx3 = bexp.rearrange("p (t h) -> p t h", t=NT)
                kd3 = kds.rearrange("p (t h) -> p t h", t=NT)
                for t in range(NT):
                    V.tensor_tensor(gdiag[:, t], ident[:, :].unsqueeze(1).to_broadcast([P, GH, P]),
                                    gc3[:, t, :].unsqueeze(2).to_broadcast([P, GH, P]), ALU.mult).then_inc(g_diag, 1)
                for t in range(NT):
                    dve.wait_ge(row_ps, NT * l + t + 1)
                    link(V.tensor_tensor(DTm[:, t], B[2 + t][:, :].rearrange("p (h n) -> p h n", h=GH),
                                         gc3[:, t, :].unsqueeze(2).to_broadcast([P, GH, P]), ALU.subtract))
                    link(V.tensor_scalar(Dcl[:, t], DTm[:, t], 0.0, None, ALU.max))
                    V.tensor_scalar(DTm[:, t], DTm[:, t], 0.0, None, ALU.min).then_inc(dec_in, 1)
                dve.wait_ge(g_bexp, l + 1)
                link(V.tensor_tensor(bexp, bexp, beta, ALU.mult))
                for t in range(NT):
                    dve.wait_ge(dec_ready, 3 * NT * l + 3 * t + 3)
                    link(V.tensor_tensor(decT[:, t], decT[:, t], cum_mask[:, :].unsqueeze(1).to_broadcast([P, GH, P]),
                                         ALU.mult))
                    link(V.tensor_tensor(kd3[:, t, :], decT[:, t, :, GL - 1], decT[:, t, :, 2 * GL - 1], ALU.add))

                def per_token(s3, t):
                    return s3[:, t, :].unsqueeze(2).to_broadcast([P, GH, GD])

                for t in range(NT):
                    dve.wait_ge(kv_evac, NT * l + t + 1)
                    V.tensor_tensor(kbeg[:, t], k_tok[:, t], per_token(bx3, t), ALU.mult)
                    V.tensor_tensor(kdec[:, t], k_tok[:, t], per_token(kd3, t), ALU.mult)
                    dve.wait_ge(kv_ps, 4 * l + 2 + t + 1)
                    V.scalar_tensor_tensor(vbeta[:, t], B[6 + t][:, :].rearrange("p (h n) -> p h n", h=GH), 0.5,
                                           per_token(be3, t), ALU.mult, ALU.mult).then_inc(uw_in, 1)
                for t in range(NT):
                    dve.wait_ge(kk_ps, 2 * NT * l + t + 1)
                    link(V.tensor_tensor(A_low[:, t], B[4 + t][:, :].rearrange("p (h n) -> p h n", h=GH), dec[:, t], ALU.mult))
                    V.tensor_tensor(A_low[:, t], A_low[:, t], per_token(be3, t), ALU.mult).then_inc(a_ready, 1)
                for t in range(NT):
                    dve.wait_ge(kk_ps, 2 * NT * l + NT + t + 1)
                    V.tensor_tensor(qkT[:, t], B[6 + t][:, :].rearrange("p (h n) -> p h n", h=GH), decT[:, t], ALU.mult)
                    qc = cv[:, 0:4, t * P:(t + 1) * P]
                    V.tensor_tensor(qc, qc, e_row[:, t], ALU.mult).then_inc(qd_ready, 1)
                for k in range(6):
                    for t in range(NT):
                        n = (6 * l + k) * NT + t
                        if k == 0:
                            dve.wait_ge(xz_init, 2 * NT * l + 2 * t + 2)
                        dve.wait_ge(xz_ps, n + 1)
                        V.tensor_tensor(Xi[:, t], Xi[:, t], B[2 + t][:, :].rearrange("p (h n) -> p h n", h=GH), ALU.subtract)
                        V.tensor_tensor(Zi[:, t], Zi[:, t], B[4 + t][:, :].rearrange("p (h n) -> p h n", h=GH),
                                        ALU.subtract).then_inc(xz_ready, 1)
                    for t in range(NT):
                        dve.wait_ge(xz_ready, (6 * l + k) * NT + t + 1)
                V.memset(state[:, 0], 0.0).then_inc(s_init, 1)
                for t in range(NT):
                    dve.wait_ge(uw_ps, NT * l + t + 1)
                    V.tensor_copy(u_tok[:, t], B[2 + t][:, :].rearrange("p (h n) -> p h n", h=GH)).then_inc(u_done, 1)
                dve.wait_ge(u_done, NT * (l + 1))
                for c in range(NCHUNK):
                    n, t, off = NCHUNK * l + c, c // 2, (c % 2) * GL
                    rows_ = slice(off, off + GL)
                    dve.wait_ge(vn_ps, n + 1)
                    V.tensor_tensor(vn[rows_], u_tok[rows_, t], B[4][rows_, :].rearrange("p (h n) -> p h n", h=GH),
                                    ALU.subtract).then_inc(vn_ready, 1)
                    if c < NCHUNK - 1:
                        new, old = state[:, (c + 1) % 2], state[:, c % 2]
                        eg = e_row[:, t, :, off + GL - 1].unsqueeze(2).to_broadcast([P, GH, GD])
                        if c == 0:
                            dve.wait_ge(s_init, l + 1)
                        dve.wait_ge(s_ready, n - l) if c > 0 else None
                        link(V.tensor_tensor(new, old, eg, ALU.mult))
                        dve.wait_ge(su_ps, (NCHUNK - 1) * l + c + 1)
                        V.tensor_tensor(new, new, B[7][:, :].rearrange("p (h n) -> p h n", h=GH), ALU.add).then_inc(s_ready, 1)
                dve.wait_ge(o_evac, (NCHUNK + 1) * (l + 1))
                o_all = o_tok.rearrange("p t h n -> p (t h) n")
                sq = DTm.rearrange("p t h n -> p (t h) n")
                link(V.tensor_tensor(sq, o_all, o_all, ALU.mult))
                V.tensor_reduce(gate_z, sq, AX.X, ALU.add).then_inc(og_ss, 1)
                dve.wait_ge(og_rs, l + 1)
                link(V.tensor_tensor(o_all, o_all, gate_z.unsqueeze(2).to_broadcast([P, NT * GH, GD]), ALU.mult))
                link(V.tensor_tensor(o_all, o_all, gnorm_bc[:, l, :].unsqueeze(1).to_broadcast([P, NT * GH, GD]), ALU.mult))
                zf = z_tok[:, :, :].rearrange("p t n -> p (t n)")
                gz = gdiag.rearrange("p t h n -> p (t h n)")
                of = o_tok.rearrange("p t h n -> p (t h n)")
                link(V.scalar_tensor_tensor(gz, gz, 1.0, zf, ALU.add, ALU.mult))
                V.scalar_tensor_tensor(of, gz, 0.5, of, ALU.mult, ALU.mult).then_inc(og_ready, 1)
                for i in range(4):
                    n_, t = i // 2, i % 2
                    dve.wait_ge(up_ps, 8 * l + 4 + i + 1)
                    tmp = (DTm if t == 0 else Dcl).rearrange("p t h n -> p (t h n)")[:, 0:512]
                    V.scalar_tensor_tensor(tmp, gates[:, t, 2 * D + n_ * 512:2 * D + (n_ + 1) * 512], 1.0, B[i % 2][:, :],
                                           ALU.add, ALU.mult).then_inc(up_used, 1)
                    dve.wait_ge(up_used, 8 * l + 4 + i + 1)
                    m = merged[:, t, n_ * 512:(n_ + 1) * 512]
                    last = V.tensor_tensor(m, m, tmp, ALU.add)
                last.then_inc(mg_ready, 1)
                for i in range(4):
                    n_, t = i // 2, i % 2
                    dve.wait_ge(wo_ps, 4 * l + i + 1)
                    xs = x[:, t, n_ * 512:(n_ + 1) * 512]
                    V.scalar_tensor_tensor(xs, B[i % 2][:, :], 0.5, xs, ALU.mult, ALU.add).then_inc(wo_used, 1)
                normalise(x[:, :, :], h_tok, 2 + 3 * l)
                for h in range(XH):
                    n_, o = XH * l + h, 2 * (h % 2)
                    dve.wait_ge(xs_ps, n_ + 1)
                    if n_ >= 2:
                        dve.wait_ge(xs_exp, n_ - 1)
                    link(V.tensor_reduce(mx[:, o:o + 2], B[2 + h % 2][:, :].rearrange("p (t n) -> p t n", t=NT), AX.X, ALU.max))
                    V.tensor_scalar(nm[:, o:o + 2], mx[:, o:o + 2], -XD ** -0.5, None, ALU.mult).then_inc(xs_neg, 1)
                    dve.wait_ge(xs_exp, n_ + 1)
                    link(V.reciprocal(rs[:, o:o + 2], rs[:, o:o + 2]))
                    for t in range(NT):
                        last = V.tensor_scalar(xp[h % 2][:, t, :], xp[h % 2][:, t, :], rs[:, o + t:o + t + 1], None, ALU.mult)
                    last.then_inc(xs_norm, 1)
                for i in range(4):
                    n_, t = i // 2, i % 2
                    dve.wait_ge(xo_ps, 4 * l + i + 1)
                    xs = x[:, t, n_ * 512:(n_ + 1) * 512]
                    V.tensor_tensor(xs, xs, B[i % 2][:, :], ALU.add).then_inc(xo_used, 1)
                normalise(x[:, :, :], h_tok, 3 + 3 * l)
                if l % 2 == 1:
                    dve.wait_ge(rl_ps, l // 2 + 1)
                    link(V.tensor_copy(r_log, B[0][:, 0:NT * NE].rearrange("p (t e) -> p t e", t=NT)))
                    for t in range(NT):
                        link(V.max(r_max[:, t, :], r_log[:, t, :]))
                        link(V.max_index(r_idx[:, t, :], r_max[:, t, :], r_log[:, t, :]))
                    link(V.tensor_copy(r_idf, r_idx[:, :, :]))
                    V.tensor_tensor(r_w[:, :, 0:1], r_max[:, :, 1:2], r_max[:, :, 0:1], ALU.subtract).then_inc(rl_d, 1)
                    dve.wait_ge(rl_e, l // 2 + 1)
                    link(V.tensor_scalar(r_w[:, :, 2:3], r_w[:, :, 1:2], 1.0, None, ALU.add))
                    link(V.reciprocal(r_w[:, :, 2:3], r_w[:, :, 2:3]))
                    link(V.tensor_tensor(r_w[:, :, 3:4], r_w[:, :, 1:2], r_w[:, :, 2:3], ALU.mult))
                    for t in range(NT):
                        for i in range(2):
                            last = V.tensor_scalar(r_eq[:, i, t, :], idx8[:, :], r_idf[:, t, i:i + 1],
                                                   r_w[:, t, 2 + i:3 + i], ALU.is_equal, ALU.mult)
                    link(last)
                    cols = slice(0, NE)
                    V.memset(comb[:, :, NE:NE + 1], 0.0)
                    V.memset(chosen[:, :, NE:NE + 1], 0.0)
                    V.memset(place[:, :, NE:NE + 1], 0.0)
                    link(V.tensor_tensor(comb[:, :, cols], r_eq[:, 0], r_eq[:, 1], ALU.add))
                    for t in range(NT):
                        for i in range(2):
                            last = V.tensor_scalar(r_eq[:, i, t, :], idx8[:, :], r_idf[:, t, i:i + 1], None, ALU.is_equal)
                    link(last)
                    V.tensor_scalar(comb[:, :, cols], comb[:, :, cols], 0.5, None, ALU.mult)
                    V.tensor_tensor(chosen[:, :, cols], r_eq[:, 0], r_eq[:, 1], ALU.add).then_inc(comb_ready, 1)
                    dve.wait_ge(gain_in, 16)
                    dve.wait_ge(norm_ps, 4 * (4 + 3 * l))
                    for t in range(NT):
                        V.tensor_tensor(h_tok[:, t, :], h_tok[:, t, :], gain_bc, ALU.mult).then_inc(h_gain, 1)
                    dve.wait_ge(place_ps, 1)
                    V.tensor_copy(place[:, :, cols], B[1][:, 0:NT * NE].rearrange("p (t e) -> p t e", t=NT))
                    link(V.tensor_reduce(e_most, B[1][:, NT * NE:NT * NE + NE], AX.X, ALU.max))
                    V.tensor_scalar(over_i[:, :], e_most, float(P), None, ALU.is_gt).then_inc(place_ready, 1)
                    dve.wait_ge(place_ready, 1)

                base = acts_before(l)
                if l % 2 == 0:
                    def chunk(c, s):
                        first = isinstance(c, int) and c == 0 and l == 0
                        for t in range(NT):
                            v = c * NT + (base + t + 1)
                            dve.wait_ge(gu_th, v)
                            V.scalar_tensor_tensor(f_a[t], f_th[t], 1.0, B[t][:, 0:FC], ALU.add, ALU.mult).then_inc(gu_a, 1)
                            dve.wait_ge(gu_a, v)
                            if not first:
                                dve.wait_ge(act_tr, c * NT + (base + t + 1 - NT))
                            V.scalar_tensor_tensor(f_act[t], f_a[t], 0.5, B[t][:, FC:2 * FC],
                                                   ALU.mult, ALU.mult).then_inc(act_ready, 1)
                    chunks_of_expert(dve, chunk)
                    dve.wait_ge(chunk_used, NCH * (experts_before(l) + 1))
                    for i in range(4):
                        n_, t = i // 2, i % 2
                        xs = x[:, t, n_ * 512:(n_ + 1) * 512]
                        last = V.tensor_tensor(xs, xs, B[4 + i][:, :], ALU.add)
                    last.then_inc(y_added, 1)
                    dve.wait_ge(y_added, l // 2 + 1)
                else:
                    def gather_matrix(e, k):
                        dve.wait_ge(he_ps, k - 1)
                        for t in range(NT):
                            last = V.tensor_scalar(gather_m[:, t, :], steps[:, 0:P], place[:, t, bass.ds(e, 1)],
                                                   chosen[:, t, bass.ds(e, 1)], ALU.is_equal, ALU.mult)
                        last.then_inc(gm_ready, 1)

                    def add_scattered(k):
                        for i in range(4):
                            n_, t = i // 2, i % 2
                            xs = x[:, t, n_ * 512:(n_ + 1) * 512]
                            dve.wait_ge(sc_ps, 4 * k + (i + 1))
                            V.tensor_tensor(xs, xs, B[6 + i % 2][:, :], ALU.add).then_inc(sc_used, 1)

                    def one_pass(p):
                        ab_, kb = base + p * NE * NCH, p * (NE + 1)
                        if p == 1:
                            dve.wait_ge(wm_ready, NE)
                            link(V.tensor_scalar(place, place, -float(P), None, ALU.add))
                            dve.wait_ge(he_ps, kb)
                            for t in range(NT):
                                last = V.tensor_scalar(gather_m[:, t, :], steps[:, 0:P], place[:, t, 0:1],
                                                       chosen[:, t, 0:1], ALU.is_equal, ALU.mult)
                            last.then_inc(gm_ready, 1)
                        else:
                            for t in range(NT):
                                last = V.tensor_scalar(gather_m[:, t, :], steps[:, 0:P], place[:, t, 0:1],
                                                       chosen[:, t, 0:1], ALU.is_equal, ALU.mult)
                            last.then_inc(gm_ready, 1)
                        V.memset(y_e, 0.0).then_inc(ye_ready, 1)
                        V.memset(scatter_m, 0.0).then_inc(sm_ready, 1)
                        with dve.Fori(0, NE) as e:
                            for t in range(NT):
                                last = V.tensor_scalar(weight_m[:, t, :], steps[:, 0:P], place[:, t, bass.ds(e, 1)],
                                                       comb[:, t, bass.ds(e, 1)], ALU.is_equal, ALU.mult)
                            last.then_inc(wm_ready, 1)
                            gather_matrix(e + 1, e + (kb + 2))

                            def chunk(c, s):
                                v = e * NCH + c + (ab_ + 1)
                                dve.wait_ge(gu_th, v)
                                V.scalar_tensor_tensor(f_a[0], f_th[0], 1.0, B[s][:, 0:FC], ALU.add,
                                                       ALU.mult).then_inc(gu_a, 1)
                                dve.wait_ge(gu_a, v)
                                dve.wait_ge(act_tr, v - 1)
                                V.tensor_tensor(f_act[0], f_a[0], B[s][:, FC:2 * FC], ALU.mult).then_inc(act_ready, 1)
                                if isinstance(c, int) and c == 0:
                                    add_scattered(e + kb)
                            chunks_of_expert(dve, chunk)
                            dve.wait_ge(sm_ps, e + (NE * p + 1))
                            dve.wait_ge(sc_used, 4 * e + (4 * kb + 4))
                        add_scattered(kb + NE)
                        dve.wait_ge(sc_used, 4 * (kb + NE + 1))
                    moe_passes(dve, one_pass)
            n = NNORM
            dve.wait_ge(norm_ss, n + 1)
            dve.wait_ge(fin_in, 16)
            for t in range(NT):
                last = V.scalar_tensor_tensor(x[:, t, :], x[:, t, :], rstd[:, t:t + 1], gain_out, ALU.mult, ALU.mult)
            last.then_inc(fin_ready, 1)

        @block.tensor
        def _(pe):
            mm = nc.tensor.matmul
            tr = nc.tensor.transpose
            pe.wait_ge(consts, 1)
            pe.wait_ge(consts, 2)
            pe.wait_ge(par_in, 16 * 9)
            rows = phase[:, 0:3 * P].rearrange("p (a n) -> p a n", a=3)
            tr(B[0][:, 0:P], rows[:, 0, :], ident[:, :])
            tr(B[0][:, P:2 * P], rows[:, 1, :], ident[:, :])
            tr(B[0][:, 2 * P:2 * P + 8], rows[0:8, 2, :], ident[0:8, 0:8]).then_inc(par_ps, 1)

            def transpose_rows(src, n):
                pe.wait_ge(norm_h, NT * (n + 1))
                for b in range(4):
                    for i in range(2):
                        for t in range(NT):
                            k = 2 * b + i
                            last = tr(B[4 + b][:, i * SEQ + t * P:i * SEQ + (t + 1) * P],
                                      src[:, t, k * P:(k + 1) * P], ident[:, :])
                    last.then_inc(norm_ps, 1)

            def arrived(l, j):
                pe.wait_ge(slot_full[j % NSLOT], slot_after_unit(l, j))

            def features_out(l, j, src, banks, ready, free):
                arrived(l, j)
                w = slot(j)[:, 0:4096].rearrange("p (k w) -> p k w", w=512)
                for m in range(4):
                    if m % 2 == 0 and free is not None:
                        free(m // 2)
                    for k in range(KD):
                        last = mm(B[banks[m // 2]][:, (m % 2) * SEQ:(m % 2 + 1) * SEQ],
                                  w[:, k, m * P:(m + 1) * P], src[:, k, :], start=k == 0, stop=k == KD - 1)
                    if m % 2 == 1:
                        last.then_inc(ready, 1)

            def tokens_out(bank, src, t, w, kt, n0):
                for k in range(kt):
                    last = mm(B[bank][:, :], src[:, k, t * P:(t + 1) * P], w[:, k, n0:n0 + 512],
                              start=k == 0, stop=k == kt - 1)
                return last

            transpose_rows(h_tok, 0)

            for l in range(DEPTH):
                if l == 0:
                    pe.wait_ge(hT_ready, 1)
                transpose_rows(h_tok, 1 + 3 * l)
                pe.wait_ge(hT_ready, 2 + 3 * l)
                if l == 0:
                    pe.wait_ge(par_ready, 1)

                features_out(l, U_U, hT[:, :, :], (0, 1), ws_ready, None)

                def pad_tr(q, half):
                    n = 2 * (NQ * l + q) + half
                    pe.wait_ge(pad_ready, 2 * n + 2)
                    if n >= 1:
                        pe.wait_ge(bct_ready, n)
                    for c in range(2):
                        for j in range(NQ):
                            last = tr(B[6 + c][:, j * P:(j + 1) * P], pads[:, c, j * P:(j + 1) * P], ident[:, :])
                    last.then_inc(pad_ps, 1)

                pad_tr(0, 0)
                pad_tr(0, 1)
                pe.wait_ge(ab_in, 16 * (l + 1))
                for t in range(NT):
                    for k in range(KD):
                        last = mm(B[4][:, t * 8:(t + 1) * 8], hT[:, k, t * P:(t + 1) * P], ab_w[:, k, :],
                                  start=k == 0, stop=k == KD - 1)
                last.then_inc(ab_ps, 1)

                def fill(f):
                    j, t = U_Q + f // 2, f % 2
                    if t == 0:
                        arrived(l, j)
                    if f < 2:
                        pe.wait_ge(ws_evac, 8 * l + 1 + f)
                    elif f < 6:
                        pe.wait_ge(rope_done, 4 * l + f - 1)
                    else:
                        pe.wait_ge(fill_evac, 16 * l + f - 5)
                    w = slot(j)[:, 0:4096].rearrange("p (k w) -> p k w", w=512)
                    tokens_out(t, hT[:, :, :], t, w, KD, 0).then_inc(fill_ready, 1)

                def s5_in(i):
                    q, n = i // NQ, NS5 * l + i
                    if i % NQ == 0:
                        pe.wait_ge(bct_ready, 2 * (NQ * l + q) + 2)
                    if i == 0:
                        pe.wait_ge(ws_evac, 8 * l + 2)
                    if n >= 2:
                        pe.wait_ge(bu_read, n - 1)
                    for c in range(2):
                        last = mm(B[2 + n % 2][:, c * SEQ:(c + 1) * SEQ], bct[q % 2][c][:, i % NQ, :], uT[:, q, :],
                                  start=True, stop=True)
                    last.then_inc(bu_ready, 1)

                def s5_out(i):
                    q, n = i // NQ, NS5 * l + i
                    if i == 0:
                        pe.wait_ge(ab_sb, l + 1)
                    if i % NQ == 0 and q >= 2:
                        pe.wait_ge(gel_in, NQ * l + q - 1)
                    pe.wait_ge(h_rot, n + 1)
                    hr = wk5[3 + n % 2]
                    for c in range(2):
                        last = mm(B[4 + q % 2][:, 0:SEQ], bct[q % 2][2 + c][:, i % NQ, :], hr[:, c, :],
                                  start=(i % NQ == 0 and c == 0), stop=(i % NQ == NQ - 1 and c == 1))
                    last.then_inc(y_read, 1)

                for f in range(4):
                    fill(f)
                for i in range(NS5):
                    s5_in(i)
                    fill(4 + i)
                    if i > 0:
                        s5_out(i - 1)
                    if i % NQ == 1 and i // NQ + 1 < NQ:
                        pad_tr(i // NQ + 1, 0)
                        pad_tr(i // NQ + 1, 1)
                s5_out(NS5 - 1)

                pe.wait_ge(fill_evac, 16 * (l + 1))
                features_out(l, U_CONV, hT[:, :, :], (0, 1), ws_ready, None)
                pe.wait_ge(bu_read, NS5 * (l + 1))
                features_out(l, U_CONV + 1, hT[:, :, :], (2, 3), ws_ready, None)
                features_out(l, U_CONV + 2, hT[:, :, :], (0, 1), ws_ready,
                             lambda b: pe.wait_ge(ws_evac, 8 * l + 3 + b))

                pe.wait_ge(gel_in, NQ * (l + 1))
                pe.wait_ge(bct_ready, 2 * NQ * (l + 1))
                for i in range(4):
                    for k in range(KW):
                        last = tr(B[4 + i][:, k * P:(k + 1) * P], qk[:, i // 2, i % 2, k * P:(k + 1) * P], ident[:, :])
                    last.then_inc(mtr_ps, 1)
                pe.wait_ge(mtr_ready, 4 * (l + 1))

                def m_scores(h):
                    n = MH * l + h
                    if h >= 2:
                        pe.wait_ge(ms_neg, n - 1)
                    else:
                        pe.wait_ge(ws_evac, 8 * l + 5 + h)
                    ps = slice((h % 2) * MD, (h % 2 + 1) * MD)
                    mm(B[2 + h % 2][:, 0:P], mqT[ps, h // 2, 0:P], mkT[ps, h // 2, 0:P], start=True, stop=True)
                    mm(B[2 + h % 2][:, P:3 * P], mqT[ps, h // 2, P:2 * P], mkT[ps, h // 2, :], start=True,
                       stop=True).then_inc(ms_ready, 1)

                def m_tr(h):
                    n = MH * l + h
                    pe.wait_ge(ms_norm, n + 1)
                    if h >= 2:
                        pe.wait_ge(ms_pT, n - 1)
                    for b in range(3):
                        last = tr(B[4 + h % 2][:, b * P:(b + 1) * P], mp_[h % 2][:, b * P:(b + 1) * P], ident[:, :])
                    last.then_inc(ms_tr, 1)

                def m_out(h):
                    n = MH * l + h
                    pe.wait_ge(ms_pT, n + 1)
                    if h >= 4 and h % 2 == 0:
                        pe.wait_ge(ms_oT, 4 * l + h // 2 - 1)
                    ps = slice((h % 2) * MD, (h % 2 + 1) * MD)
                    o = B[6 + (h // 2) % 2]
                    pT, vh = mpT[h % 2], v_tok[:, :, h * MD:(h + 1) * MD]
                    mm(o[ps, 0:P], vh[:, 0, :], pT[:, 0:P], start=True, stop=True)
                    mm(o[ps, P:2 * P], vh[:, 0, :], pT[:, P:2 * P], start=True, stop=False)
                    mm(o[ps, P:2 * P], vh[:, 1, :], pT[:, 2 * P:3 * P], start=False, stop=True).then_inc(ms_o, 1)

                for s in range(MH + 2):
                    if s < MH:
                        m_scores(s)
                    if 1 <= s <= MH:
                        m_tr(s - 1)
                    if s >= 2:
                        m_out(s - 2)

                def up(j, src, first, n):
                    arrived(l, j)
                    w = slot(j)[:, 0:4096].rearrange("p (k w) -> p k w", w=D)
                    for i in range(4):
                        if i >= 2:
                            pe.wait_ge(up_used, n + i - 1)
                        last = tokens_out(i % 2, src, i % 2, w, KW, (i // 2) * 512)
                        last.then_inc(up_ps, 1)

                pe.wait_ge(ms_oT, 4 * (l + 1))
                pe.wait_ge(ws_evac, 8 * (l + 1))
                up(U_UPM, m_oT, True, 8 * l)
                pe.wait_ge(y_ready, l + 1)
                pe.wait_ge(up_used, 8 * l + 4)
                for n_ in range(2):
                    j = U_GLU + n_
                    arrived(l, j)
                    w = slot(j)[:, 0:4096].rearrange("p (k w) -> p k w", w=D)
                    for t in range(NT):
                        if n_ == 1:
                            pe.wait_ge(glu_used, 4 * l + t + 1)
                        tokens_out(2 * t, yT[:, :, :], t, w, KW, 0)
                        tokens_out(2 * t + 1, yT[:, :, :], t, w, KW, 512).then_inc(glu_ps, 1)
                pe.wait_ge(glu_used, 4 * l + 4)
                pe.wait_ge(g_step, l + 1)
                mm(B[1][:, 0:NT * GH], cum_mask[:, :], gstep, start=True, stop=True).then_inc(gc_ps, 1)
                for i in range(4):
                    pe.wait_ge(cv_sq, 4 * l + i + 1)
                    tmp = (DTm, Dcl)[i // 2].rearrange("p t h n -> p (t h n)")[:, (i % 2) * 512:(i % 2 + 1) * 512]
                    mm(B[4 + i][:, :], ones[:, :], tmp, start=True, stop=True).then_inc(cv_ss, 1)
                for t in range(NT):
                    pe.wait_ge(g_diag, NT * l + t + 1)
                    mm(B[2 + t][:, :], ones[:, :], gdiag[:, t].rearrange("p h n -> p (h n)"), start=True,
                       stop=True).then_inc(row_ps, 1)
                pe.wait_ge(kq_ready, 4 * (l + 1))
                for t in range(NT):
                    for h in range(GH):
                        last = tr(B[4 + t][:, h * P:(h + 1) * P], cv[:, 4 + h, t * P:(t + 1) * P], ident[:, :])
                    last.then_inc(kv_ps, 1)
                pe.wait_ge(cv_ready, 3 * (l + 1))
                for t in range(NT):
                    for h in range(GH):
                        last = tr(B[6 + t][:, h * P:(h + 1) * P], cv[:, 8 + h, t * P:(t + 1) * P], ident[:, :])
                    last.then_inc(kv_ps, 1)
                for t in range(NT):
                    pe.wait_ge(kv_evac, NT * l + t + 1)
                    for h in range(GH):
                        kh = cv[:, 4 + h, t * P:(t + 1) * P]
                        last = mm(B[4 + t][:, h * P:(h + 1) * P], kh, kh, start=True, stop=True)
                    last.then_inc(kk_ps, 1)
                for t in range(NT):
                    pe.wait_ge(uw_in, NT * l + t + 1)
                    for h in range(GH):
                        last = mm(B[6 + t][:, h * P:(h + 1) * P], cv[:, 4 + h, t * P:(t + 1) * P],
                                  cv[:, h, t * P:(t + 1) * P], start=True, stop=True)
                    last.then_inc(kk_ps, 1)
                for k in range(6):
                    for t in range(NT):
                        n = (6 * l + k) * NT + t
                        pe.wait_ge(m_ready, n + 1)
                        if k == 0:
                            pe.wait_ge(xz_init, 2 * NT * l + 2 * t + 2)
                            pe.wait_ge(dec_in, NT * (l + 1))
                            pe.wait_ge(dec_ready, 3 * NT * (l + 1))
                        else:
                            pe.wait_ge(xz_ready, n - NT + 1)
                        for h in range(GH):
                            last = mm(B[t][:, h * P:(h + 1) * P], M_lvl[:, t, h, :], Zi[:, t, h, :], start=True, stop=True)
                        last.then_inc(w_ps, 1)
                    for t in range(NT):
                        n = (6 * l + k) * NT + t
                        pe.wait_ge(w_evac, n + 1)
                        for h in range(GH):
                            mm(B[2 + t][:, h * P:(h + 1) * P], W_lvl[:, t, h, :], Xi[:, t, h, :], start=True, stop=True)
                        for h in range(GH):
                            last = mm(B[4 + t][:, h * P:(h + 1) * P], Xi[:, t, h, :], W_lvl[:, t, h, :], start=True, stop=True)
                        last.then_inc(xz_ps, 1)
                for t in range(NT):
                    pe.wait_ge(xz_ready, (6 * l + 5) * NT + t + 1)
                    pe.wait_ge(qd_ready, NT * l + t + 1)
                    for h in range(GH):
                        mm(B[t][:, h * P:(h + 1) * P], kbeg[:, t, h, :], Zi[:, t, h, :], start=True, stop=True)
                    for h in range(GH):
                        last = mm(B[2 + t][:, h * P:(h + 1) * P], Zi[:, t, h, :], vbeta[:, t, h, :], start=True, stop=True)
                    last.then_inc(uw_ps, 1)
                pe.wait_ge(w_done, NT * (l + 1))
                pe.wait_ge(s_init, l + 1)
                pe.wait_ge(xz_ready, 6 * NT * (l + 1))
                for c in range(NCHUNK):
                    n, t, off = NCHUNK * l + c, c // 2, (c % 2) * GL
                    rows_ = slice(off, off + GL)
                    if c > 0:
                        pe.wait_ge(s_ready, (NCHUNK - 1) * l + c)
                    S = state[:, c % 2]
                    for h in range(GH):
                        last = mm(B[4][rows_, h * P:(h + 1) * P], wT[:, t, h, rows_], S[:, h, :], start=True, stop=True)
                    last.then_inc(vn_ps, 1)
                    pe.wait_ge(vn_ready, n + 1)
                    if c < NCHUNK - 1:
                        for h in range(GH):
                            last = mm(B[7][:, h * P:(h + 1) * P], kdec[rows_, t, h, :], vn[rows_, h, :], start=True, stop=True)
                        last.then_inc(su_ps, 1)
                    if c >= 2:
                        pe.wait_ge(o_evac, (NCHUNK + 1) * l + c - 1)
                    for h in range(GH):
                        o = B[5 + c % 2][rows_, h * P:(h + 1) * P]
                        mm(o, cv[:, h, t * P + off:t * P + off + GL], S[:, h, :], start=True, stop=False)
                        last = mm(o, qkT[rows_, t, h, rows_], vn[rows_, h, :], start=False, stop=True)
                    last.then_inc(o_ps, 1)
                pe.wait_ge(og_ready, l + 1)
                for t in range(NT):
                    for h in range(GH):
                        last = tr(B[4 + t][:, h * P:(h + 1) * P], o_tok[:, t, h, :], ident[:, :])
                    last.then_inc(og_ps, 1)
                pe.wait_ge(og_T, NT * (l + 1))
                up(U_UPG, g_oT, False, 8 * l + 4)
                pe.wait_ge(up_used, 8 * (l + 1))
                pe.wait_ge(mg_ready, l + 1)
                for b in range(4):
                    for i in range(2):
                        for t in range(NT):
                            k = 2 * b + i
                            last = tr(B[4 + b][:, i * SEQ + t * P:i * SEQ + (t + 1) * P], merged[:, t, k * P:(k + 1) * P], ident[:, :])
                    last.then_inc(mg_ps, 1)
                pe.wait_ge(mg_T, 4 * (l + 1))
                for n_ in range(2):
                    arrived(l, U_OUT + n_)
                    w = slot(U_OUT + n_)[:, 0:4096].rearrange("p (k w) -> p k w", w=512)
                    for t in range(NT):
                        if n_ == 1:
                            pe.wait_ge(wo_used, 4 * l + t + 1)
                        tokens_out(t, hT[:, :, :], t, w, KD, 0).then_inc(wo_ps, 1)
                pe.wait_ge(memn_ready, l + 1)
                features_out(l, U_WK, memnT, (2, 3), xk_ps, None)
                pe.wait_ge(wo_used, 4 * (l + 1))
                arrived(l, U_WV)
                w = slot(U_WV)[:, 0:4096].rearrange("p (k w) -> p k w", w=512)
                for t in range(NT):
                    tokens_out(t, memnT, t, w, KD, 0).then_inc(xk_ps, 1)
                transpose_rows(h_tok, 2 + 3 * l)
                pe.wait_ge(hT_ready, 3 + 3 * l)
                pe.wait_ge(xk_sb, 6 * l + 4)
                features_out(l, U_WQ, hT[:, :, :], (0, 1), xk_ps, None)
                pe.wait_ge(xk_sb, 6 * l + 6)

                def x_scores(h):
                    n = XH * l + h
                    if h >= 2:
                        pe.wait_ge(xs_exp, n - 1)
                    for t in range(NT):
                        last = mm(B[2 + h % 2][:, t * SEQ:(t + 1) * SEQ], xqT[:, h, t * P:(t + 1) * P], xkT[:, h, :],
                                  start=True, stop=True)
                    last.then_inc(xs_ps, 1)

                def x_tr(h):
                    n = XH * l + h
                    pe.wait_ge(xs_norm, n + 1)
                    if h >= 2:
                        pe.wait_ge(xs_pT, n - 1)
                    for m in range(NT):
                        for t in range(NT):
                            last = tr(B[4 + h % 2][:, m * SEQ + t * P:m * SEQ + (t + 1) * P],
                                      xp[h % 2][:, t, m * P:(m + 1) * P], ident[:, :])
                    last.then_inc(xs_tr, 1)

                def x_out(h):
                    n = XH * l + h
                    pe.wait_ge(xs_pT, n + 1)
                    if h >= 2:
                        pe.wait_ge(xs_oT, n - 1)
                    for m in range(NT):
                        last = mm(B[6 + h % 2][:, 0:SEQ], x_v[:, m, h * XD:(h + 1) * XD], xpT[h % 2][:, m, :],
                                  start=m == 0, stop=m == NT - 1)
                    last.then_inc(xs_o, 1)

                for s in range(XH + 2):
                    if s < XH:
                        x_scores(s)
                    if 1 <= s <= XH:
                        x_tr(s - 1)
                    if s >= 2:
                        x_out(s - 2)
                pe.wait_ge(xs_oT, XH * (l + 1))
                arrived(l, U_WO)
                w = slot(U_WO)[:, 0:4096].rearrange("p (k w) -> p k w", w=D)
                for i in range(4):
                    if i >= 2:
                        pe.wait_ge(xo_used, 4 * l + i - 1)
                    tokens_out(i % 2, x_oT, i % 2, w, KW, (i // 2) * 512).then_inc(xo_ps, 1)
                transpose_rows(h_tok, 3 + 3 * l)
                pe.wait_ge(hT_ready, 4 + 3 * l)
                if l % 2 == 1:
                    pe.wait_ge(rout_in, 16)
                    for t in range(NT):
                        for k in range(KD):
                            last = mm(B[0][:, t * NE:(t + 1) * NE], hT[:, k, t * P:(t + 1) * P], router_w[:, k, :],
                                      start=k == 0, stop=k == KD - 1)
                    last.then_inc(rl_ps, 1)
                base = acts_before(l)
                if l % 2 == 0:
                    def at(c, t):
                        return c * NT + (base + t + 1)

                    def first_of_all(c):
                        return isinstance(c, int) and c == 0 and l == 0

                    def gate_up(c, t, s):
                        w = ring[:, s * SLOT:s * SLOT + 4096].rearrange("p (k w) -> p k w", w=512)
                        if not first_of_all(c):
                            pe.wait_ge(act_ready, at(c, t) - NT)
                        tokens_out(t, hT[:, :, :], t, w, KD, 0).then_inc(gu_ps, 1)

                    def flip(c, t):
                        pe.wait_ge(act_ready, at(c, t))
                        if not first_of_all(c):
                            pe.wait_ge(actT_ready, at(c, t) - NT)
                        for k in range(FC // P):
                            last = tr(B[2 + t][:, k * P:(k + 1) * P], f_act[t][:, k * P:(k + 1) * P], ident[:, :])
                        last.then_inc(act_tr, 1)

                    def down(c, s, first, last_one):
                        w = ring[:, s * SLOT + 4096:(s + 1) * SLOT].rearrange("p (k n) -> p k n", n=D)
                        pe.wait_ge(actT_ready, at(c, NT - 1))
                        for t in range(NT):
                            for n_ in range(2):
                                for k in range(FC // P):
                                    last = mm(B[4 + 2 * n_ + t][:, :], f_actT[:, k, t * P:(t + 1) * P],
                                              w[:, k, n_ * 512:(n_ + 1) * 512], start=first and k == 0,
                                              stop=last_one and k == FC // P - 1)
                        last.then_inc(chunk_used, 1)

                    def chunk(c, s, in_slot):
                        pe.wait_ge(slot_full[s], slot_after_chunk(l, 0, in_slot, s))
                        gate_up(c, 0, s)
                        if not (isinstance(c, int) and c == 0):
                            flip(c - 1, 1)
                        gate_up(c, 1, s)
                        if not (isinstance(c, int) and c == 0):
                            down(c - 1, (s - 1) % NSLOT, isinstance(c, int) and c == 1, False)
                        flip(c, 0)

                    chunk(0, 0, 0)
                    chunk(1, 1, 0)
                    loops = (NCH - 2) // NSLOT
                    with pe.Fori(0, loops) as r:
                        for i in range(NSLOT):
                            c = 2 + i
                            chunk(r * NSLOT + c, c % NSLOT, r + c // NSLOT)
                    for c in range(2 + loops * NSLOT, NCH):
                        chunk(c, c % NSLOT, c // NSLOT)
                    flip(NCH - 1, 1)
                    down(NCH - 1, (NCH - 1) % NSLOT, False, True)
                else:
                    pe.wait_ge(comb_ready, 1)
                    cols = slice(0, NE)
                    mm(B[1][:, 0:NE], before[:, :], chosen[:, 0, cols], start=True, stop=True)
                    mm(B[1][:, NE:2 * NE], ones[:, :], chosen[:, 0, cols], start=True, stop=False)
                    mm(B[1][:, NE:2 * NE], before[:, :], chosen[:, 1, cols], start=False, stop=True)
                    mm(B[1][:, 2 * NE:3 * NE], ones[:, :], chosen[:, 0, cols], start=True, stop=False)
                    mm(B[1][:, 2 * NE:3 * NE], ones[:, :], chosen[:, 1, cols], start=False, stop=True).then_inc(place_ps, 1)

                    def gather():
                        for k in range(KD):
                            for t in range(NT):
                                last = mm(B[6 + k // 4][:, (k % 4) * P:(k % 4 + 1) * P], h_tok[:, t, k * P:(k + 1) * P],
                                          gather_m[:, t, :], start=t == 0, stop=t == NT - 1)
                        last.then_inc(he_ps, 1)

                    def scatter(k):
                        pe.wait_ge(sm_ready, k)
                        pe.wait_ge(ye_ready, k)
                        for i in range(4):
                            n_, t = i // 2, i % 2
                            if i >= 2:
                                pe.wait_ge(sc_used, 4 * k + (i - 5))
                            mm(B[6 + i % 2][:, :], scatter_m[:, t * P:(t + 1) * P], y_e[:, n_ * 512:(n_ + 1) * 512],
                               start=True, stop=True).then_inc(sc_ps, 1)

                    def one_pass(p):
                        ab_, kb = base + p * NE * NCH, p * (NE + 1)
                        if p == 0:
                            pe.wait_ge(h_gain, NT)
                            pe.wait_ge(hT_ready, 4 + 3 * l)
                        else:
                            pe.wait_ge(sc_used, 4 * kb)
                        pe.wait_ge(gm_ready, kb + 1)
                        gather()
                        with pe.Fori(0, NE) as e:
                            def flip(c):
                                if isinstance(c, int) and c == 0:
                                    pe.wait_ge(sm_ready, e + (kb + 2))
                                pe.wait_ge(act_ready, e * NCH + c + (ab_ + 1))
                                pe.wait_ge(actT_ready, e * NCH + c + ab_)
                                for k in range(FC // P):
                                    last = tr(B[3][:, k * P:(k + 1) * P], f_act[0][:, k * P:(k + 1) * P], ident[:, :])
                                last.then_inc(act_tr, 1)

                            def down(c, s, first, last_one):
                                w = ring[:, s * SLOT + 4096:(s + 1) * SLOT].rearrange("p (k n) -> p k n", n=D)
                                pe.wait_ge(actT_ready, e * NCH + c + (ab_ + 1))
                                for n_ in range(2):
                                    for k in range(FC // P):
                                        last = mm(B[4 + n_][:, :], f_actT[:, k, 0:P], w[:, k, n_ * 512:(n_ + 1) * 512],
                                                  start=first and k == 0, stop=last_one and k == FC // P - 1)
                                last.then_inc(chunk_used, 1)

                            def chunk(c, s, in_slot):
                                head = isinstance(c, int) and c == 0
                                w = ring[:, s * SLOT:s * SLOT + 4096].rearrange("p (k w) -> p k w", w=512)
                                pe.wait_ge(slot_full[s], slot_after_chunk(l, e + p * NE, in_slot, s))
                                if head:
                                    pe.wait_ge(he_ready, e + (kb + 1))
                                for k in range(KD):
                                    if k == KD // 2 and not head:
                                        flip(c - 1)
                                    last = mm(B[s][:, :], h_e[:, k, :], w[:, k, :], start=k == 0, stop=k == KD - 1)
                                last.then_inc(gu_ps, 1)
                                if head:
                                    scatter(e + (kb + 1))
                                    pe.wait_ge(wm_ready, e + (p * NE + 1))
                                    for t in range(NT):
                                        last = tr(B[3][:, (2 + t) * P:(3 + t) * P], weight_m[:, t, :], ident[:, :])
                                    last.then_inc(sm_ps, 1)
                                if isinstance(c, int) and c == NCH - 1:
                                    pe.wait_ge(gm_ready, e + (kb + 2))
                                    pe.wait_ge(sc_used, 4 * e + (4 * kb + 4))
                                    gather()
                                if not head:
                                    down(c - 1, (s - 1) % NSLOT, isinstance(c, int) and c == 1, False)

                            chunk(0, 0, 0)
                            chunk(1, 1, 0)
                            loops = (NCH - 3) // NSLOT
                            with pe.Fori(0, loops) as r:
                                for i in range(NSLOT):
                                    c = 2 + i
                                    chunk(r * NSLOT + c, c % NSLOT, r + c // NSLOT)
                            for c in range(2 + loops * NSLOT, NCH):
                                chunk(c, c % NSLOT, c // NSLOT)
                            flip(NCH - 1)
                            down(NCH - 1, (NCH - 1) % NSLOT, False, True)
                        scatter(kb + NE + 1)
                    moe_passes(pe, one_pass)


_INS = ["x", "mem", "positions", "norm_mix", "w_in", "ssm_a_re", "ssm_a_im", "ssm_log_dt", "ssm_b_re",
        "ssm_b_im", "ssm_c_re", "ssm_c_im", "ssm_d", "ssm_w_glu", "gdn_conv", "gdn_a_log", "gdn_dt_bias",
        "gdn_norm", "w_up_moba", "w_up_gdn", "w_out", "norm_xa", "norm_mem", "xa_wq", "xa_wk", "xa_wv",
        "xa_wo", "norm_ffn", "ffn_w_gate", "ffn_w_up", "ffn_w_down", "moe_w_router", "moe_w_gate",
        "moe_w_up", "moe_w_down", "norm_final"]


def kernel(**inputs):
    import numpy as _np
    import concourse.bacc as _bacc
    from concourse import mybir as _mybir
    from concourse.bass_utils import run_bass_kernel_spmd as _run

    nc = _bacc.Bacc("TRN2", target_bir_lowering=False, num_devices=1)
    arrays, args = {}, []
    for name in _INS:
        a = _np.ascontiguousarray(inputs[name])
        arrays[f"in_{name}"] = a
        args.append(nc.dram_tensor(f"in_{name}", a.shape, _mybir.dt.from_np(a.dtype), kind="ExternalInput").ap())
    shape = inputs["x"].shape
    args.append(nc.dram_tensor("out", shape, _mybir.dt.float32, kind="ExternalOutput").ap())
    hybrid_trunk(nc, *args)
    r = _run(nc, [arrays], core_ids=[0])
    return r.results[0]["out"]
```

```python
import math
from contextlib import ExitStack

import concourse.bass as bass
from concourse import mybir


def hybrid_trunk(nc: bass.Bass, x_d, mem_d, positions_d, norm_mix_d, w_in_d, a_re_d, a_im_d, log_dt_d,
                 b_re_d, b_im_d, c_re_d, c_im_d, ssm_d_d, w_glu_d, conv_d, a_log_d, dt_bias_d,
                 gdn_norm_d, w_up_moba_d, w_up_gdn_d, w_out_d, norm_xa_d, norm_mem_d, wq_d, wk_d, wv_d,
                 wo_d, norm_ffn_d, ffn_gate_d, ffn_up_d, ffn_down_d, router_d, moe_gate_d, moe_up_d,
                 moe_down_d, norm_final_d, out_d):
    F32 = mybir.dt.float32
    I32 = mybir.dt.int32
    ALU = mybir.AluOpType
    ACT = mybir.ActivationFunctionType
    AX = mybir.AxisListType

    P = 128
    SEQ, D = x_d.shape[1], x_d.shape[2]
    DEPTH = w_in_d.shape[0]
    NT = SEQ // P
    KD = D // P
    W = w_up_moba_d.shape[1]
    KW = W // P
    EPS = 1e-6
    NEG = -1e30
    MH, MD = 8, 64
    GH, GD, GL = 4, 128, 64
    NCHUNK = SEQ // GL
    XH, XD = 4, 128
    NS5 = 16
    NQ = 4
    D_FF = ffn_gate_d.shape[2]
    FC = 256
    NCH = D_FF // FC
    NE = moe_gate_d.shape[1]
    THETA = 10000.0
    TWO_PI = 2.0 * math.pi
    C1 = 6.28125
    C2 = TWO_PI - C1
    MAGIC = 1.5 * 2.0 ** 23
    PI_IN = 3.141592
    GELU_C = math.sqrt(2.0 / math.pi)
    NSLOT = 3
    SLOT = 6144
    IN_U, IN_QG, IN_KG, IN_VG, IN_AB, IN_Z, IN_GATE = 1536, 2048, 2560, 3072, 3584, 3592, 4104

    def in_cols(l, c0):
        return [(w_in_d[l].rearrange("(k p) n -> p k n", p=P)[:, :, c0:c0 + 512], 0, 512)]

    def half_width(w, l):
        return [(w[l].rearrange("(k p) n -> p k n", p=P), 0, D)]

    def glu_cols(l, n):
        v = w_glu_d[l].rearrange("(k p) (s n) -> s p k n", p=P, s=2)
        return [(v[s, :, :, n * 512:(n + 1) * 512], s * 512, D) for s in range(2)]

    def out_cols(l, n):
        return [(w_out_d[l].rearrange("(k p) n -> p k n", p=P)[:, :, n * 512:(n + 1) * 512], 0, 512)]

    def full_width(w, l):
        return [(w[l].rearrange("(k p) n -> p k n", p=P), 0, 512)]

    def mixer_units(l):
        return ([in_cols(l, c) for c in (IN_U, 0, 512, 1024, IN_Z)]
                + [in_cols(l, IN_GATE + 512 * g) for g in range(6)]
                + [in_cols(l, c) for c in (IN_QG, IN_KG, IN_VG)]
                + [glu_cols(l, 0), glu_cols(l, 1), half_width(w_up_moba_d, l), half_width(w_up_gdn_d, l),
                   out_cols(l, 0), out_cols(l, 1), full_width(wk_d, l), full_width(wv_d, l),
                   full_width(wq_d, l), half_width(wo_d, l)])

    U_U, U_Q, U_CONV = 0, 1, 11
    U_GLU, U_UPM, U_UPG, U_OUT, U_WK, U_WV, U_WQ, U_WO = 14, 16, 17, 18, 20, 21, 22, 23
    NUNIT = 24
    GRP, NGRP = 1024, 6

    def experts(l):
        return 1 if l % 2 == 0 else NE

    def unit_base(l):
        return sum(NUNIT + NCH * experts(m) for m in range(l))

    def glu_extra(j):
        return 2 if j in (U_GLU, U_GLU + 1) else 1

    def slot_before(l, s):
        n = 0
        for m in range(l):
            n += sum(glu_extra(j) for j in range(NUNIT) if j % NSLOT == s)
            n += 3 * experts(m) * len([c for c in range(NCH) if c % NSLOT == s])
        return n

    def slot_after_unit(l, j):
        s = j % NSLOT
        return 16 * (slot_before(l, s) + sum(glu_extra(i) for i in range(j + 1) if i % NSLOT == s))

    def slot_after_chunk(l, e, c_in_slot, s):
        per_expert = 3 * len([c for c in range(NCH) if c % NSLOT == s])
        start = slot_before(l, s) + sum(glu_extra(i) for i in range(NUNIT) if i % NSLOT == s)
        return 16 * start + e * (16 * per_expert) + 48 * c_in_slot + 48

    ctx = ExitStack()
    with ctx:
        def sb(name, shape, dt=F32):
            return ctx.enter_context(nc.sbuf_tensor(name, shape, dt))

        def next_at():
            return -(-nc.sbuf_base // 32) * 32

        def over(name, shape, at):
            return nc.alloc_sbuf_tensor_at(name, shape, mybir.dt.float32r, offset=at)

        def sem(name):
            return ctx.enter_context(nc.semaphore(name))

        class Region:

            def __init__(self, buf, end):
                self.buf, self.at, self.end = buf, 0, end

            def take(self, *shape):
                n = int(math.prod(shape))
                v = self.buf[:, self.at:self.at + n]
                self.at += n
                assert self.at <= self.end, (self.at, self.end)
                if len(shape) > 1:
                    names = "abcd"[:len(shape)]
                    v = v.rearrange(f"p ({' '.join(names)}) -> p {' '.join(names)}",
                                    **{n_: s for n_, s in zip(names, shape)})
                return v

        ring = sb("ring", [P, NSLOT * SLOT])
        x = sb("x", [P, NT, D])
        hT = sb("hT", [P, KD, SEQ])
        memT = sb("memT", [P, KD, SEQ])
        qk_at = next_at()
        qk = sb("qk", [P, 2, NT, W])
        v_tok = sb("v_tok", [P, NT, W])
        z_tok = sb("z_tok", [P, NT, W])
        uT = sb("uT", [P, NQ, SEQ])
        yT = sb("yT", [P, NQ, SEQ])
        gates = sb("gates", [P, NT, 3 * D])
        RAW = SEQ + 3
        PH = 11776
        phase_at = next_at()
        phase = sb("phase", [P, PH])
        raw = phase[:, 8192:8192 + 12 * RAW].rearrange("p (j n) -> p j n", n=RAW)
        merged = qk[:, :, :, :].rearrange("p a t n -> p (a t n)").rearrange("p (t n) -> p t n", t=NT)
        h_tok = gates[:, :, :].rearrange("p t n -> p (t n)")[:, 2 * D:4 * D].rearrange("p (t n) -> p t n", t=NT)
        gain_out = gates[:, :, :].rearrange("p t n -> p (t n)")[:, 4 * D:5 * D]
        spare = [ring[:, s * SLOT + 4096:(s + 1) * SLOT] for s in range(NSLOT)]

        def spare_half(s, i):
            return spare[s][:, i * 1024:(i + 1) * 1024]

        ident = sb("ident", [P, P])
        ones = sb("ones", [P, P])
        cum_mask = sb("cum_mask", [P, P])
        level_mask = sb("level_mask", [P, 6, P])
        causal = sb("causal", [P, 3 * P])
        b_mask = sb("b_mask", [P, NQ, 8, 16])
        c_mask = sb("c_mask", [P, NQ, 2, 64])
        steps = sb("steps", [P, SEQ])
        before = sb("before", [P, P])
        inv_freq = sb("inv_freq", [P, MD // 2])
        params = sb("params", [P, 3 * P])
        small_bc = sb("small_bc", [P, DEPTH, 2, GH])
        gnorm_bc = sb("gnorm_bc", [P, DEPTH, GD])
        cosr = sb("cosr", [P, NT, MD // 2])
        sinr = sb("sinr", [P, NT, MD // 2])
        pos_i = sb("pos_i", [P, NT], I32)
        pos_f = sb("pos_f", [P, NT])
        s5c = sb("s5c", [P, 14, DEPTH * NS5])
        idx8 = sb("idx8", [P, 8])
        eps_col = sb("eps_col", [P, 3])
        router_w = sb("router_w", [P, KD, NE])
        ab_w = sb("ab_w", [P, KD, 2 * GH])
        st = sb("st", [P, 96])

        NG = DEPTH * KD
        gain_mix, gain_xa, gain_mem, gain_ffn = (params[:, i * NG:(i + 1) * NG] for i in range(4))
        p_are = params[:, 64:96]
        p_aim = params[:, 96:128]
        p_conv = params[:, 128:224]
        p_dt = params[:, 224:256]
        p_d = params[:, 256:264]
        DEC, THR, BCR, BCI = (s5c[:, i, :] for i in range(4))

        ss, rstd = st[:, 0:2], st[:, 2:4]
        mx, nm, rs = st[:, 4:8], st[:, 8:12], st[:, 12:16]
        ab = st[:, 16:32]
        gate_z, gate_e = st[:, 32:40], st[:, 40:48]
        gcum, beta = st[:, 48:56], st[:, 56:64]
        bexp = st[:, 64:72]
        kds = st[:, 72:80]
        gstep = st[:, 80:88]
        ealog = st[:, 88:92]

        r5 = Region(phase, PH)
        tab = [r5.take(NQ, 2, SEQ) for _ in range(2)]
        bct = [[r5.take(NQ, P) for _ in range(4)] for _ in range(2)]
        c_nat = r5.take(2, NQ, 64)
        b_bar = r5.take(2, NS5, 16)
        wk5 = [r5.take(2, SEQ) for _ in range(5)]
        ang, turns = spare_half(0, 0), spare_half(0, 1)
        s_half = spare_half(1, 0)
        pads = spare_half(1, 1).rearrange("p (c n) -> p c n", c=2)
        y5 = yT[:, :, :]
        b_nat = spare_half(2, 0)[:, 0:2 * NS5 * 16].rearrange("p (c t n) -> p c t n", c=2, t=NS5)
        y5b = spare_half(2, 1).rearrange("p (c n) -> p c n", n=SEQ)

        rm = Region(phase, PH)
        mqT, mkT = rm.take(KW, SEQ), rm.take(KW, SEQ)
        m_oT = rm.take(KW, SEQ)
        mp_ = [rm.take(3 * P) for _ in range(2)]
        mpT = [rm.take(3 * P) for _ in range(2)]
        glu_t = [rm.take(512) for _ in range(2)]
        glu_y = [rm.take(512) for _ in range(2)]
        gl_tmp = [rm.take(512) for _ in range(2)]

        rg = Region(phase, PH)
        cv = rg.take(12, SEQ)
        k_tok = rg.take(NT, GH, GD)
        kbeg = rg.take(NT, GH, GD)
        vbeta = rg.take(NT, GH, GD)
        kdec = rg.take(NT, GH, GD)
        e_row = rg.take(NT, GH, P)
        dec = rg.take(NT, GH, P)
        decT = rg.take(NT, GH, P)
        qkT = rg.take(NT, GH, P)
        vn = rg.take(GH, GD)
        wT, u_tok = dec, decT
        o_tok, g_oT = k_tok, kbeg.rearrange("p t h d -> p (t h d)").rearrange("p (k n) -> p k n", k=KW)
        Xi = uT[:, :, :].rearrange("p q n -> p (q n)").rearrange("p (t h n) -> p t h n", t=NT, h=GH)
        Zi = yT[:, :, :].rearrange("p q n -> p (q n)").rearrange("p (t h n) -> p t h n", t=NT, h=GH)
        state = v_tok[:, :, :].rearrange("p t (h n) -> p t h n", h=GH)
        rq = [kbeg, vbeta, kdec, qkT]
        A_low, M_lvl, W_lvl, DTm, Dcl, gdiag = (
            spare_half(i // 2, i % 2).rearrange("p (t h n) -> p t h n", t=NT, h=GH) for i in range(6))

        rx = Region(phase, PH)
        memnT = rx.take(KD, SEQ)
        xkT, xqT, x_oT = rx.take(XH, SEQ), rx.take(XH, SEQ), rx.take(XH, SEQ)
        x_v = rx.take(NT, W)
        xp = [rx.take(NT, SEQ) for _ in range(2)]
        xpT = [rx.take(NT, SEQ) for _ in range(2)]

        rf = Region(phase, PH)
        f_th = [rf.take(FC) for _ in range(NT)]
        f_a = [rf.take(FC) for _ in range(NT)]
        f_act = [rf.take(FC) for _ in range(NT)]
        rf.take(2 * KD * P + 2 * FC // P * SEQ)
        r_log = rf.take(NT, NE)
        r_max = rf.take(NT, NE)
        r_w = rf.take(NT, 4)
        r_eq = rf.take(2, NT, NE)
        r_idx = sb("r_idx", [P, NT, NE], mybir.dt.uint32)
        r_idf = rf.take(NT, NE)
        comb, chosen, place = (rf.take(NT, NE + 1) for _ in range(3))
        e_count = rf.take(NE)
        e_most = rf.take(1)
        over_i = sb("over_i", [P, 1], I32)
        gather_m = rf.take(NT, P)
        weight_m = rf.take(NT, P)
        scatter_m = rf.take(NT * P)
        y_e = rf.take(D)
        MIX = 4
        assert MIX * 2 * GRP <= 6 * NT * W + 2 * D
        end_at = PH - (NGRP - MIX) * 2 * GRP
        split_mix = over("split_mix", [P, MIX, 2, GRP], qk_at)
        split_end = over("split_end", [P, NGRP - MIX, 2, GRP], phase_at + 4 * end_at)
        split = [split_mix[:, i] for i in range(MIX)] + [split_end[:, i] for i in range(NGRP - MIX)]
        op_at = NT * 3 * FC
        assert op_at + 2 * KD * SEQ + 2 * FC // P * SEQ <= end_at and rf.at <= end_at
        fx = over("fx", [P, 2, KD, SEQ], phase_at + 4 * op_at)
        f_actT = over("f_actT", [P, 2, FC // P, SEQ], phase_at + 4 * (op_at + 2 * KD * SEQ))
        fx_e = over("fx_e", [P, 2, KD, P], phase_at + 4 * op_at)
        f_actT_e = over("f_actT_e", [P, 2, FC // P, P], phase_at + 4 * (op_at + 2 * KD * P))
        HI, LO = 0, 1
        gain_bc = gates[:, :, :].rearrange("p t n -> p (t n)")[:, 5 * D:6 * D]

        B = [ctx.enter_context(nc.psum_tensor(f"bank{i}", [P, 512], F32)) for i in range(8)]

        x_in, mem_in, par_in, tables_in = sem("x_in"), sem("mem_in"), sem("par_in"), sem("tables_in")
        TABLES = 16 * (3 * DEPTH + 2)
        out_done = sem("out_done")
        slot_full = [sem(f"slot_full{s}") for s in range(NSLOT)]
        split_hi, split_lo, split_used = sem("split_hi"), sem("split_lo"), sem("split_used")
        fx_hi, fx_ready, actT_hi = sem("fx_hi"), sem("fx_ready"), sem("actT_hi")
        ab_in, bc_nat_in = sem("ab_in"), sem("bc_nat_in")
        consts = sem("consts")
        pool_chain, act_chain, dve_chain = sem("pool_chain"), sem("act_chain"), sem("dve_chain")
        par_ps, par_ready = sem("par_ps"), sem("par_ready")
        norm_sq, norm_ss, norm_h, norm_ps, hT_ready = sem("norm_sq"), sem("norm_ss"), sem("norm_h"), sem("norm_ps"), sem("hT_ready")
        s5_dt, s5_ang, s5_sin, s5_const = sem("s5_dt"), sem("s5_ang"), sem("s5_sin"), sem("s5_const")
        rot_ang, rot_sin = sem("rot_ang"), sem("rot_sin")
        ws_ready, ws_evac = sem("ws_ready"), sem("ws_evac")
        ab_ps, ab_sb = sem("ab_ps"), sem("ab_sb")
        fill_ready, rope_done, fill_evac = sem("fill_ready"), sem("rope_done"), sem("fill_evac")
        tab_ang, tab_ready, tab_sin = sem("tab_ang"), sem("tab_ready"), sem("tab_sin")
        b_bar_ready, pad_ready, pad_ps, bct_ready = sem("b_bar_ready"), sem("pad_ready"), sem("pad_ps"), sem("bct_ready")
        bu_ready, bu_read, h_rot, y_read = sem("bu_ready"), sem("bu_read"), sem("h_rot"), sem("y_read")
        gel_in, gel_t, y_ready = sem("gel_in"), sem("gel_t"), sem("y_ready")
        mtr_ps, mtr_ready = sem("mtr_ps"), sem("mtr_ready")
        ms_ready, ms_neg, ms_exp, ms_norm, ms_tr, ms_pT, ms_o, ms_oT = (
            sem(n) for n in ("ms_ready", "ms_neg", "ms_exp", "ms_norm", "ms_tr", "ms_pT", "ms_o", "ms_oT"))
        up_ps, up_used = sem("up_ps"), sem("up_used")
        glu_ps, glu_th, glu_used = sem("glu_ps"), sem("glu_th"), sem("glu_used")
        cv_tap, cv_pre, cv_th, cv_ready, cv_sq, cv_ss, cv_rs, kq_ready = (
            sem(n) for n in ("cv_tap", "cv_pre", "cv_th", "cv_ready", "cv_sq", "cv_ss", "cv_rs", "kq_ready"))
        g_z, gate_tanh, g_ln, g_step, gc_ps, gc_sb, g_bexp, g_diag, row_ps = (
            sem(n) for n in ("g_z", "gate_tanh", "g_ln", "g_step", "gc_ps", "gc_sb", "g_bexp", "g_diag", "row_ps"))
        dec_in, dec_ready, kv_ps, kv_evac, kk_ps, a_ready, qk_ready = (
            sem(n) for n in ("dec_in", "dec_ready", "kv_ps", "kv_evac", "kk_ps", "a_ready", "qk_ready"))
        xz_init, m_ready, w_ps, w_evac, xz_ps, xz_ready = (
            sem(n) for n in ("xz_init", "m_ready", "w_ps", "w_evac", "xz_ps", "xz_ready"))
        uw_in, uw_ps, w_done, u_done, qd_ready = (sem(n) for n in ("uw_in", "uw_ps", "w_done", "u_done", "qd_ready"))
        s_init, vn_ps, vn_ready, o_ps, su_ps, s_ready, o_evac = (
            sem(n) for n in ("s_init", "vn_ps", "vn_ready", "o_ps", "su_ps", "s_ready", "o_evac"))
        og_ss, og_rs, og_ready, og_ps, og_T = sem("og_ss"), sem("og_rs"), sem("og_ready"), sem("og_ps"), sem("og_T")
        mg_ready, mg_ps, mg_T, wo_ps, wo_used = sem("mg_ready"), sem("mg_ps"), sem("mg_T"), sem("wo_ps"), sem("wo_used")
        memn_ready, xk_ps, xk_sb = sem("memn_ready"), sem("xk_ps"), sem("xk_sb")
        xs_ps, xs_neg, xs_exp, xs_norm, xs_tr, xs_pT, xs_o, xs_oT = (
            sem(n) for n in ("xs_ps", "xs_neg", "xs_exp", "xs_norm", "xs_tr", "xs_pT", "xs_o", "xs_oT"))
        xo_ps, xo_used = sem("xo_ps"), sem("xo_used")
        rl_ps, rl_d, rl_e, comb_ready = (sem(n) for n in ("rl_ps", "rl_d", "rl_e", "comb_ready"))
        gain_in, h_gain, place_ps, place_ready = (sem(n) for n in ("gain_in", "h_gain", "place_ps", "place_ready"))
        gm_ready, wm_ready, he_ps, sm_ps, sm_ready, ye_ready, sc_ps, sc_used = (
            sem(n) for n in ("gm_ready", "wm_ready", "he_ps", "sm_ps", "sm_ready", "ye_ready", "sc_ps",
                             "sc_used"))
        gu_th, gu_a, act_ready, act_tr, actT_ready, y_added = (
            sem(n) for n in ("gu_th", "gu_a", "act_ready", "act_tr", "actT_ready", "y_added"))
        fin_ready = sem("fin_ready")


        NNORM = 3 * DEPTH + 1

        def multiplied(l, j):
            if j == U_U:
                return ws_ready, 8 * l + 2
            if j < U_CONV:
                return fill_ready, 20 * l + 2 * (j - U_Q) + 2
            if j < U_GLU:
                return ws_ready, 8 * l + 2 * (j - U_CONV) + 4
            return {U_UPM: (up_ps, 8 * l + 4), U_GLU: (glu_ps, 4 * l + 2), U_GLU + 1: (glu_ps, 4 * l + 4),
                    U_UPG: (up_ps, 8 * l + 8), U_OUT: (wo_ps, 4 * l + 2), U_OUT + 1: (wo_ps, 4 * l + 4),
                    U_WK: (xk_ps, 6 * l + 2), U_WV: (xk_ps, 6 * l + 4), U_WQ: (xk_ps, 6 * l + 6),
                    U_WO: (xo_ps, 4 * l + 4)}[j]

        def slot(j):
            return ring[:, (j % NSLOT) * SLOT:(j % NSLOT) * SLOT + SLOT]

        def experts_before(l):
            return sum(experts(m) for m in range(l))

        def gu_at(c, i):
            return i if isinstance(c, int) and c == 0 else c * 6 + (i - 2)

        def down_at(c, i):
            return 6 * NCH - 2 + i if isinstance(c, int) and c == NCH - 1 else c * 6 + (8 + i)

        def gu_buf(c, i):
            return i + 2 if isinstance(c, int) and c == 0 else i

        def down_buf(c, i):
            return i if isinstance(c, int) and c == NCH - 1 else 4 + i

        def raw_group(s, i):
            return ring[:, s * SLOT + i * GRP:s * SLOT + (i + 1) * GRP]

        def full_at(l, c, s, e=0):
            return slot_after_chunk(l, e, 0, s) + (c - s) * (48 // NSLOT)

        def fx_before(l):
            return (l + 1) // 2

        def chunks_of_expert(eng, chunk, alone=1):
            for c in range(alone):
                chunk(c, c)
            loops = (NCH - alone) // NSLOT
            with eng.Fori(0, loops) as r:
                for i in range(NSLOT):
                    chunk(r * NSLOT + (alone + i), (alone + i) % NSLOT)
            for c in range(alone + loops * NSLOT, NCH):
                chunk(c, c % NSLOT)

        def moe_passes(eng, one_pass):
            one_pass(0)
            eng.wait_ge(place_ready, 1)
            more = eng.value_load(over_i[0:1, 0:1], min_val=0, max_val=1)
            with eng.If(more > 0):
                one_pass(1)

        def acts_before(l):
            return sum(NCH * (NT if m % 2 == 0 else NE) for m in range(l))

        block = ctx.enter_context(nc.Block())

        @block.sync
        def _(sp):
            x_v_ = x_d[0].rearrange("(t p) n -> p t n", p=P)
            sp.dma_start(x[:, :, :], x_v_).then_inc(x_in, 16)

            def load(pieces, l, j):
                for src, at, width in pieces:
                    n = src.shape[2]
                    dst = slot(j)[:, 0:4096].rearrange("p (k w) -> p k w", w=width)[:, :, at:at + n]
                    sp.dma_start(dst, src).then_inc(slot_full[j % NSLOT], 16)

            def layer_units(l):
                for j, pieces in enumerate(mixer_units(l)):
                    if j >= NSLOT:
                        sp.wait_ge(*multiplied(l, j - NSLOT))
                    elif l > 0:
                        sp.wait_ge(split_lo, 6 * NCH * (experts_before(l) - 1) + down_at((9, 10, 8)[j], 1) + 1)
                    load(pieces, l, j)
                    if l == 0 and j == 0:
                        sp.wait_ge(par_in, 16 * 9)

            def expert_chunks(l):
                if l % 2 == 0:
                    gate, up, down = (w[l // 2:l // 2 + 1] for w in (ffn_gate_d, ffn_up_d, ffn_down_d))
                else:
                    gate, up, down = (w[l // 2] for w in (moe_gate_d, moe_up_d, moe_down_d))
                gate = gate.rearrange("e (k p) (c f) -> e c p k f", p=P, f=FC)
                up = up.rearrange("e (k p) (c f) -> e c p k f", p=P, f=FC)
                down = down.rearrange("e (c k p) n -> e c p k n", p=P, k=FC // P)

                def expert(e, first):
                    def gate_up(c, s):
                        gu = ring[:, s * SLOT:s * SLOT + 4096].rearrange("p (k b f) -> p k b f", b=2, f=FC)
                        sp.dma_start(gu[:, :, 0, :], gate[e, c]).then_inc(slot_full[s], 16)
                        sp.dma_start(gu[:, :, 1, :], up[e, c]).then_inc(slot_full[s], 16)

                    def down_(c, s):
                        sp.dma_start(ring[:, s * SLOT + 4096:(s + 1) * SLOT].rearrange("p (k n) -> p k n", n=D),
                                     down[e, c]).then_inc(slot_full[s], 16)

                    def step(c, s):
                        i = isinstance(c, int)
                        if i and c + 1 < NSLOT:
                            free_gate_up(c + 1)
                        elif not i or c + 1 < NCH:
                            sp.wait_ge(split_lo, e * (6 * NCH) + gu_at(c + 1 - NSLOT, 3) + (first + 1))
                        if not i or c + 1 < NCH:
                            gate_up(c + 1, (s + 1) % NSLOT)
                        if i and c < NSLOT:
                            if not isinstance(e, int):
                                sp.wait_ge(split_lo, e * (6 * NCH) + (first - 6 * NCH + down_at((9, 10, 8)[c], 1) + 1))
                        else:
                            sp.wait_ge(split_lo, e * (6 * NCH) + down_at(c - NSLOT, 1) + (first + 1))
                        down_(c, s)

                    def free_gate_up(c):
                        sp.wait_ge(*multiplied(l, NUNIT - NSLOT + c))
                        if not isinstance(e, int):
                            sp.wait_ge(split_lo, e * (6 * NCH) + (first - 6 * NCH + gu_at((9, 10, 8)[c], 3) + 1))

                    free_gate_up(0)
                    gate_up(0, 0)
                    for c in range(NSLOT):
                        step(c, c)
                    loops = NCH // NSLOT - 1
                    with sp.Fori(0, loops - (NCH % NSLOT == 0)) as r:
                        for i in range(NSLOT):
                            step(r * NSLOT + (NSLOT + i), i)
                    for c in range(NSLOT * (loops + 1 - (NCH % NSLOT == 0)), NCH):
                        step(c, c % NSLOT)

                def one_pass(p):
                    with sp.Fori(0, NE) as e:
                        expert(e, 6 * NCH * (experts_before(l) + p * NE))

                if l % 2 == 0:
                    expert(0, 6 * NCH * experts_before(l))
                else:
                    moe_passes(sp, one_pass)

            for l in range(DEPTH):
                layer_units(l)
                expert_chunks(l)
            sp.wait_ge(fin_ready, 1)
            sp.dma_start(out_d[0].rearrange("(t p) n -> p t n", p=P), x[:, :, :]).then_inc(out_done, 16)
            sp.wait_ge(out_done, 16)

        @block.gpsimd
        def _(pool):
            chain = [0]

            def link(ins):
                chain[0] += 1
                ins.then_inc(pool_chain, 1)
                pool.wait_ge(pool_chain, chain[0])

            def keep(v, pattern, base, cm):
                link(nc.gpsimd.affine_select(out=v, in_=v, pattern=pattern, base=base, channel_multiplier=cm,
                                             compare_op=ALU.is_ge, fill=0.0))

            link(nc.gpsimd.memset(ident[:, :], 0.0))
            nc.gpsimd.affine_select(out=ident[:, :], in_=ident[:, :], pattern=[[-1, P]], base=0,
                                    channel_multiplier=1, compare_op=ALU.not_equal,
                                    fill=1.0).then_inc(consts, 1)
            rows = phase[:, 0:3 * P].rearrange("p (a n) -> p a n", a=3)
            for i, w in enumerate((norm_mix_d, norm_xa_d, norm_mem_d, norm_ffn_d)):
                pool.dma_start(rows[i * NG:(i + 1) * NG, 0, :],
                               w.rearrange("l (k p) -> (l k) p", p=P)).then_inc(par_in, 16)
            pool.dma_start(rows[64:96, 0, :], a_re_d.rearrange("l (t g) s -> (l t) (g s)", g=2)).then_inc(par_in, 16)
            pool.dma_start(rows[96:128, 0, :], a_im_d.rearrange("l (t g) s -> (l t) (g s)", g=2)).then_inc(par_in, 16)
            pool.dma_start(rows[0:96, 1, :], conv_d.rearrange("l i (j p) -> (l i j) p", p=P)).then_inc(par_in, 16)
            dtr = phase[:, 3 * P:3 * P + 2]
            pool.dma_start(dtr[96:128, :], log_dt_d.rearrange("l (t g) -> (l t) g", g=2)).then_inc(par_in, 16)
            pool.dma_start(rows[0:8, 2, :], ssm_d_d.rearrange("l (k p) -> (l k) p", p=P)).then_inc(par_in, 16)
            link(nc.gpsimd.memset(ones[:, :], 1.0))
            for i, e in enumerate((EPS, 4.0 * EPS, 1.0)):
                nc.gpsimd.memset(eps_col[:, i:i + 1], e)
            for j in range(MD // 2):
                nc.gpsimd.memset(inv_freq[:, j:j + 1], THETA ** (-2.0 * j / MD))
            link(nc.gpsimd.iota(steps[:, :], pattern=[[1, SEQ]], base=0, channel_multiplier=0,
                                allow_small_or_imprecise_dtypes=True))
            link(nc.gpsimd.iota(idx8[:, :], pattern=[[1, 8]], base=0, channel_multiplier=0,
                                allow_small_or_imprecise_dtypes=True))
            pool.wait_ge(par_in, 16 * 9)
            link(nc.gpsimd.tensor_copy(rows[96:128, 1, :].rearrange("p (g s) -> p g s", g=2),
                                       dtr[96:128, :].unsqueeze(2).to_broadcast([32, 2, 64])))
            nc.gpsimd.memset(st[:, :], 0.0).then_inc(consts, 1)
            for m in (b_mask, c_mask):
                link(nc.gpsimd.memset(m[:, :, :, :], 1.0))
            keep(b_mask[:, :, :, :], [[128, NQ], [-64, 8], [0, 16]], 0, 1)
            keep(b_mask[:, :, :, :], [[-128, NQ], [64, 8], [0, 16]], 63, -1)
            keep(c_mask[:, :, :, :], [[-32, NQ], [-16, 2], [0, 64]], 0, 1)
            keep(c_mask[:, :, :, :], [[32, NQ], [16, 2], [0, 64]], 15, -1)
            link(nc.gpsimd.memset(cum_mask[:, :], 1.0))
            keep(cum_mask[:, :], [[1, P]], 0, -1)
            cm2 = cum_mask[:, :].rearrange("p (a b) -> p a b", b=GL)
            keep(cm2, [[-GL, P // GL], [0, GL]], 0, 1)
            keep(cm2, [[GL, P // GL], [0, GL]], GL - 1, -1)
            link(nc.gpsimd.memset(before[:, :], 1.0))
            keep(before[:, :], [[1, P]], -1, -1)
            link(nc.gpsimd.memset(level_mask[:, :, :], 0.0))
            for k in range(6):
                b = 2 ** k
                q = level_mask[:, k, :].rearrange("p (a h b) -> p a h b", h=2, b=b)[:, :, 0, :]
                link(nc.gpsimd.memset(q, 1.0))
                keep(q, [[-2 * b, P // (2 * b)], [0, b]], -b, 1)
                keep(q, [[2 * b, P // (2 * b)], [0, b]], 2 * b - 1, -1)
            link(nc.gpsimd.memset(causal[:, :], 0.0))
            for at in (0, 2 * P):
                last = nc.gpsimd.affine_select(out=causal[:, at:at + P], in_=causal[:, at:at + P],
                                               pattern=[[-1, P]], base=0, channel_multiplier=1,
                                               compare_op=ALU.is_ge, fill=NEG)
            last.then_inc(consts, 1)

            def angle_table(l, q):
                n = NQ * l + q
                if n >= 1:
                    pool.wait_ge(tab_sin, n)
                a3 = ang.rearrange("p (c n) -> p c n", n=SEQ)
                th = THR[:, l * NS5 + NQ * q:l * NS5 + NQ * (q + 1)].unsqueeze(2).to_broadcast([P, NQ, SEQ])
                sx = steps[:, :].unsqueeze(1).to_broadcast([P, NQ, SEQ])
                link(nc.gpsimd.tensor_tensor(a3, th, sx, ALU.mult))
                link(nc.gpsimd.tensor_scalar(turns, ang, 1.0 / TWO_PI, MAGIC, ALU.mult, ALU.add))
                link(nc.gpsimd.tensor_scalar(turns, turns, -MAGIC, None, ALU.add))
                link(nc.gpsimd.tensor_scalar(s_half, turns, C1, None, ALU.mult))
                link(nc.gpsimd.tensor_tensor(ang, ang, s_half, ALU.subtract))
                link(nc.gpsimd.tensor_scalar(s_half, turns, C2, None, ALU.mult))
                link(nc.gpsimd.tensor_tensor(ang, ang, s_half, ALU.subtract))
                nc.gpsimd.tensor_scalar(ang, ang, PI_IN, -PI_IN, ALU.min, ALU.max).then_inc(tab_ang, 1)

            def pad_b(l, q):
                n = 2 * (NQ * l + q)
                if n >= 1:
                    pool.wait_ge(pad_ps, n)
                for c in range(2):
                    src = b_bar[:, c, NQ * q:NQ * (q + 1), :].unsqueeze(2).to_broadcast([P, NQ, 8, 16])
                    last = nc.gpsimd.tensor_tensor(pads[:, c, :].rearrange("p (t g n) -> p t g n", t=NQ, g=8),
                                                   src, b_mask[:, :, :, :], ALU.mult)
                    last.then_inc(pad_ready, 1)

            def pad_c(l, q):
                pool.wait_ge(pad_ps, 2 * (NQ * l + q) + 1)
                for c in range(2):
                    src = c_nat[:, c, q, :].unsqueeze(1).unsqueeze(1).to_broadcast([P, NQ, 2, 64])
                    last = nc.gpsimd.tensor_tensor(pads[:, c, :].rearrange("p (t g n) -> p t g n", t=NQ, g=2),
                                                   src, c_mask[:, :, :, :], ALU.mult)
                    last.then_inc(pad_ready, 1)

            for l in range(DEPTH):
                if l > 0:
                    pool.wait_ge(y_added, (l + 1) // 2)
                if l > 0:
                    pool.wait_ge(hT_ready, 1 + 3 * l)
                pool.wait_ge(par_ready, 1)
                pool.dma_start(b_nat[:, 0], b_re_d[l].rearrange("(t g) s n -> (g s) t n", g=2)).then_inc(bc_nat_in, 16)
                pool.dma_start(b_nat[:, 1], b_im_d[l].rearrange("(t g) s n -> (g s) t n", g=2)).then_inc(bc_nat_in, 16)
                pool.dma_start(c_nat[:, 0], c_re_d[l].rearrange("(q g) n s -> (g n) q s", q=NQ)).then_inc(bc_nat_in, 16)
                pool.dma_start(c_nat[:, 1], c_im_d[l].rearrange("(q g) n s -> (g n) q s", q=NQ)).then_inc(bc_nat_in, 16)
                if l == 0:
                    pool.wait_ge(s5_const, 1)
                for q in range(NQ):
                    angle_table(l, q)
                    if q == 0:
                        pool.wait_ge(bc_nat_in, 64 * (l + 1))
                        pool.wait_ge(b_bar_ready, l + 1)
                    pad_b(l, q)
                    pad_c(l, q)
                pool.wait_ge(glu_ps, 4 * (l + 1))
                for t in range(NT):
                    for m in (Xi, Zi):
                        last = nc.gpsimd.tensor_copy(m[:, t], ident[:, :].unsqueeze(1).to_broadcast([P, GH, P]))
                        last.then_inc(xz_init, 1)
                for k in range(6):
                    for t in range(NT):
                        n = (6 * l + k) * NT + t
                        if k > 0:
                            pool.wait_ge(w_ps, n - NT + 1)
                        else:
                            pool.wait_ge(a_ready, NT * l + t + 1)
                        nc.gpsimd.tensor_tensor(M_lvl[:, t], A_low[:, t],
                                                level_mask[:, k, :].unsqueeze(1).to_broadcast([P, GH, P]),
                                                ALU.mult).then_inc(m_ready, 1)

        @block.scalar
        def _(act):
            chain = [0]

            def link(ins):
                chain[0] += 1
                ins.then_inc(act_chain, 1)
                act.wait_ge(act_chain, chain[0])

            act.dma_start(h_tok, mem_d[0].rearrange("(t p) n -> p t n", p=P)).then_inc(mem_in, 16)
            with nc.allow_non_contiguous_dma("one position per partition"):
                act.dma_start(pos_i[:, :], positions_d[0].rearrange("(t p) -> p t", p=P)).then_inc(tables_in, 16)
            for l in range(DEPTH):
                act.dma_start(small_bc[:, l, 0, :], a_log_d[l:l + 1, :].to_broadcast([P, GH])).then_inc(tables_in, 16)
                act.dma_start(small_bc[:, l, 1, :], dt_bias_d[l:l + 1, :].to_broadcast([P, GH])).then_inc(tables_in, 16)
                act.dma_start(gnorm_bc[:, l, :], gdn_norm_d[l:l + 1, :].to_broadcast([P, GD])).then_inc(tables_in, 16)
            act.dma_start(router_w[:, :, :], router_d[0].rearrange("(k p) n -> p k n", p=P)).then_inc(tables_in, 16)

            def load_ab(l):
                act.dma_start(ab_w[:, :, :], w_in_d[l].rearrange("(k p) n -> p k n", p=P)
                              [:, :, IN_AB:IN_AB + 2 * GH]).then_inc(ab_in, 16)

            load_ab(0)

            def sum_squares(src, n):
                for t in range(NT):
                    nc.scalar.activation(hT[:, :, :].rearrange("p k n -> p (k n)")[:, t * D:(t + 1) * D],
                                         src[:, t, :], ACT.Square,
                                         accum_out=ss[:, t:t + 1]).then_inc(norm_sq, 1)
                act.wait_ge(norm_sq, NT * (n + 1))
                link(nc.scalar.activation(ss, ss, ACT.Ln, scale=1.0 / D, bias=eps_col[:, 0:1]))
                nc.scalar.activation(rstd, ss, ACT.Exp, scale=-0.5).then_inc(norm_ss, 1)

            def evac_norm(n, dst, gain, at, done):
                for b in range(4):
                    act.wait_ge(norm_ps, 4 * n + b + 1)
                    for i in range(2):
                        k = 2 * b + i
                        if gain is None:
                            last = nc.scalar.activation(dst[:, k, :], B[4 + b][:, i * SEQ:(i + 1) * SEQ], ACT.Copy)
                        else:
                            last = nc.scalar.activation(dst[:, k, :], B[4 + b][:, i * SEQ:(i + 1) * SEQ], ACT.Copy,
                                                        scale=gain[:, at + k:at + k + 1])
                last.then_inc(done, 1)

            def split_group(at, buf, s, i):
                if not (isinstance(at, int) and at < NGRP):
                    act.wait_ge(split_used, at - (NGRP - 1))
                nc.scalar.activation(split[buf][:, HI, :], raw_group(s, i), ACT.Copy).then_inc(split_hi, 1)

            act.wait_ge(par_ps, 1)
            nc.scalar.activation(params[:, 0:2 * P + 8], B[0][:, 0:2 * P + 8], ACT.Copy).then_inc(par_ready, 1)
            act.wait_ge(mem_in, 16)
            act.wait_ge(consts, 2)
            sum_squares(h_tok, 0)
            evac_norm(0, memT[:, :, :], None, 0, hT_ready)
            act.wait_ge(x_in, 16)
            sum_squares(x[:, :, :], 1)
            act.wait_ge(par_ready, 1)
            evac_norm(1, hT[:, :, :], gain_mix, 0, hT_ready)

            nc.scalar.activation(s5c[:, 4, :], p_dt, ACT.Exp).then_inc(s5_dt, 1)
            act.wait_ge(s5_ang, 1)
            nc.scalar.activation(DEC, s5c[:, 5, :], ACT.Exp)
            nc.scalar.activation(s5c[:, 6, :], THR, ACT.Sin)
            nc.scalar.activation(s5c[:, 7, :], THR, ACT.Sin, scale=0.5).then_inc(s5_sin, 1)
            act.wait_ge(rot_ang, 1)
            link(nc.scalar.activation(sinr[:, :, :], cosr[:, :, :], ACT.Sin))
            nc.scalar.activation(cosr[:, :, :], cosr[:, :, :], ACT.Sin, scale=0.5).then_inc(rot_sin, 1)
            act.wait_ge(tables_in, TABLES)

            def table(l, q):
                n = NQ * l + q
                if n >= 2:
                    act.wait_ge(h_rot, NS5 * l + NQ * (q - 2) + NQ if q >= 2 else NS5 * l)
                act.wait_ge(tab_ang, n + 1)
                T = tab[q % 2]
                nc.scalar.activation(T[:, :, 1, :], ang.rearrange("p (c n) -> p c n", n=SEQ), ACT.Sin)
                link(nc.scalar.activation(T[:, :, 0, :], ang.rearrange("p (c n) -> p c n", n=SEQ), ACT.Sin, scale=0.5))
                nc.scalar.activation(T[:, :, 0, :], T[:, :, 0, :], ACT.Square).then_inc(tab_sin, 1)

            def bct_evac(l, q):
                for half in range(2):
                    n = 2 * (NQ * l + q) + half
                    act.wait_ge(pad_ps, n + 1)
                    if NQ * l + q >= 2 and half == 0:
                        act.wait_ge(y_read, NQ * (NQ * l + q - 1))
                    for c in range(2):
                        last = nc.scalar.activation(bct[q % 2][2 * half + c].rearrange("p t n -> p (t n)"),
                                                    B[6 + c][:, :], ACT.Copy,
                                                    scale=-1.0 if (half == 1 and c == 1) else 1.0)
                    last.then_inc(bct_ready, 1)

            for l in range(DEPTH):
                if l > 0:
                    n = 1 + 3 * l
                    sum_squares(x[:, :, :], n)
                    evac_norm(n, hT[:, :, :], gain_mix, l * KD, hT_ready)
                def ws_copy(w):
                    for b in range(2):
                        act.wait_ge(ws_ready, 8 * l + 2 * w + b + 1)
                        src = B[(2 if w == 2 else 0) + b][:, :].rearrange("p (c n) -> p c n", n=SEQ)
                        dst = (uT[:, 2 * b:2 * b + 2, :] if w == 0
                               else raw[:, 4 * (w - 1) + 2 * b:4 * (w - 1) + 2 * b + 2, 3:RAW])
                        nc.scalar.activation(dst, src, ACT.Copy).then_inc(ws_evac, 1)

                ws_copy(0)
                act.wait_ge(ab_ps, l + 1)
                nc.scalar.activation(ab, B[4][:, 0:16], ACT.Copy).then_inc(ab_sb, 1)
                if l + 1 < DEPTH:
                    act.wait_ge(ab_ps, l + 1)
                    load_ab(l + 1)
                table(l, 0)
                bct_evac(l, 0)
                for f in range(4, 20):
                    i = f - 4
                    q, t = f // 2, f % 2
                    act.wait_ge(fill_ready, 20 * l + f + 1)
                    if q == 2:
                        nc.scalar.activation(v_tok[:, t, :], B[t][:, :], ACT.Copy).then_inc(fill_evac, 1)
                    elif q == 3:
                        nc.scalar.activation(z_tok[:, t, :], B[t][:, :], ACT.Copy).then_inc(fill_evac, 1)
                    else:
                        nc.scalar.activation(gates[:, t, (q - 4) * 512:(q - 3) * 512], B[t][:, :], ACT.Tanh,
                                             scale=0.5).then_inc(fill_evac, 1)
                    if i % NQ == 1 and i // NQ + 1 < NQ:
                        bct_evac(l, i // NQ + 1)
                    if i % NQ == 0 and i // NQ + 1 < NQ:
                        table(l, i // NQ + 1)
                for q in range(NQ):
                    act.wait_ge(gel_in, NQ * l + q + 1)
                    nc.scalar.activation(y5b[:, q, :], y5b[:, q, :], ACT.Tanh, scale=GELU_C).then_inc(gel_t, 1)
                act.wait_ge(y_ready, l + 1)
                for w in range(1, 4):
                    ws_copy(w)
                for i in range(4):
                    act.wait_ge(mtr_ps, 4 * l + i + 1)
                    dst = (mqT, mkT)[i // 2][:, :, (i % 2) * P:(i % 2 + 1) * P]
                    nc.scalar.activation(dst, B[4 + i][:, :].rearrange("p (k n) -> p k n", n=P),
                                         ACT.Copy).then_inc(mtr_ready, 1)

                def moba_exp(h):
                    n = MH * l + h
                    act.wait_ge(ms_neg, n + 1)
                    p = mp_[h % 2]
                    o = 2 * (h % 2)
                    nc.scalar.activation(p[:, 0:P], p[:, 0:P], ACT.Exp, bias=nm[:, o:o + 1], scale=MD ** -0.5,
                                         accum_out=rs[:, o:o + 1])
                    nc.scalar.activation(p[:, P:3 * P], p[:, P:3 * P], ACT.Exp, bias=nm[:, o + 1:o + 2],
                                         scale=MD ** -0.5, accum_out=rs[:, o + 1:o + 2]).then_inc(ms_exp, 1)

                def moba_pT(h):
                    n = MH * l + h
                    act.wait_ge(ms_tr, n + 1)
                    if n >= 2:
                        act.wait_ge(ms_o, n - 1)
                    nc.scalar.activation(mpT[h % 2], B[4 + h % 2][:, 0:3 * P], ACT.Copy).then_inc(ms_pT, 1)

                def moba_oT(j):
                    act.wait_ge(ms_o, MH * l + 2 * j + 2)
                    nc.scalar.activation(m_oT[:, j, :], B[6 + j % 2][:, 0:SEQ], ACT.Copy).then_inc(ms_oT, 1)

                def glu_tanh(i):
                    act.wait_ge(glu_ps, 4 * l + i + 1)
                    if i >= 2:
                        act.wait_ge(glu_used, 4 * l + i - 1)
                    nc.scalar.activation(glu_t[i % 2], B[1][:, :], ACT.Tanh, scale=0.5).then_inc(glu_th, 1)

                for s in range(MH + 2):
                    if s < MH:
                        moba_exp(s)
                    if 2 <= s <= MH and s % 2 == 0:
                        glu_tanh(s // 2 - 1)
                    if 1 <= s <= MH:
                        moba_pT(s - 1)
                    if s >= 3 and s % 2 == 1:
                        moba_oT((s - 3) // 2)
                def first_taps(js):
                    for j in js:
                        nc.scalar.activation(cv[:, j, :], raw[:, j, 0:SEQ], ACT.Copy,
                                             scale=p_conv[:, 48 * l + j:48 * l + j + 1]).then_inc(cv_tap, 1)

                def conv_tanh(i):
                    act.wait_ge(cv_pre, 3 * l + i + 1)
                    tmp = (A_low, M_lvl, W_lvl)[i].rearrange("p t h n -> p (t h n)")
                    nc.scalar.activation(tmp, cv[:, 4 * i:4 * i + 4, :].rearrange("p c n -> p (c n)"), ACT.Tanh,
                                         scale=0.5).then_inc(cv_th, 1)

                act.wait_ge(ms_ready, MH * (l + 1))
                first_taps(range(8))
                act.wait_ge(g_z, l + 1)
                nc.scalar.activation(ealog, small_bc[:, l, 0, :], ACT.Exp)
                link(nc.scalar.activation(gate_e, gate_e, ACT.Exp, scale=-1.0))
                nc.scalar.activation(gate_e, gate_e, ACT.Ln, bias=eps_col[:, 2:3]).then_inc(g_ln, 1)
                nc.scalar.activation(beta.rearrange("p (t h) -> p t h", t=NT),
                                     ab.rearrange("p (t c h) -> p t c h", t=NT, c=2)[:, :, 1, :],
                                     ACT.Tanh, scale=0.5).then_inc(gate_tanh, 1)
                act.wait_ge(up_ps, 8 * l + 4)
                first_taps(range(8, 12))
                for i in range(3):
                    conv_tanh(i)
                for i in range(4):
                    act.wait_ge(cv_ready, 3 * l + i // 2 + 1)
                    tmp = (DTm, Dcl)[i // 2].rearrange("p t h n -> p (t h n)")[:, (i % 2) * 512:(i % 2 + 1) * 512]
                    nc.scalar.activation(tmp, cv[:, 2 * i:2 * i + 2, :].rearrange("p c n -> p (c n)"),
                                         ACT.Square).then_inc(cv_sq, 1)
                for i in range(4):
                    act.wait_ge(cv_ss, 4 * l + i + 1)
                    r_ = rq[i].rearrange("p t h n -> p (t h n)")[:, 0:512]
                    last = nc.scalar.activation(r_, B[4 + i][:, :], ACT.Ln, bias=eps_col[:, 1:2])
                link(last)
                for i in range(4):
                    r_ = rq[i].rearrange("p t h n -> p (t h n)")[:, 0:512]
                    nc.scalar.activation(r_, r_, ACT.Exp, scale=-0.5).then_inc(cv_rs, 1)
                act.wait_ge(gc_sb, l + 1)
                nc.scalar.activation(bexp, gcum, ACT.Exp).then_inc(g_bexp, 1)
                for t in range(NT):
                    act.wait_ge(dec_in, NT * l + t + 1)
                    nc.scalar.activation(e_row[:, t], B[2 + t][:, :].rearrange("p (h n) -> p h n", h=GH),
                                         ACT.Exp).then_inc(dec_ready, 1)
                    nc.scalar.activation(dec[:, t], Dcl[:, t], ACT.Exp, scale=-1.0).then_inc(dec_ready, 1)
                    nc.scalar.activation(decT[:, t], DTm[:, t], ACT.Exp).then_inc(dec_ready, 1)
                for t in range(NT):
                    act.wait_ge(kv_ps, 4 * l + t + 1)
                    nc.scalar.activation(k_tok[:, t], B[4 + t][:, :].rearrange("p (h n) -> p h n", h=GH),
                                         ACT.Copy).then_inc(kv_evac, 1)
                act.wait_ge(row_ps, NT * (l + 1))
                nc.scalar.activation(gdiag.rearrange("p t h n -> p (t h n)"),
                                     z_tok[:, :, :].rearrange("p t n -> p (t n)"), ACT.Tanh,
                                     scale=0.5).then_inc(gate_tanh, 1)
                for k in range(6):
                    for t in range(NT):
                        n = (6 * l + k) * NT + t
                        act.wait_ge(w_ps, n + 1)
                        nc.scalar.activation(W_lvl[:, t], B[t][:, :].rearrange("p (h n) -> p h n", h=GH),
                                             ACT.Copy).then_inc(w_evac, 1)
                for t in range(NT):
                    act.wait_ge(uw_ps, NT * l + t + 1)
                    nc.scalar.activation(wT[:, t], B[t][:, :].rearrange("p (h n) -> p h n", h=GH),
                                         ACT.Copy).then_inc(w_done, 1)
                for c in range(NCHUNK):
                    rows_ = slice((c % 2) * GL, (c % 2 + 1) * GL)
                    act.wait_ge(o_ps, NCHUNK * l + c + 1)
                    nc.scalar.activation(o_tok[rows_, c // 2], B[5 + c % 2][rows_, :].rearrange("p (h n) -> p h n", h=GH),
                                         ACT.Copy).then_inc(o_evac, 1)
                act.wait_ge(og_ss, l + 1)
                link(nc.scalar.activation(gate_z, gate_z, ACT.Ln, scale=1.0 / GD, bias=eps_col[:, 0:1]))
                nc.scalar.activation(gate_z, gate_z, ACT.Exp, scale=-0.5).then_inc(og_rs, 1)
                for t in range(NT):
                    act.wait_ge(og_ps, NT * l + t + 1)
                    nc.scalar.activation(g_oT[:, :, t * P:(t + 1) * P], B[4 + t][:, :].rearrange("p (k n) -> p k n", n=P),
                                         ACT.Copy).then_inc(og_T, 1)
                for b in range(4):
                    act.wait_ge(mg_ps, 4 * l + b + 1)
                    nc.scalar.activation(hT[:, 2 * b:2 * b + 2, :], B[4 + b][:, :].rearrange("p (c n) -> p c n", n=SEQ),
                                         ACT.Copy).then_inc(mg_T, 1)
                for k in range(KD):
                    last = nc.scalar.activation(memnT[:, k, :], memT[:, k, :], ACT.Copy,
                                                scale=gain_mem[:, l * KD + k:l * KD + k + 1])
                last.then_inc(memn_ready, 1)
                n = 2 + 3 * l
                act.wait_ge(wo_used, 4 * (l + 1))
                sum_squares(x[:, :, :], n)
                for b in range(2):
                    act.wait_ge(xk_ps, 6 * l + b + 1)
                    nc.scalar.activation(xkT[:, 2 * b:2 * b + 2, :], B[2 + b][:, :].rearrange("p (c n) -> p c n", n=SEQ),
                                         ACT.Copy).then_inc(xk_sb, 1)
                for b in range(2):
                    act.wait_ge(xk_ps, 6 * l + 2 + b + 1)
                    nc.scalar.activation(x_v[:, b, :], B[b][:, :], ACT.Copy).then_inc(xk_sb, 1)
                evac_norm(n, hT[:, :, :], gain_xa, l * KD, hT_ready)
                for b in range(2):
                    act.wait_ge(xk_ps, 6 * l + 4 + b + 1)
                    nc.scalar.activation(xqT[:, 2 * b:2 * b + 2, :], B[b][:, :].rearrange("p (c n) -> p c n", n=SEQ),
                                         ACT.Copy).then_inc(xk_sb, 1)

                def xa_exp(h):
                    n_ = XH * l + h
                    act.wait_ge(xs_neg, n_ + 1)
                    if n_ >= 2:
                        act.wait_ge(xs_tr, n_ - 1)
                    for t in range(NT):
                        o = 2 * (h % 2) + t
                        last = nc.scalar.activation(xp[h % 2][:, t, :], B[2 + h % 2][:, t * SEQ:(t + 1) * SEQ], ACT.Exp,
                                                    bias=nm[:, o:o + 1], scale=XD ** -0.5, accum_out=rs[:, o:o + 1])
                    last.then_inc(xs_exp, 1)

                def xa_pT(h):
                    n_ = XH * l + h
                    act.wait_ge(xs_tr, n_ + 1)
                    if n_ >= 2:
                        act.wait_ge(xs_o, n_ - 1)
                    nc.scalar.activation(xpT[h % 2], B[4 + h % 2][:, :].rearrange("p (c n) -> p c n", n=SEQ),
                                         ACT.Copy).then_inc(xs_pT, 1)

                def xa_oT(h):
                    act.wait_ge(xs_o, XH * l + h + 1)
                    nc.scalar.activation(x_oT[:, h, :], B[6 + h % 2][:, 0:SEQ], ACT.Copy).then_inc(xs_oT, 1)

                for s in range(XH + 2):
                    if s < XH:
                        xa_exp(s)
                    if 1 <= s <= XH:
                        xa_pT(s - 1)
                    if s >= 2:
                        xa_oT(s - 2)
                n = 3 + 3 * l
                if l % 2 == 0:
                    act.wait_ge(slot_full[0], slot_after_chunk(l, 0, 0, 0))
                    for i in range(4):
                        split_group(6 * NCH * experts_before(l) + gu_at(0, i), gu_buf(0, i), 0, i)
                act.wait_ge(xo_used, 4 * (l + 1))
                sum_squares(x[:, :, :], n)
                if l % 2 == 0:
                    for b in range(4):
                        act.wait_ge(norm_ps, 4 * n + b + 1)
                        for i in range(2):
                            k = 2 * b + i
                            last = nc.scalar.activation(fx[:, HI, k, :], B[4 + b][:, i * SEQ:(i + 1) * SEQ], ACT.Copy,
                                                        scale=gain_ffn[:, l * KD + k:l * KD + k + 1])
                        last.then_inc(*((fx_hi, 1) if b < 3 else (hT_ready, 1)))
                else:
                    evac_norm(n, hT[:, :, :], gain_ffn, l * KD, hT_ready)
                    act.wait_ge(rl_d, l // 2 + 1)
                    nc.scalar.activation(r_w[:, :, 1:2], r_w[:, :, 0:1], ACT.Exp).then_inc(rl_e, 1)
                base = acts_before(l)
                g0 = 6 * NCH * experts_before(l)
                if l % 2 == 0:
                    def tail(c):
                        for t in range(NT):
                            act.wait_ge(act_tr, c * NT + (base + t + 1))
                            nc.scalar.activation(f_actT[:, HI, :, t * P:(t + 1) * P],
                                                 B[2 + t][:, 0:2 * P].rearrange("p (k n) -> p k n", n=P),
                                                 ACT.Copy).then_inc(actT_hi, 1)

                    def chunk(c, s):
                        head = isinstance(c, int) and c == 0
                        if not head:
                            act.wait_ge(slot_full[s], full_at(l, c, s))
                            for i in range(4):
                                split_group(gu_at(c, i) + g0, gu_buf(c, i), s, i)
                            tail(c - 1)
                            for i in range(2):
                                split_group(down_at(c - 1, i) + g0, down_buf(1, i), (s - 1) % NSLOT, 4 + i)
                        act.wait_ge(split_used, gu_at(c, 3) + (g0 + 1))
                        for t in range(NT):
                            if not (head and l == 0):
                                act.wait_ge(gu_a, c * NT + (base + t + 1 - NT))
                            nc.scalar.activation(f_th[t], B[t][:, 0:FC], ACT.Tanh, scale=0.5).then_inc(gu_th, 1)

                    chunks_of_expert(act, chunk, 2)
                    for i in range(2):
                        c = NCH - 1
                        split_group(down_at(c, i) + g0, down_buf(c, i), c % NSLOT, 4 + i)
                    tail(NCH - 1)
                    act.wait_ge(y_added, l // 2 + 1)
                else:
                    act.dma_start(gain_bc, norm_ffn_d[l:l + 1, :].to_broadcast([P, D])).then_inc(gain_in, 16)

                    def take_he(k):
                        act.wait_ge(he_ps, k)
                        for b in range(2):
                            nc.scalar.activation(fx_e[:, HI, 4 * b:4 * b + 4, 0:P],
                                                 B[6 + b][:, :].rearrange("p (k n) -> p k n", n=P),
                                                 ACT.Copy).then_inc(fx_hi, 1)

                    def one_pass(p):
                        ab_, kb = base + p * NE * NCH, p * (NE + 1)
                        gb = g0 + 6 * NCH * p * NE
                        take_he(kb + 1)

                        def take_y(e):
                            act.wait_ge(split_used, e * (6 * NCH) + gb)
                            for b in range(2):
                                last = nc.scalar.activation(y_e[:, b * 512:(b + 1) * 512], B[4 + b][:, :], ACT.Copy)
                            last.then_inc(ye_ready, 1)

                        with act.Fori(0, NE) as e:
                            def tail(c):
                                act.wait_ge(act_tr, e * NCH + c + (ab_ + 1))
                                nc.scalar.activation(f_actT_e[:, HI, :, :],
                                                     B[3][:, 0:2 * P].rearrange("p (k n) -> p k n", n=P),
                                                     ACT.Copy).then_inc(actT_hi, 1)

                            def chunk(c, s):
                                head = isinstance(c, int) and c == 0
                                ge = e * (6 * NCH) + gb
                                act.wait_ge(slot_full[s], full_at(l, c, s, e + p * NE))
                                for i in range(4):
                                    split_group(ge + gu_at(c, i), gu_buf(c, i), s, i)
                                if head:
                                    take_y(e)
                                else:
                                    tail(c - 1)
                                    for i in range(2):
                                        split_group(ge + down_at(c - 1, i), down_buf(1, i), (s - 1) % NSLOT, 4 + i)
                                act.wait_ge(split_used, ge + gu_at(c, 3) + 1)
                                act.wait_ge(gu_a, e * NCH + c + ab_)
                                nc.scalar.activation(f_th[0], B[s][:, 0:FC], ACT.Tanh, scale=0.5).then_inc(gu_th, 1)
                                if head:
                                    act.wait_ge(sm_ps, e + (NE * p + 1))
                                    nc.scalar.activation(scatter_m, B[3][:, 2 * P:4 * P], ACT.Copy).then_inc(sm_ready, 1)
                                if isinstance(c, int) and c == NCH - 1:
                                    take_he(e + (kb + 2))
                            chunks_of_expert(act, chunk)
                            for i in range(2):
                                c = NCH - 1
                                split_group(e * (6 * NCH) + (gb + down_at(c, i)), down_buf(c, i), c % NSLOT, 4 + i)
                            tail(NCH - 1)
                        take_y(NE)
                        act.wait_ge(sc_used, 4 * (NE + 1) * (p + 1))
                    moe_passes(act, one_pass)
            act.dma_start(gain_out, norm_final_d.rearrange("(a n) -> a n", a=1).to_broadcast([P, D])).then_inc(gain_in, 16)
            sum_squares(x[:, :, :], NNORM)

        @block.vector
        def _(dve):
            V = nc.vector
            chain = [0]

            def link(ins):
                chain[0] += 1
                ins.then_inc(dve_chain, 1)
                dve.wait_ge(dve_chain, chain[0])

            def normalise(src, dst, n):
                dve.wait_ge(norm_ss, n + 1)
                for t in range(NT):
                    V.tensor_scalar(dst[:, t, :], src[:, t, :], rstd[:, t:t + 1], None, ALU.mult).then_inc(norm_h, 1)

            def reduce_angle(a, tmp):
                link(V.tensor_scalar(tmp, a, 1.0 / TWO_PI, MAGIC, ALU.mult, ALU.add))
                link(V.tensor_scalar(tmp, tmp, -MAGIC, None, ALU.add))
                link(V.scalar_tensor_tensor(a, tmp, -C1, a, ALU.mult, ALU.add))
                link(V.scalar_tensor_tensor(a, tmp, -C2, a, ALU.mult, ALU.add))
                return V.tensor_scalar(a, a, PI_IN, -PI_IN, ALU.min, ALU.max)

            def split_rest(at, buf, s, i):
                dve.wait_ge(split_hi, at + 1)
                V.tensor_tensor(split[buf][:, LO, :], raw_group(s, i), split[buf][:, HI, :].bitcast(F32),
                                ALU.subtract).then_inc(split_lo, 1)

            dve.wait_ge(mem_in, 16)
            normalise(h_tok, h_tok, 0)
            dve.wait_ge(x_in, 16)
            dve.wait_ge(norm_ps, 4)
            normalise(x[:, :, :], h_tok, 1)
            c_ = [s5c[:, i, :] for i in range(14)]
            dve.wait_ge(par_ready, 1)
            dve.wait_ge(s5_dt, 1)
            V.tensor_tensor(c_[5], c_[4], p_are, ALU.mult)
            link(V.tensor_tensor(THR, c_[4], p_aim, ALU.mult))
            reduce_angle(THR, c_[8]).then_inc(s5_ang, 1)
            dve.wait_ge(tables_in, TABLES)
            link(V.tensor_copy(pos_f[:, :], pos_i[:, :]))
            dve.wait_ge(consts, 2)
            for t in range(NT):
                link(V.tensor_scalar(cosr[:, t, :], inv_freq[:, :], pos_f[:, t:t + 1], None, ALU.mult))
            reduce_angle(cosr[:, :, :], sinr[:, :, :]).then_inc(rot_ang, 1)
            dve.wait_ge(s5_sin, 1)
            link(V.tensor_tensor(c_[7], c_[7], c_[7], ALU.mult))
            link(V.tensor_scalar(c_[7], c_[7], -2.0, 1.0, ALU.mult, ALU.add))
            link(V.tensor_tensor(c_[7], c_[7], DEC, ALU.mult))
            link(V.tensor_scalar(c_[7], c_[7], -1.0, None, ALU.add))
            link(V.tensor_tensor(c_[6], c_[6], DEC, ALU.mult))
            V.tensor_tensor(c_[8], p_are, p_are, ALU.mult)
            link(V.tensor_tensor(c_[9], p_aim, p_aim, ALU.mult))
            link(V.tensor_tensor(c_[8], c_[8], c_[9], ALU.add))
            link(V.reciprocal(c_[8], c_[8]))
            V.tensor_tensor(c_[9], c_[7], p_are, ALU.mult)
            V.tensor_tensor(c_[10], c_[6], p_aim, ALU.mult)
            V.tensor_tensor(c_[11], c_[6], p_are, ALU.mult)
            link(V.tensor_tensor(c_[12], c_[7], p_aim, ALU.mult))
            V.tensor_tensor(c_[9], c_[9], c_[10], ALU.add)
            link(V.tensor_tensor(c_[11], c_[11], c_[12], ALU.subtract))
            V.tensor_tensor(BCR, c_[9], c_[8], ALU.mult)
            V.tensor_tensor(BCI, c_[11], c_[8], ALU.mult).then_inc(s5_const, 1)
            dve.wait_ge(rot_sin, 1)
            link(V.tensor_tensor(cosr[:, :, :], cosr[:, :, :], cosr[:, :, :], ALU.mult))
            link(V.tensor_scalar(cosr[:, :, :], cosr[:, :, :], -2.0, 1.0, ALU.mult, ALU.add))
            dve.wait_ge(s5_const, 1)

            for l in range(DEPTH):
                if l > 0:
                    normalise(x[:, :, :], h_tok, 1 + 3 * l)
                dve.wait_ge(bc_nat_in, 64 * (l + 1))
                cr = BCR[:, l * NS5:(l + 1) * NS5].unsqueeze(2).to_broadcast([P, NS5, 16])
                ci = BCI[:, l * NS5:(l + 1) * NS5].unsqueeze(2).to_broadcast([P, NS5, 16])
                tb = [wk5[i][:, 0, :].rearrange("p (t n) -> p t n", n=16) for i in range(4)]
                V.tensor_tensor(tb[0], b_nat[:, 0], cr, ALU.mult)
                V.tensor_tensor(tb[1], b_nat[:, 1], ci, ALU.mult)
                V.tensor_tensor(tb[2], b_nat[:, 0], ci, ALU.mult)
                link(V.tensor_tensor(tb[3], b_nat[:, 1], cr, ALU.mult))
                link(V.tensor_tensor(b_bar[:, 0], tb[0], tb[1], ALU.subtract))
                V.tensor_tensor(b_bar[:, 1], tb[2], tb[3], ALU.add).then_inc(b_bar_ready, 1)
                dve.wait_ge(b_bar_ready, l + 1)
                for f in range(4):
                    c, t = f // 2, f % 2
                    dve.wait_ge(fill_ready, 20 * l + f + 1)
                    src = B[t][:, :].rearrange("p (h c n) -> p h c n", c=2, n=MD // 2)
                    dst = qk[:, c, t, :].rearrange("p (h c n) -> p h c n", c=2, n=MD // 2)
                    cs = cosr[:, t, :].unsqueeze(1).to_broadcast([P, MH, MD // 2])
                    sn = sinr[:, t, :].unsqueeze(1).to_broadcast([P, MH, MD // 2])
                    tmp = wk5[3 + f % 2].rearrange("p a b -> p (a b)").rearrange("p (h c n) -> p h c n", c=2, n=MD // 2)
                    for i in range(2):
                        V.tensor_tensor(dst[:, :, i, :], src[:, :, i, :], cs, ALU.mult)
                    V.tensor_tensor(tmp[:, :, 0, :], src[:, :, 1, :], sn, ALU.mult)
                    link(V.tensor_tensor(tmp[:, :, 1, :], src[:, :, 0, :], sn, ALU.mult))
                    V.tensor_tensor(dst[:, :, 0, :], dst[:, :, 0, :], tmp[:, :, 0, :], ALU.subtract)
                    V.tensor_tensor(dst[:, :, 1, :], dst[:, :, 1, :], tmp[:, :, 1, :], ALU.add).then_inc(rope_done, 1)
                dve.wait_ge(rope_done, 4 * (l + 1))
                for i in range(NS5):
                    q, n = i // NQ, NS5 * l + i
                    T = tab[q % 2][:, i % NQ]
                    if i % NQ == 0:
                        dve.wait_ge(tab_sin, NQ * l + q + 1)
                        cosn = tab[q % 2][:, :, 0, :]
                        link(V.tensor_scalar(cosn, cosn, -2.0, 1.0, ALU.mult, ALU.add))
                    dve.wait_ge(bu_ready, n + 1)
                    bu = B[2 + n % 2][:, :].rearrange("p (c n) -> p c n", n=SEQ)
                    cs2 = T[:, 0, :].unsqueeze(1).to_broadcast([P, 2, SEQ])
                    sn = T[:, 1, :]
                    m1, m2, gin = wk5[0], wk5[1], wk5[2]
                    if n >= 1:
                        dve.wait_ge(h_rot, n)
                    V.tensor_tensor(m1, bu, cs2, ALU.mult)
                    V.tensor_tensor(m2[:, 0, :], bu[:, 1, :], sn, ALU.mult)
                    V.tensor_tensor(m2[:, 1, :], bu[:, 0, :], sn, ALU.mult).then_inc(bu_read, 1)
                    dve.wait_ge(bu_read, n + 1)
                    V.tensor_tensor(gin[:, 0, :], m1[:, 0, :], m2[:, 0, :], ALU.add)
                    link(V.tensor_tensor(gin[:, 1, :], m1[:, 1, :], m2[:, 1, :], ALU.subtract))
                    dc = DEC[:, NS5 * l + i:NS5 * l + i + 1].to_broadcast([P, SEQ])
                    for c in range(2):
                        last = V.tensor_tensor_scan(m1[:, c, :], dc, gin[:, c, :], 0.0, ALU.mult, ALU.add)
                    link(last)
                    hr = wk5[3 + n % 2]
                    if n >= 2:
                        dve.wait_ge(y_read, n - 1)
                    V.tensor_tensor(m2, m1, cs2, ALU.mult)
                    V.tensor_tensor(gin[:, 0, :], m1[:, 1, :], sn, ALU.mult)
                    link(V.tensor_tensor(gin[:, 1, :], m1[:, 0, :], sn, ALU.mult))
                    V.tensor_tensor(hr[:, 0, :], m2[:, 0, :], gin[:, 0, :], ALU.subtract)
                    V.tensor_tensor(hr[:, 1, :], m2[:, 1, :], gin[:, 1, :], ALU.add).then_inc(h_rot, 1)
                    if i % NQ == 0:
                        dve.wait_ge(h_rot, n + 1)
                    if i % NQ == NQ - 1:
                        dve.wait_ge(h_rot, n + 1)
                        dve.wait_ge(y_read, n + 1)
                        link(V.scalar_tensor_tensor(y5[:, q, :], uT[:, q, :], p_d[:, l * NQ + q:l * NQ + q + 1],
                                                    B[4 + q % 2][:, 0:SEQ], ALU.mult, ALU.add))
                        link(V.tensor_tensor(y5b[:, q, :], y5[:, q, :], y5[:, q, :], ALU.mult))
                        link(V.tensor_scalar(y5b[:, q, :], y5b[:, q, :], 0.044715, 1.0, ALU.mult, ALU.add))
                        V.tensor_tensor(y5b[:, q, :], y5b[:, q, :], y5[:, q, :], ALU.mult).then_inc(gel_in, 1)
                dve.wait_ge(gel_t, NQ * (l + 1))
                yflat = yT[:, :, :].rearrange("p q n -> p (q n)")
                link(V.scalar_tensor_tensor(yflat, y5b.rearrange("p q n -> p (q n)"), 1.0,
                                            y5.rearrange("p q n -> p (q n)"), ALU.add, ALU.mult))
                V.tensor_scalar(yflat, yflat, 0.5, None, ALU.mult).then_inc(y_ready, 1)
                link(V.memset(raw[:, :, 0:3], 0.0))
                def moba_max(h):
                    n = MH * l + h
                    p, o = mp_[h % 2], 2 * (h % 2)
                    dve.wait_ge(ms_ready, n + 1)
                    if n >= 2:
                        dve.wait_ge(ms_tr, n - 1)
                    link(V.tensor_tensor(p, B[2 + h % 2][:, 0:3 * P], causal[:, :], ALU.add))
                    V.tensor_reduce(mx[:, o:o + 1], p[:, 0:P], AX.X, ALU.max)
                    link(V.tensor_reduce(mx[:, o + 1:o + 2], p[:, P:3 * P], AX.X, ALU.max))
                    V.tensor_scalar(nm[:, o:o + 2], mx[:, o:o + 2], -MD ** -0.5, None, ALU.mult).then_inc(ms_neg, 1)

                def moba_norm(h):
                    n = MH * l + h
                    p, o = mp_[h % 2], 2 * (h % 2)
                    dve.wait_ge(ms_exp, n + 1)
                    link(V.reciprocal(rs[:, o:o + 2], rs[:, o:o + 2]))
                    V.tensor_scalar(p[:, 0:P], p[:, 0:P], rs[:, o:o + 1], None, ALU.mult)
                    V.tensor_scalar(p[:, P:3 * P], p[:, P:3 * P], rs[:, o + 1:o + 2], None, ALU.mult).then_inc(ms_norm, 1)

                def glu_branch(i):
                    n_, t = i // 2, i % 2
                    dve.wait_ge(glu_th, 4 * l + i + 1)
                    V.scalar_tensor_tensor(glu_y[t], glu_t[t], 1.0, B[0][:, :], ALU.add, ALU.mult).then_inc(glu_used, 1)
                    dve.wait_ge(glu_used, 4 * l + i + 1)
                    g = gates[:, t, D + n_ * 512:D + (n_ + 1) * 512]
                    link(V.scalar_tensor_tensor(gl_tmp[t], g, 1.0, glu_y[t], ALU.add, ALU.mult))
                    link(V.tensor_scalar(merged[:, t, n_ * 512:(n_ + 1) * 512], gl_tmp[t], 0.5, None, ALU.mult))

                if l == 0:
                    dve.wait_ge(consts, 3)
                dve.wait_ge(mtr_ready, 4 * (l + 1))
                moba_max(0)
                for h in range(MH):
                    if h + 1 < MH:
                        moba_max(h + 1)
                    moba_norm(h)
                    if h % 2 == 1:
                        glu_branch(h // 2)
                ab4 = ab.rearrange("p (t c h) -> p t c h", t=NT, c=2)
                z4 = gate_z.rearrange("p (t h) -> p t h", t=NT)
                dve.wait_ge(ab_sb, l + 1)
                for t in range(NT):
                    last = V.tensor_tensor(z4[:, t, :], ab4[:, t, 0, :], small_bc[:, l, 1, :], ALU.add)
                link(last)
                V.scalar_tensor_tensor(gate_e, gate_z, -1.0, gate_z, ALU.mult, ALU.max).then_inc(g_z, 1)

                def taps(w, js):
                    for j in js:
                        if w == 1:
                            dve.wait_ge(cv_tap, 12 * l + j + 1)
                        k = 48 * l + 12 * w + j
                        last = V.scalar_tensor_tensor(cv[:, j, :], raw[:, j, w:w + SEQ], p_conv[:, k:k + 1],
                                                      cv[:, j, :], ALU.mult, ALU.add)
                        if w == 3 and j % 4 == 3:
                            last.then_inc(cv_pre, 1)
                    if w < 3:
                        link(last)

                def moba_branch(i):
                    n_, t = i // 2, i % 2
                    dve.wait_ge(up_ps, 8 * l + i + 1)
                    V.scalar_tensor_tensor(gl_tmp[t], gates[:, t, n_ * 512:(n_ + 1) * 512], 1.0, B[i % 2][:, :],
                                           ALU.add, ALU.mult).then_inc(up_used, 1)
                    dve.wait_ge(up_used, 8 * l + i + 1)
                    m = merged[:, t, n_ * 512:(n_ + 1) * 512]
                    link(V.tensor_tensor(m, m, gl_tmp[t], ALU.add))

                for i in range(4):
                    if i > 0:
                        taps(i, range(8))
                    moba_branch(i)
                for w in range(1, 4):
                    taps(w, range(8, 12))
                dve.wait_ge(g_ln, l + 1)
                link(V.scalar_tensor_tensor(gate_z, gate_z, 0.0, gate_e, ALU.max, ALU.add))
                for t in range(NT):
                    last = V.scalar_tensor_tensor(gstep.rearrange("p (t h) -> p t h", t=NT)[:, t, :], z4[:, t, :],
                                                  -1.0, ealog, ALU.mult, ALU.mult)
                last.then_inc(g_step, 1)
                dve.wait_ge(gate_tanh, 2 * l + 1)
                link(V.tensor_scalar(beta, beta, 0.5, 0.5, ALU.mult, ALU.add))
                for i in range(3):
                    dve.wait_ge(cv_th, 3 * l + i + 1)
                    tmp = (A_low, M_lvl, W_lvl)[i].rearrange("p t h n -> p (t h n)")
                    c4 = cv[:, 4 * i:4 * i + 4, :].rearrange("p c n -> p (c n)")
                    V.scalar_tensor_tensor(c4, tmp, 1.0, c4, ALU.add, ALU.mult).then_inc(cv_ready, 1)
                for i in range(4):
                    dve.wait_ge(cv_rs, 4 * l + i + 1)
                    r_ = rq[i].rearrange("p t h n -> p (t h n)")[:, 0:512]
                    c2 = cv[:, 2 * i:2 * i + 2, :].rearrange("p c n -> p (c n)")
                    V.scalar_tensor_tensor(c2, r_, GD ** -0.5 if i < 2 else 1.0, c2, ALU.mult, ALU.mult).then_inc(kq_ready, 1)
                dve.wait_ge(gc_ps, l + 1)
                V.tensor_copy(gcum, B[1][:, 0:NT * GH]).then_inc(gc_sb, 1)
                dve.wait_ge(gc_sb, l + 1)
                gc3 = gcum.rearrange("p (t h) -> p t h", t=NT)
                be3 = beta.rearrange("p (t h) -> p t h", t=NT)
                bx3 = bexp.rearrange("p (t h) -> p t h", t=NT)
                kd3 = kds.rearrange("p (t h) -> p t h", t=NT)
                for t in range(NT):
                    V.tensor_tensor(gdiag[:, t], ident[:, :].unsqueeze(1).to_broadcast([P, GH, P]),
                                    gc3[:, t, :].unsqueeze(2).to_broadcast([P, GH, P]), ALU.mult).then_inc(g_diag, 1)
                for t in range(NT):
                    dve.wait_ge(row_ps, NT * l + t + 1)
                    link(V.tensor_tensor(DTm[:, t], B[2 + t][:, :].rearrange("p (h n) -> p h n", h=GH),
                                         gc3[:, t, :].unsqueeze(2).to_broadcast([P, GH, P]), ALU.subtract))
                    link(V.tensor_scalar(Dcl[:, t], DTm[:, t], 0.0, None, ALU.max))
                    V.tensor_scalar(DTm[:, t], DTm[:, t], 0.0, None, ALU.min).then_inc(dec_in, 1)
                dve.wait_ge(g_bexp, l + 1)
                link(V.tensor_tensor(bexp, bexp, beta, ALU.mult))
                for t in range(NT):
                    dve.wait_ge(dec_ready, 3 * NT * l + 3 * t + 3)
                    link(V.tensor_tensor(decT[:, t], decT[:, t], cum_mask[:, :].unsqueeze(1).to_broadcast([P, GH, P]),
                                         ALU.mult))
                    link(V.tensor_tensor(kd3[:, t, :], decT[:, t, :, GL - 1], decT[:, t, :, 2 * GL - 1], ALU.add))

                def per_token(s3, t):
                    return s3[:, t, :].unsqueeze(2).to_broadcast([P, GH, GD])

                for t in range(NT):
                    dve.wait_ge(kv_evac, NT * l + t + 1)
                    V.tensor_tensor(kbeg[:, t], k_tok[:, t], per_token(bx3, t), ALU.mult)
                    V.tensor_tensor(kdec[:, t], k_tok[:, t], per_token(kd3, t), ALU.mult)
                    dve.wait_ge(kv_ps, 4 * l + 2 + t + 1)
                    V.scalar_tensor_tensor(vbeta[:, t], B[6 + t][:, :].rearrange("p (h n) -> p h n", h=GH), 0.5,
                                           per_token(be3, t), ALU.mult, ALU.mult).then_inc(uw_in, 1)
                for t in range(NT):
                    dve.wait_ge(kk_ps, 2 * NT * l + t + 1)
                    link(V.tensor_tensor(A_low[:, t], B[4 + t][:, :].rearrange("p (h n) -> p h n", h=GH), dec[:, t], ALU.mult))
                    V.tensor_tensor(A_low[:, t], A_low[:, t], per_token(be3, t), ALU.mult).then_inc(a_ready, 1)
                for t in range(NT):
                    dve.wait_ge(kk_ps, 2 * NT * l + NT + t + 1)
                    V.tensor_tensor(qkT[:, t], B[6 + t][:, :].rearrange("p (h n) -> p h n", h=GH), decT[:, t], ALU.mult)
                    qc = cv[:, 0:4, t * P:(t + 1) * P]
                    V.tensor_tensor(qc, qc, e_row[:, t], ALU.mult).then_inc(qd_ready, 1)
                dve.wait_ge(gate_tanh, 2 * l + 2)
                gz = gdiag.rearrange("p t h n -> p (t h) n")
                link(V.scalar_tensor_tensor(gz, gz, 1.0, z_tok[:, :, :].rearrange("p t (h n) -> p (t h) n", h=GH),
                                            ALU.add, ALU.mult))
                link(V.scalar_tensor_tensor(gz, gz, 0.5, gnorm_bc[:, l, :].unsqueeze(1).to_broadcast([P, NT * GH, GD]),
                                            ALU.mult, ALU.mult))
                for k in range(6):
                    for t in range(NT):
                        n = (6 * l + k) * NT + t
                        if k == 0:
                            dve.wait_ge(xz_init, 2 * NT * l + 2 * t + 2)
                        dve.wait_ge(xz_ps, n + 1)
                        V.tensor_tensor(Xi[:, t], Xi[:, t], B[2 + t][:, :].rearrange("p (h n) -> p h n", h=GH), ALU.subtract)
                        V.tensor_tensor(Zi[:, t], Zi[:, t], B[4 + t][:, :].rearrange("p (h n) -> p h n", h=GH),
                                        ALU.subtract).then_inc(xz_ready, 1)
                    for t in range(NT):
                        dve.wait_ge(xz_ready, (6 * l + k) * NT + t + 1)
                V.memset(state[:, 0], 0.0).then_inc(s_init, 1)
                for t in range(NT):
                    dve.wait_ge(uw_ps, NT * l + t + 1)
                    V.tensor_copy(u_tok[:, t], B[2 + t][:, :].rearrange("p (h n) -> p h n", h=GH)).then_inc(u_done, 1)
                dve.wait_ge(u_done, NT * (l + 1))
                for c in range(NCHUNK):
                    n, t, off = NCHUNK * l + c, c // 2, (c % 2) * GL
                    rows_ = slice(off, off + GL)
                    dve.wait_ge(vn_ps, n + 1)
                    V.tensor_tensor(vn[rows_], u_tok[rows_, t], B[4][rows_, :].rearrange("p (h n) -> p h n", h=GH),
                                    ALU.subtract).then_inc(vn_ready, 1)
                    if c < NCHUNK - 1:
                        new, old = state[:, (c + 1) % 2], state[:, c % 2]
                        eg = e_row[:, t, :, off + GL - 1].unsqueeze(2).to_broadcast([P, GH, GD])
                        if c == 0:
                            dve.wait_ge(s_init, l + 1)
                        dve.wait_ge(s_ready, n - l) if c > 0 else None
                        link(V.tensor_tensor(new, old, eg, ALU.mult))
                        dve.wait_ge(su_ps, (NCHUNK - 1) * l + c + 1)
                        V.tensor_tensor(new, new, B[7][:, :].rearrange("p (h n) -> p h n", h=GH), ALU.add).then_inc(s_ready, 1)
                dve.wait_ge(o_evac, NCHUNK * (l + 1))
                o_all = o_tok.rearrange("p t h n -> p (t h) n")
                sq = DTm.rearrange("p t h n -> p (t h) n")
                link(V.tensor_tensor(sq, o_all, o_all, ALU.mult))
                V.tensor_reduce(gate_z, sq, AX.X, ALU.add).then_inc(og_ss, 1)
                dve.wait_ge(og_rs, l + 1)
                link(V.tensor_tensor(o_all, o_all, gate_z.unsqueeze(2).to_broadcast([P, NT * GH, GD]), ALU.mult))
                V.tensor_tensor(o_all, o_all, gz, ALU.mult).then_inc(og_ready, 1)
                for i in range(4):
                    n_, t = i // 2, i % 2
                    dve.wait_ge(up_ps, 8 * l + 4 + i + 1)
                    tmp = (DTm if t == 0 else Dcl).rearrange("p t h n -> p (t h n)")[:, 0:512]
                    V.scalar_tensor_tensor(tmp, gates[:, t, 2 * D + n_ * 512:2 * D + (n_ + 1) * 512], 1.0, B[i % 2][:, :],
                                           ALU.add, ALU.mult).then_inc(up_used, 1)
                    dve.wait_ge(up_used, 8 * l + 4 + i + 1)
                    m = merged[:, t, n_ * 512:(n_ + 1) * 512]
                    last = V.tensor_tensor(m, m, tmp, ALU.add)
                last.then_inc(mg_ready, 1)
                for i in range(4):
                    n_, t = i // 2, i % 2
                    dve.wait_ge(wo_ps, 4 * l + i + 1)
                    xs = x[:, t, n_ * 512:(n_ + 1) * 512]
                    V.scalar_tensor_tensor(xs, B[i % 2][:, :], 0.5, xs, ALU.mult, ALU.add).then_inc(wo_used, 1)
                normalise(x[:, :, :], h_tok, 2 + 3 * l)
                for h in range(XH):
                    n_, o = XH * l + h, 2 * (h % 2)
                    dve.wait_ge(xs_ps, n_ + 1)
                    if n_ >= 2:
                        dve.wait_ge(xs_exp, n_ - 1)
                    link(V.tensor_reduce(mx[:, o:o + 2], B[2 + h % 2][:, :].rearrange("p (t n) -> p t n", t=NT), AX.X, ALU.max))
                    V.tensor_scalar(nm[:, o:o + 2], mx[:, o:o + 2], -XD ** -0.5, None, ALU.mult).then_inc(xs_neg, 1)
                    dve.wait_ge(xs_exp, n_ + 1)
                    link(V.reciprocal(rs[:, o:o + 2], rs[:, o:o + 2]))
                    for t in range(NT):
                        last = V.tensor_scalar(xp[h % 2][:, t, :], xp[h % 2][:, t, :], rs[:, o + t:o + t + 1], None, ALU.mult)
                    last.then_inc(xs_norm, 1)
                if l % 2 == 0:
                    for i in range(4):
                        split_rest(6 * NCH * experts_before(l) + gu_at(0, i), gu_buf(0, i), 0, i)
                for i in range(4):
                    n_, t = i // 2, i % 2
                    dve.wait_ge(xo_ps, 4 * l + i + 1)
                    xs = x[:, t, n_ * 512:(n_ + 1) * 512]
                    V.tensor_tensor(xs, xs, B[i % 2][:, :], ALU.add).then_inc(xo_used, 1)
                normalise(x[:, :, :], h_tok, 3 + 3 * l)
                if l % 2 == 1:
                    dve.wait_ge(rl_ps, l // 2 + 1)
                    link(V.tensor_copy(r_log, B[0][:, 0:NT * NE].rearrange("p (t e) -> p t e", t=NT)))
                    for t in range(NT):
                        link(V.max(r_max[:, t, :], r_log[:, t, :]))
                        link(V.max_index(r_idx[:, t, :], r_max[:, t, :], r_log[:, t, :]))
                    link(V.tensor_copy(r_idf, r_idx[:, :, :]))
                    V.tensor_tensor(r_w[:, :, 0:1], r_max[:, :, 1:2], r_max[:, :, 0:1], ALU.subtract).then_inc(rl_d, 1)
                    dve.wait_ge(rl_e, l // 2 + 1)
                    link(V.tensor_scalar(r_w[:, :, 2:3], r_w[:, :, 1:2], 1.0, None, ALU.add))
                    link(V.reciprocal(r_w[:, :, 2:3], r_w[:, :, 2:3]))
                    link(V.tensor_tensor(r_w[:, :, 3:4], r_w[:, :, 1:2], r_w[:, :, 2:3], ALU.mult))
                    for t in range(NT):
                        for i in range(2):
                            last = V.tensor_scalar(r_eq[:, i, t, :], idx8[:, :], r_idf[:, t, i:i + 1],
                                                   r_w[:, t, 2 + i:3 + i], ALU.is_equal, ALU.mult)
                    link(last)
                    cols = slice(0, NE)
                    V.memset(comb[:, :, NE:NE + 1], 0.0)
                    V.memset(chosen[:, :, NE:NE + 1], 0.0)
                    V.memset(place[:, :, NE:NE + 1], 0.0)
                    link(V.tensor_tensor(comb[:, :, cols], r_eq[:, 0], r_eq[:, 1], ALU.add))
                    for t in range(NT):
                        for i in range(2):
                            last = V.tensor_scalar(r_eq[:, i, t, :], idx8[:, :], r_idf[:, t, i:i + 1], None, ALU.is_equal)
                    link(last)
                    V.tensor_scalar(comb[:, :, cols], comb[:, :, cols], 0.5, None, ALU.mult)
                    V.tensor_tensor(chosen[:, :, cols], r_eq[:, 0], r_eq[:, 1], ALU.add).then_inc(comb_ready, 1)
                    dve.wait_ge(gain_in, 16 * (l // 2 + 1))
                    dve.wait_ge(norm_ps, 4 * (4 + 3 * l))
                    for t in range(NT):
                        V.tensor_tensor(h_tok[:, t, :], h_tok[:, t, :], gain_bc, ALU.mult).then_inc(h_gain, 1)
                    dve.wait_ge(place_ps, 1)
                    V.tensor_copy(place[:, :, cols], B[1][:, 0:NT * NE].rearrange("p (t e) -> p t e", t=NT))
                    link(V.tensor_reduce(e_most, B[1][:, NT * NE:NT * NE + NE], AX.X, ALU.max))
                    V.tensor_scalar(over_i[:, :], e_most, float(P), None, ALU.is_gt).then_inc(place_ready, 1)
                    dve.wait_ge(place_ready, 1)

                base = acts_before(l)
                if l % 2 == 0:
                    n = 3 + 3 * l
                    for b in range(4):
                        dve.wait_ge(*((fx_hi, 3 * fx_before(l) + b + 1) if b < 3 else (hT_ready, n + 1)))
                        for i in range(2):
                            k = 2 * b + i
                            last = V.scalar_tensor_tensor(fx[:, LO, k, :], B[4 + b][:, i * SEQ:(i + 1) * SEQ],
                                                          gain_ffn[:, l * KD + k:l * KD + k + 1],
                                                          fx[:, HI, k, :].bitcast(F32), ALU.mult, ALU.subtract)
                    last.then_inc(fx_ready, 1)
                    g0 = 6 * NCH * experts_before(l)

                    def tail(c):
                        for t in range(NT):
                            dve.wait_ge(actT_hi, c * NT + (base + t + 1))
                            V.tensor_tensor(f_actT[:, LO, :, t * P:(t + 1) * P],
                                            B[2 + t][:, 0:2 * P].rearrange("p (k n) -> p k n", n=P),
                                            f_actT[:, HI, :, t * P:(t + 1) * P].bitcast(F32),
                                            ALU.subtract).then_inc(actT_ready, 1)

                    def chunk(c, s):
                        head = isinstance(c, int) and c == 0
                        if not head:
                            for i in range(4):
                                if i == 3:
                                    tail(c - 1)
                                split_rest(gu_at(c, i) + g0, gu_buf(c, i), s, i)
                            for i in range(2):
                                split_rest(down_at(c - 1, i) + g0, down_buf(1, i), (s - 1) % NSLOT, 4 + i)
                        for t in range(NT):
                            v = c * NT + (base + t + 1)
                            dve.wait_ge(gu_th, v)
                            V.scalar_tensor_tensor(f_a[t], f_th[t], 1.0, B[t][:, 0:FC], ALU.add, ALU.mult).then_inc(gu_a, 1)
                            dve.wait_ge(gu_a, v)
                            if not (head and l == 0):
                                dve.wait_ge(act_tr, c * NT + (base + t + 1 - NT))
                            V.scalar_tensor_tensor(f_act[t], f_a[t], 0.5, B[t][:, FC:2 * FC],
                                                   ALU.mult, ALU.mult).then_inc(act_ready, 1)
                    chunks_of_expert(dve, chunk)
                    for i in range(2):
                        c = NCH - 1
                        split_rest(down_at(c, i) + g0, down_buf(c, i), c % NSLOT, 4 + i)
                    tail(NCH - 1)
                    dve.wait_ge(split_used, 6 * NCH * (experts_before(l) + 1))
                    for i in range(4):
                        n_, t = i // 2, i % 2
                        xs = x[:, t, n_ * 512:(n_ + 1) * 512]
                        last = V.tensor_tensor(xs, xs, B[4 + i][:, :], ALU.add)
                    last.then_inc(y_added, 1)
                    dve.wait_ge(y_added, l // 2 + 1)
                else:
                    def gather_matrix(e, k):
                        dve.wait_ge(he_ps, k - 1)
                        for t in range(NT):
                            last = V.tensor_scalar(gather_m[:, t, :], steps[:, 0:P], place[:, t, bass.ds(e, 1)],
                                                   chosen[:, t, bass.ds(e, 1)], ALU.is_equal, ALU.mult)
                        last.then_inc(gm_ready, 1)

                    def add_scattered(k):
                        for i in range(4):
                            n_, t = i // 2, i % 2
                            xs = x[:, t, n_ * 512:(n_ + 1) * 512]
                            dve.wait_ge(sc_ps, 4 * k + (i + 1))
                            V.tensor_tensor(xs, xs, B[6 + i % 2][:, :], ALU.add).then_inc(sc_used, 1)

                    def one_pass(p):
                        ab_, kb = base + p * NE * NCH, p * (NE + 1)
                        if p == 1:
                            dve.wait_ge(wm_ready, NE)
                            link(V.tensor_scalar(place, place, -float(P), None, ALU.add))
                            dve.wait_ge(he_ps, kb)
                            for t in range(NT):
                                last = V.tensor_scalar(gather_m[:, t, :], steps[:, 0:P], place[:, t, 0:1],
                                                       chosen[:, t, 0:1], ALU.is_equal, ALU.mult)
                            last.then_inc(gm_ready, 1)
                        else:
                            for t in range(NT):
                                last = V.tensor_scalar(gather_m[:, t, :], steps[:, 0:P], place[:, t, 0:1],
                                                       chosen[:, t, 0:1], ALU.is_equal, ALU.mult)
                            last.then_inc(gm_ready, 1)
                        V.memset(scatter_m, 0.0).then_inc(sm_ready, 1)
                        def he_rest(k):
                            for b in range(2):
                                dve.wait_ge(fx_hi, k * 2 + (3 * fx_before(l) + b - 1))
                                last = V.tensor_tensor(fx_e[:, LO, 4 * b:4 * b + 4, 0:P],
                                                       B[6 + b][:, :].rearrange("p (k n) -> p k n", n=P),
                                                       fx_e[:, HI, 4 * b:4 * b + 4, 0:P].bitcast(F32), ALU.subtract)
                            last.then_inc(fx_ready, 1)

                        he_rest(kb + 1)
                        gb = 6 * NCH * (experts_before(l) + p * NE)
                        with dve.Fori(0, NE) as e:
                            def tail(c):
                                dve.wait_ge(actT_hi, e * NCH + c + (ab_ + 1))
                                V.tensor_tensor(f_actT_e[:, LO, :, :], B[3][:, 0:2 * P].rearrange("p (k n) -> p k n", n=P),
                                                f_actT_e[:, HI, :, :].bitcast(F32), ALU.subtract).then_inc(actT_ready, 1)

                            def chunk(c, s):
                                head = isinstance(c, int) and c == 0
                                ge = e * (6 * NCH) + gb
                                for i in range(4):
                                    if i == 3 and not head:
                                        tail(c - 1)
                                    split_rest(ge + gu_at(c, i), gu_buf(c, i), s, i)
                                if head:
                                    for t in range(NT):
                                        last = V.tensor_scalar(weight_m[:, t, :], steps[:, 0:P], place[:, t, bass.ds(e, 1)],
                                                               comb[:, t, bass.ds(e, 1)], ALU.is_equal, ALU.mult)
                                    last.then_inc(wm_ready, 1)
                                    gather_matrix(e + 1, e + (kb + 2))
                                else:
                                    for i in range(2):
                                        split_rest(ge + down_at(c - 1, i), down_buf(1, i), (s - 1) % NSLOT, 4 + i)
                                v = e * NCH + c + (ab_ + 1)
                                dve.wait_ge(gu_th, v)
                                V.scalar_tensor_tensor(f_a[0], f_th[0], 1.0, B[s][:, 0:FC], ALU.add,
                                                       ALU.mult).then_inc(gu_a, 1)
                                dve.wait_ge(gu_a, v)
                                dve.wait_ge(act_tr, v - 1)
                                V.tensor_tensor(f_act[0], f_a[0], B[s][:, FC:2 * FC], ALU.mult).then_inc(act_ready, 1)
                                if head:
                                    add_scattered(e + kb)
                                if isinstance(c, int) and c == NCH - 1:
                                    he_rest(e + (kb + 2))
                            chunks_of_expert(dve, chunk)
                            for i in range(2):
                                c = NCH - 1
                                split_rest(e * (6 * NCH) + (gb + down_at(c, i)), down_buf(c, i), c % NSLOT, 4 + i)
                            tail(NCH - 1)
                            dve.wait_ge(sm_ps, e + (NE * p + 1))
                            dve.wait_ge(sc_used, 4 * e + (4 * kb + 4))
                        add_scattered(kb + NE)
                        dve.wait_ge(sc_used, 4 * (kb + NE + 1))
                    moe_passes(dve, one_pass)
            n = NNORM
            dve.wait_ge(norm_ss, n + 1)
            dve.wait_ge(gain_in, 16 * (DEPTH // 2 + 1))
            for t in range(NT):
                last = V.scalar_tensor_tensor(x[:, t, :], x[:, t, :], rstd[:, t:t + 1], gain_out, ALU.mult, ALU.mult)
            last.then_inc(fin_ready, 1)

        @block.tensor
        def _(pe):
            mm = nc.tensor.matmul
            tr = nc.tensor.transpose
            pe.wait_ge(consts, 1)
            pe.wait_ge(consts, 2)
            pe.wait_ge(par_in, 16 * 9)
            rows = phase[:, 0:3 * P].rearrange("p (a n) -> p a n", a=3)
            tr(B[0][:, 0:P], rows[:, 0, :], ident[:, :])
            tr(B[0][:, P:2 * P], rows[:, 1, :], ident[:, :])
            tr(B[0][:, 2 * P:2 * P + 8], rows[0:8, 2, :], ident[0:8, 0:8]).then_inc(par_ps, 1)

            def transpose_rows(src, n):
                pe.wait_ge(norm_h, NT * (n + 1))
                for b in range(4):
                    for i in range(2):
                        for t in range(NT):
                            k = 2 * b + i
                            last = tr(B[4 + b][:, i * SEQ + t * P:i * SEQ + (t + 1) * P],
                                      src[:, t, k * P:(k + 1) * P], ident[:, :])
                    last.then_inc(norm_ps, 1)

            def arrived(l, j):
                pe.wait_ge(slot_full[j % NSLOT], slot_after_unit(l, j))

            def features_out(l, j, src, banks, ready, free):
                arrived(l, j)
                w = slot(j)[:, 0:4096].rearrange("p (k w) -> p k w", w=512)
                for m in range(4):
                    if m % 2 == 0 and free is not None:
                        free(m // 2)
                    for k in range(KD):
                        last = mm(B[banks[m // 2]][:, (m % 2) * SEQ:(m % 2 + 1) * SEQ],
                                  w[:, k, m * P:(m + 1) * P], src[:, k, :], start=k == 0, stop=k == KD - 1)
                    if m % 2 == 1:
                        last.then_inc(ready, 1)

            def tokens_out(bank, src, t, w, kt, n0):
                for k in range(kt):
                    last = mm(B[bank][:, :], src[:, k, t * P:(t + 1) * P], w[:, k, n0:n0 + 512],
                              start=k == 0, stop=k == kt - 1)
                return last

            transpose_rows(h_tok, 0)

            for l in range(DEPTH):
                if l == 0:
                    pe.wait_ge(hT_ready, 1)
                transpose_rows(h_tok, 1 + 3 * l)
                pe.wait_ge(hT_ready, 2 + 3 * l)
                if l == 0:
                    pe.wait_ge(par_ready, 1)

                features_out(l, U_U, hT[:, :, :], (0, 1), ws_ready, None)

                def pad_tr(q, half):
                    n = 2 * (NQ * l + q) + half
                    pe.wait_ge(pad_ready, 2 * n + 2)
                    if n >= 1:
                        pe.wait_ge(bct_ready, n)
                    for c in range(2):
                        for j in range(NQ):
                            last = tr(B[6 + c][:, j * P:(j + 1) * P], pads[:, c, j * P:(j + 1) * P], ident[:, :])
                    last.then_inc(pad_ps, 1)

                pe.wait_ge(ab_in, 16 * (l + 1))
                for t in range(NT):
                    for k in range(KD):
                        last = mm(B[4][:, t * 8:(t + 1) * 8], hT[:, k, t * P:(t + 1) * P], ab_w[:, k, :],
                                  start=k == 0, stop=k == KD - 1)
                last.then_inc(ab_ps, 1)

                def fill(f):
                    j, t = U_Q + f // 2, f % 2
                    if t == 0:
                        arrived(l, j)
                    if f < 2:
                        pe.wait_ge(ws_evac, 8 * l + 1 + f)
                    elif f < 6:
                        pe.wait_ge(rope_done, 4 * l + f - 1)
                    else:
                        pe.wait_ge(fill_evac, 16 * l + f - 5)
                    w = slot(j)[:, 0:4096].rearrange("p (k w) -> p k w", w=512)
                    tokens_out(t, hT[:, :, :], t, w, KD, 0).then_inc(fill_ready, 1)

                def s5_in(i):
                    q, n = i // NQ, NS5 * l + i
                    if i % NQ == 0:
                        pe.wait_ge(bct_ready, 2 * (NQ * l + q) + 2)
                    if i == 0:
                        pe.wait_ge(ws_evac, 8 * l + 2)
                    if n >= 2:
                        pe.wait_ge(bu_read, n - 1)
                    for c in range(2):
                        last = mm(B[2 + n % 2][:, c * SEQ:(c + 1) * SEQ], bct[q % 2][c][:, i % NQ, :], uT[:, q, :],
                                  start=True, stop=True)
                    last.then_inc(bu_ready, 1)

                def s5_out(i):
                    q, n = i // NQ, NS5 * l + i
                    if i == 0:
                        pe.wait_ge(ab_sb, l + 1)
                    if i % NQ == 0 and q >= 2:
                        pe.wait_ge(gel_in, NQ * l + q - 1)
                    pe.wait_ge(h_rot, n + 1)
                    hr = wk5[3 + n % 2]
                    for c in range(2):
                        last = mm(B[4 + q % 2][:, 0:SEQ], bct[q % 2][2 + c][:, i % NQ, :], hr[:, c, :],
                                  start=(i % NQ == 0 and c == 0), stop=(i % NQ == NQ - 1 and c == 1))
                    last.then_inc(y_read, 1)

                for f in range(4):
                    fill(f)
                pad_tr(0, 0)
                pad_tr(0, 1)
                for i in range(NS5):
                    s5_in(i)
                    fill(4 + i)
                    if i > 0:
                        s5_out(i - 1)
                    if i % NQ == 1 and i // NQ + 1 < NQ:
                        pad_tr(i // NQ + 1, 0)
                        pad_tr(i // NQ + 1, 1)
                s5_out(NS5 - 1)

                pe.wait_ge(fill_evac, 16 * (l + 1))
                features_out(l, U_CONV, hT[:, :, :], (0, 1), ws_ready, None)
                pe.wait_ge(bu_read, NS5 * (l + 1))
                features_out(l, U_CONV + 1, hT[:, :, :], (2, 3), ws_ready, None)
                features_out(l, U_CONV + 2, hT[:, :, :], (0, 1), ws_ready,
                             lambda b: pe.wait_ge(ws_evac, 8 * l + 3 + b))

                pe.wait_ge(gel_in, NQ * (l + 1))
                pe.wait_ge(bct_ready, 2 * NQ * (l + 1))
                for i in range(4):
                    for k in range(KW):
                        last = tr(B[4 + i][:, k * P:(k + 1) * P], qk[:, i // 2, i % 2, k * P:(k + 1) * P], ident[:, :])
                    last.then_inc(mtr_ps, 1)
                pe.wait_ge(mtr_ready, 4 * (l + 1))

                def m_scores(h):
                    n = MH * l + h
                    if h >= 2:
                        pe.wait_ge(ms_neg, n - 1)
                    else:
                        pe.wait_ge(ws_evac, 8 * l + 5 + h)
                    ps = slice((h % 2) * MD, (h % 2 + 1) * MD)
                    mm(B[2 + h % 2][:, 0:P], mqT[ps, h // 2, 0:P], mkT[ps, h // 2, 0:P], start=True, stop=True)
                    mm(B[2 + h % 2][:, P:3 * P], mqT[ps, h // 2, P:2 * P], mkT[ps, h // 2, :], start=True,
                       stop=True).then_inc(ms_ready, 1)

                def m_tr(h):
                    n = MH * l + h
                    pe.wait_ge(ms_norm, n + 1)
                    if h >= 2:
                        pe.wait_ge(ms_pT, n - 1)
                    for b in range(3):
                        last = tr(B[4 + h % 2][:, b * P:(b + 1) * P], mp_[h % 2][:, b * P:(b + 1) * P], ident[:, :])
                    last.then_inc(ms_tr, 1)

                def m_out(h):
                    n = MH * l + h
                    pe.wait_ge(ms_pT, n + 1)
                    if h >= 4 and h % 2 == 0:
                        pe.wait_ge(ms_oT, 4 * l + h // 2 - 1)
                    ps = slice((h % 2) * MD, (h % 2 + 1) * MD)
                    o = B[6 + (h // 2) % 2]
                    pT, vh = mpT[h % 2], v_tok[:, :, h * MD:(h + 1) * MD]
                    mm(o[ps, 0:P], vh[:, 0, :], pT[:, 0:P], start=True, stop=True)
                    mm(o[ps, P:2 * P], vh[:, 0, :], pT[:, P:2 * P], start=True, stop=False)
                    mm(o[ps, P:2 * P], vh[:, 1, :], pT[:, 2 * P:3 * P], start=False, stop=True).then_inc(ms_o, 1)

                def glu_half(i, half):
                    n_, t = i // 2, i % 2
                    if half == 0:
                        if i == 0:
                            pe.wait_ge(y_ready, l + 1)
                            pe.wait_ge(ws_evac, 8 * (l + 1))
                        else:
                            pe.wait_ge(glu_used, 4 * l + i)
                    if t == 0:
                        arrived(l, U_GLU + n_)
                    w = slot(U_GLU + n_)[:, 0:4096].rearrange("p (k w) -> p k w", w=D)
                    last = tokens_out(half, yT[:, :, :], t, w, KW, half * 512)
                    if half == 1:
                        last.then_inc(glu_ps, 1)

                for s in range(MH + 2):
                    if s < MH:
                        m_scores(s)
                    if 1 <= s <= MH:
                        glu_half((s - 1) // 2, (s - 1) % 2)
                    if 1 <= s <= MH:
                        m_tr(s - 1)
                    if s >= 2:
                        m_out(s - 2)

                def up(j, src, first, n):
                    arrived(l, j)
                    w = slot(j)[:, 0:4096].rearrange("p (k w) -> p k w", w=D)
                    for i in range(4):
                        if i >= 2:
                            pe.wait_ge(up_used, n + i - 1)
                        last = tokens_out(i % 2, src, i % 2, w, KW, (i // 2) * 512)
                        last.then_inc(up_ps, 1)

                pe.wait_ge(ms_oT, 4 * (l + 1))
                pe.wait_ge(glu_used, 4 * (l + 1))
                up(U_UPM, m_oT, True, 8 * l)
                pe.wait_ge(up_used, 8 * l + 4)
                pe.wait_ge(g_step, l + 1)
                mm(B[1][:, 0:NT * GH], cum_mask[:, :], gstep, start=True, stop=True).then_inc(gc_ps, 1)
                for i in range(4):
                    pe.wait_ge(cv_sq, 4 * l + i + 1)
                    tmp = (DTm, Dcl)[i // 2].rearrange("p t h n -> p (t h n)")[:, (i % 2) * 512:(i % 2 + 1) * 512]
                    mm(B[4 + i][:, :], ones[:, :], tmp, start=True, stop=True).then_inc(cv_ss, 1)
                for t in range(NT):
                    pe.wait_ge(g_diag, NT * l + t + 1)
                    mm(B[2 + t][:, :], ones[:, :], gdiag[:, t].rearrange("p h n -> p (h n)"), start=True,
                       stop=True).then_inc(row_ps, 1)
                pe.wait_ge(kq_ready, 4 * (l + 1))
                for t in range(NT):
                    for h in range(GH):
                        last = tr(B[4 + t][:, h * P:(h + 1) * P], cv[:, 4 + h, t * P:(t + 1) * P], ident[:, :])
                    last.then_inc(kv_ps, 1)
                pe.wait_ge(cv_ready, 3 * (l + 1))
                for t in range(NT):
                    for h in range(GH):
                        last = tr(B[6 + t][:, h * P:(h + 1) * P], cv[:, 8 + h, t * P:(t + 1) * P], ident[:, :])
                    last.then_inc(kv_ps, 1)
                for t in range(NT):
                    pe.wait_ge(kv_evac, NT * l + t + 1)
                    for h in range(GH):
                        kh = cv[:, 4 + h, t * P:(t + 1) * P]
                        last = mm(B[4 + t][:, h * P:(h + 1) * P], kh, kh, start=True, stop=True)
                    last.then_inc(kk_ps, 1)
                for t in range(NT):
                    pe.wait_ge(uw_in, NT * l + t + 1)
                    for h in range(GH):
                        last = mm(B[6 + t][:, h * P:(h + 1) * P], cv[:, 4 + h, t * P:(t + 1) * P],
                                  cv[:, h, t * P:(t + 1) * P], start=True, stop=True)
                    last.then_inc(kk_ps, 1)
                for k in range(6):
                    for t in range(NT):
                        n = (6 * l + k) * NT + t
                        pe.wait_ge(m_ready, n + 1)
                        if k == 0:
                            pe.wait_ge(xz_init, 2 * NT * l + 2 * t + 2)
                            pe.wait_ge(dec_in, NT * (l + 1))
                            pe.wait_ge(dec_ready, 3 * NT * (l + 1))
                        else:
                            pe.wait_ge(xz_ready, n - NT + 1)
                        for h in range(GH):
                            last = mm(B[t][:, h * P:(h + 1) * P], M_lvl[:, t, h, :], Zi[:, t, h, :], start=True, stop=True)
                        last.then_inc(w_ps, 1)
                    for t in range(NT):
                        n = (6 * l + k) * NT + t
                        pe.wait_ge(w_evac, n + 1)
                        for h in range(GH):
                            mm(B[2 + t][:, h * P:(h + 1) * P], W_lvl[:, t, h, :], Xi[:, t, h, :], start=True, stop=True)
                        for h in range(GH):
                            last = mm(B[4 + t][:, h * P:(h + 1) * P], Xi[:, t, h, :], W_lvl[:, t, h, :], start=True, stop=True)
                        last.then_inc(xz_ps, 1)
                for t in range(NT):
                    pe.wait_ge(xz_ready, (6 * l + 5) * NT + t + 1)
                    pe.wait_ge(qd_ready, NT * l + t + 1)
                    for h in range(GH):
                        mm(B[t][:, h * P:(h + 1) * P], kbeg[:, t, h, :], Zi[:, t, h, :], start=True, stop=True)
                    for h in range(GH):
                        last = mm(B[2 + t][:, h * P:(h + 1) * P], Zi[:, t, h, :], vbeta[:, t, h, :], start=True, stop=True)
                    last.then_inc(uw_ps, 1)
                pe.wait_ge(w_done, NT * (l + 1))
                pe.wait_ge(s_init, l + 1)
                pe.wait_ge(xz_ready, 6 * NT * (l + 1))
                for c in range(NCHUNK):
                    n, t, off = NCHUNK * l + c, c // 2, (c % 2) * GL
                    rows_ = slice(off, off + GL)
                    if c > 0:
                        pe.wait_ge(s_ready, (NCHUNK - 1) * l + c)
                    S = state[:, c % 2]
                    for h in range(GH):
                        last = mm(B[4][rows_, h * P:(h + 1) * P], wT[:, t, h, rows_], S[:, h, :], start=True, stop=True)
                    last.then_inc(vn_ps, 1)
                    pe.wait_ge(vn_ready, n + 1)
                    if c < NCHUNK - 1:
                        for h in range(GH):
                            last = mm(B[7][:, h * P:(h + 1) * P], kdec[rows_, t, h, :], vn[rows_, h, :], start=True, stop=True)
                        last.then_inc(su_ps, 1)
                    if c >= 2:
                        pe.wait_ge(o_evac, NCHUNK * l + c - 1)
                    for h in range(GH):
                        o = B[5 + c % 2][rows_, h * P:(h + 1) * P]
                        mm(o, cv[:, h, t * P + off:t * P + off + GL], S[:, h, :], start=True, stop=False)
                        last = mm(o, qkT[rows_, t, h, rows_], vn[rows_, h, :], start=False, stop=True)
                    last.then_inc(o_ps, 1)
                pe.wait_ge(og_ready, l + 1)
                for t in range(NT):
                    for h in range(GH):
                        last = tr(B[4 + t][:, h * P:(h + 1) * P], o_tok[:, t, h, :], ident[:, :])
                    last.then_inc(og_ps, 1)
                pe.wait_ge(og_T, NT * (l + 1))
                up(U_UPG, g_oT, False, 8 * l + 4)
                pe.wait_ge(up_used, 8 * (l + 1))
                pe.wait_ge(mg_ready, l + 1)
                for b in range(4):
                    for i in range(2):
                        for t in range(NT):
                            k = 2 * b + i
                            last = tr(B[4 + b][:, i * SEQ + t * P:i * SEQ + (t + 1) * P], merged[:, t, k * P:(k + 1) * P], ident[:, :])
                    last.then_inc(mg_ps, 1)
                pe.wait_ge(mg_T, 4 * (l + 1))
                for n_ in range(2):
                    arrived(l, U_OUT + n_)
                    w = slot(U_OUT + n_)[:, 0:4096].rearrange("p (k w) -> p k w", w=512)
                    for t in range(NT):
                        if n_ == 1:
                            pe.wait_ge(wo_used, 4 * l + t + 1)
                        tokens_out(t, hT[:, :, :], t, w, KD, 0).then_inc(wo_ps, 1)
                pe.wait_ge(memn_ready, l + 1)
                features_out(l, U_WK, memnT, (2, 3), xk_ps, None)
                pe.wait_ge(wo_used, 4 * (l + 1))
                arrived(l, U_WV)
                w = slot(U_WV)[:, 0:4096].rearrange("p (k w) -> p k w", w=512)
                for t in range(NT):
                    tokens_out(t, memnT, t, w, KD, 0).then_inc(xk_ps, 1)
                transpose_rows(h_tok, 2 + 3 * l)
                pe.wait_ge(hT_ready, 3 + 3 * l)
                pe.wait_ge(xk_sb, 6 * l + 4)
                features_out(l, U_WQ, hT[:, :, :], (0, 1), xk_ps, None)
                pe.wait_ge(xk_sb, 6 * l + 6)

                def x_scores(h):
                    n = XH * l + h
                    if h >= 2:
                        pe.wait_ge(xs_exp, n - 1)
                    for t in range(NT):
                        last = mm(B[2 + h % 2][:, t * SEQ:(t + 1) * SEQ], xqT[:, h, t * P:(t + 1) * P], xkT[:, h, :],
                                  start=True, stop=True)
                    last.then_inc(xs_ps, 1)

                def x_tr(h):
                    n = XH * l + h
                    pe.wait_ge(xs_norm, n + 1)
                    if h >= 2:
                        pe.wait_ge(xs_pT, n - 1)
                    for m in range(NT):
                        for t in range(NT):
                            last = tr(B[4 + h % 2][:, m * SEQ + t * P:m * SEQ + (t + 1) * P],
                                      xp[h % 2][:, t, m * P:(m + 1) * P], ident[:, :])
                    last.then_inc(xs_tr, 1)

                def x_out(h):
                    n = XH * l + h
                    pe.wait_ge(xs_pT, n + 1)
                    if h >= 2:
                        pe.wait_ge(xs_oT, n - 1)
                    for m in range(NT):
                        last = mm(B[6 + h % 2][:, 0:SEQ], x_v[:, m, h * XD:(h + 1) * XD], xpT[h % 2][:, m, :],
                                  start=m == 0, stop=m == NT - 1)
                    last.then_inc(xs_o, 1)

                for s in range(XH + 2):
                    if s < XH:
                        x_scores(s)
                    if 1 <= s <= XH:
                        x_tr(s - 1)
                    if s >= 2:
                        x_out(s - 2)
                pe.wait_ge(xs_oT, XH * (l + 1))
                arrived(l, U_WO)
                w = slot(U_WO)[:, 0:4096].rearrange("p (k w) -> p k w", w=D)
                for i in range(4):
                    if i >= 2:
                        pe.wait_ge(xo_used, 4 * l + i - 1)
                    tokens_out(i % 2, x_oT, i % 2, w, KW, (i // 2) * 512).then_inc(xo_ps, 1)
                transpose_rows(h_tok, 3 + 3 * l)
                pe.wait_ge(hT_ready, 4 + 3 * l)

                def split_product(bank, a, w, first, last_one):
                    mm(bank, a[HI], w[HI], start=first, stop=False)
                    mm(bank, a[HI], w[LO], start=False, stop=False)
                    return mm(bank, a[LO], w[HI], start=False, stop=last_one)

                def gate_up_group(at, c, i, src, banks, tiles):
                    pe.wait_ge(split_lo, at + 1)
                    w = split[gu_buf(c, i)].rearrange("p a (k n) -> p a k n", n=512)
                    for bank, (t0, t1) in zip(banks, tiles):
                        for k in range(2):
                            kk = 2 * i + k
                            last = split_product(bank[:, :], [src[:, a, kk, t0:t1] for a in (HI, LO)],
                                                 [w[:, a, k, :] for a in (HI, LO)], kk == 0, kk == KD - 1)
                    last.then_inc(split_used, 1)

                def down_group(at, c, i, src, banks, tiles, first, last_one):
                    pe.wait_ge(split_lo, at + 1)
                    w = split[down_buf(c, i)]
                    for t, (t0, t1) in enumerate(tiles):
                        for n_ in range(2):
                            last = split_product(banks[n_][t][:, :], [src[:, a, i, t0:t1] for a in (HI, LO)],
                                                 [w[:, a, n_ * 512:(n_ + 1) * 512] for a in (HI, LO)],
                                                 first and i == 0, last_one and i == 1)
                    last.then_inc(split_used, 1)

                if l % 2 == 1:
                    pe.wait_ge(tables_in, TABLES)
                    for t in range(NT):
                        for k in range(KD):
                            last = mm(B[0][:, t * NE:(t + 1) * NE], hT[:, k, t * P:(t + 1) * P], router_w[:, k, :],
                                      start=k == 0, stop=k == KD - 1)
                    last.then_inc(rl_ps, 1)
                base = acts_before(l)
                if l % 2 == 0:
                    def at(c, t):
                        return c * NT + (base + t + 1)

                    def first_of_all(c):
                        return isinstance(c, int) and c == 0 and l == 0

                    tiles = [(t * P, (t + 1) * P) for t in range(NT)]
                    g0 = 6 * NCH * experts_before(l)

                    def flip(c):
                        for t in range(NT):
                            pe.wait_ge(act_ready, at(c, t))
                            if not first_of_all(c):
                                pe.wait_ge(actT_ready, at(c, t) - NT)
                            for k in range(FC // P):
                                last = tr(B[2 + t][:, k * P:(k + 1) * P], f_act[t][:, k * P:(k + 1) * P], ident[:, :])
                            last.then_inc(act_tr, 1)

                    def down(c, first, last_one):
                        pe.wait_ge(actT_ready, at(c, NT - 1))
                        for i in range(2):
                            down_group(g0 + down_at(c, i), NCH - 1 if last_one else 0, i, f_actT, [[B[4], B[5]], [B[6], B[7]]],
                                       tiles, first, last_one)

                    def chunk(c):
                        if not first_of_all(c):
                            pe.wait_ge(act_ready, at(c, NT - 1) - NT)
                        head = isinstance(c, int) and c == 0
                        for i in range(4):
                            if i == 1 and not head:
                                flip(c - 1)
                            gate_up_group(g0 + gu_at(c, i), c, i, fx, B[0:2], tiles)
                        if not head:
                            down(c - 1, isinstance(c, int) and c == 1, False)

                    pe.wait_ge(fx_ready, l // 2 + 1)
                    chunk(0)
                    chunk(1)
                    with pe.Fori(0, NCH - 2) as r:
                        chunk(r + 2)
                    flip(NCH - 1)
                    down(NCH - 1, False, True)
                else:
                    pe.wait_ge(comb_ready, 1)
                    cols = slice(0, NE)
                    mm(B[1][:, 0:NE], before[:, :], chosen[:, 0, cols], start=True, stop=True)
                    mm(B[1][:, NE:2 * NE], ones[:, :], chosen[:, 0, cols], start=True, stop=False)
                    mm(B[1][:, NE:2 * NE], before[:, :], chosen[:, 1, cols], start=False, stop=True)
                    mm(B[1][:, 2 * NE:3 * NE], ones[:, :], chosen[:, 0, cols], start=True, stop=False)
                    mm(B[1][:, 2 * NE:3 * NE], ones[:, :], chosen[:, 1, cols], start=False, stop=True).then_inc(place_ps, 1)

                    def gather():
                        for k in range(KD):
                            for t in range(NT):
                                last = mm(B[6 + k // 4][:, (k % 4) * P:(k % 4 + 1) * P], h_tok[:, t, k * P:(k + 1) * P],
                                          gather_m[:, t, :], start=t == 0, stop=t == NT - 1)
                        last.then_inc(he_ps, 1)

                    def scatter(k):
                        pe.wait_ge(sm_ready, k)
                        pe.wait_ge(ye_ready, k)
                        for i in range(4):
                            n_, t = i // 2, i % 2
                            if i >= 2:
                                pe.wait_ge(sc_used, 4 * k + (i - 5))
                            mm(B[6 + i % 2][:, :], scatter_m[:, t * P:(t + 1) * P], y_e[:, n_ * 512:(n_ + 1) * 512],
                               start=True, stop=True).then_inc(sc_ps, 1)

                    def one_pass(p):
                        ab_, kb = base + p * NE * NCH, p * (NE + 1)
                        if p == 0:
                            pe.wait_ge(h_gain, NT)
                            pe.wait_ge(hT_ready, 4 + 3 * l)
                        else:
                            pe.wait_ge(sc_used, 4 * kb)
                        pe.wait_ge(gm_ready, kb + 1)
                        gather()
                        gb = 6 * NCH * (experts_before(l) + p * NE)
                        with pe.Fori(0, NE) as e:
                            def flip(c):
                                if isinstance(c, int) and c == 0:
                                    pe.wait_ge(sm_ready, e + (kb + 2))
                                pe.wait_ge(act_ready, e * NCH + c + (ab_ + 1))
                                pe.wait_ge(actT_ready, e * NCH + c + ab_)
                                for k in range(FC // P):
                                    last = tr(B[3][:, k * P:(k + 1) * P], f_act[0][:, k * P:(k + 1) * P], ident[:, :])
                                last.then_inc(act_tr, 1)

                            def down(c, first, last_one):
                                pe.wait_ge(actT_ready, e * NCH + c + (ab_ + 1))
                                for i in range(2):
                                    down_group(e * (6 * NCH) + down_at(c, i) + gb, NCH - 1 if last_one else 0, i,
                                               f_actT_e, [[B[4]], [B[5]]], [(0, P)], first, last_one)

                            def chunk(c, s):
                                head = isinstance(c, int) and c == 0
                                if head:
                                    pe.wait_ge(fx_ready, e + (kb + 1 + fx_before(l)))
                                for i in range(4):
                                    if i == 1 and not head:
                                        flip(c - 1)
                                    gate_up_group(e * (6 * NCH) + gu_at(c, i) + gb, c, i, fx_e, [B[s]], [(0, P)])
                                if head:
                                    scatter(e + (kb + 1))
                                    pe.wait_ge(wm_ready, e + (p * NE + 1))
                                    for t in range(NT):
                                        last = tr(B[3][:, (2 + t) * P:(3 + t) * P], weight_m[:, t, :], ident[:, :])
                                    last.then_inc(sm_ps, 1)
                                if isinstance(c, int) and c == NCH - 1:
                                    pe.wait_ge(gm_ready, e + (kb + 2))
                                    pe.wait_ge(sc_used, 4 * e + (4 * kb + 4))
                                    gather()
                                if not head:
                                    down(c - 1, isinstance(c, int) and c == 1, False)

                            chunk(0, 0)
                            chunk(1, 1)
                            loops = (NCH - 3) // NSLOT
                            with pe.Fori(0, loops) as r:
                                for i in range(NSLOT):
                                    chunk(r * NSLOT + (2 + i), (2 + i) % NSLOT)
                            for c in range(2 + loops * NSLOT, NCH):
                                chunk(c, c % NSLOT)
                            flip(NCH - 1)
                            down(NCH - 1, False, True)
                        scatter(kb + NE + 1)
                    moe_passes(pe, one_pass)


_INS = ["x", "mem", "positions", "norm_mix", "w_in", "ssm_a_re", "ssm_a_im", "ssm_log_dt", "ssm_b_re",
        "ssm_b_im", "ssm_c_re", "ssm_c_im", "ssm_d", "ssm_w_glu", "gdn_conv", "gdn_a_log", "gdn_dt_bias",
        "gdn_norm", "w_up_moba", "w_up_gdn", "w_out", "norm_xa", "norm_mem", "xa_wq", "xa_wk", "xa_wv",
        "xa_wo", "norm_ffn", "ffn_w_gate", "ffn_w_up", "ffn_w_down", "moe_w_router", "moe_w_gate",
        "moe_w_up", "moe_w_down", "norm_final"]


def kernel(**inputs):
    import numpy as _np
    import concourse.bacc as _bacc
    from concourse import mybir as _mybir
    from concourse.bass_utils import run_bass_kernel_spmd as _run

    nc = _bacc.Bacc("TRN2", target_bir_lowering=False, num_devices=1)
    arrays, args = {}, []
    for name in _INS:
        a = _np.ascontiguousarray(inputs[name])
        arrays[f"in_{name}"] = a
        args.append(nc.dram_tensor(f"in_{name}", a.shape, _mybir.dt.from_np(a.dtype), kind="ExternalInput").ap())
    shape = inputs["x"].shape
    args.append(nc.dram_tensor("out", shape, _mybir.dt.float32, kind="ExternalOutput").ap())
    hybrid_trunk(nc, *args)
    r = _run(nc, [arrays], core_ids=[0])
    return r.results[0]["out"]
```
